# Optimizing a Trainium2 kernel written in Bass

```python
import jax
import jax.numpy as jnp
from jax import lax
import numpy as np

D_MODEL = 1024
BATCH = 1
SEQ = 512
DEPTH = 1

GRID_W = 64
CTX_LEN = 256
N_MOD = 6
RMS_EPS = 1e-6
NEG_INF = -1e30
NA_HEADS = 8
NA_HEAD_DIM = 64
NA_WIDTH = NA_HEADS * NA_HEAD_DIM
NA_WIN_R = 8
NA_WIN_C = 16
SC_WIDTH = 512
CONV_W = 3
GLA_HEADS = 4
GLA_KEY_WIDTH = D_MODEL // 2
GLA_VAL_WIDTH = D_MODEL
GLA_DK = GLA_KEY_WIDTH // GLA_HEADS
GLA_DV = GLA_VAL_WIDTH // GLA_HEADS
GLA_GATE_RANK = 16
GLA_GATE_TAU = 16.0
GLA_CHUNK = 64
N_BRANCH = 3
N_EXPERTS = 64
N_EXPERT_GROUPS = 8
TOPK_GROUPS = 4
TOP_K = 8
EXPERT_FF = 256
ROUTED_SCALE = 2.5
MOE_BLOCK = 256
KV_COLS = (NA_WIDTH, NA_WIDTH, GLA_KEY_WIDTH, GLA_VAL_WIDTH, 2 * GLA_GATE_RANK)
LAT_COLS = (NA_WIDTH, SC_WIDTH, SC_WIDTH, SC_WIDTH, GLA_KEY_WIDTH, GLA_VAL_WIDTH, N_BRANCH * D_MODEL)
IN_COLS = KV_COLS + LAT_COLS
N_KV = sum(KV_COLS)
N_IN = sum(IN_COLS)
COL_NAMES = ('k_na', 'v_na', 'k_gla', 'v_gla', 'gate_gla', 'q_na', 'b_sc', 'c_sc', 'x_sc', 'q_gla', 'r_gla', 'merge')

kernel_name = 'hybrid_natten_conv_gla_moe_prefix_dit'

def _rmsnorm(x, g):
    x32 = x.astype(jnp.float32)
    y = x32 * lax.rsqrt(jnp.mean(x32 * x32, axis=-1, keepdims=True) + RMS_EPS)
    return (y * g.astype(jnp.float32)).astype(x.dtype)

def _modulate(x, g, shift, scale):
    return _rmsnorm(x, g) * (1 + scale) + shift

def _heads(t, n):
    return t.reshape(t.shape[:-1] + (n, t.shape[-1] // n))

def _split_cols(z, sizes):
    return dict(zip(COL_NAMES, jnp.split(z, np.cumsum(sizes)[:-1].tolist(), axis=-1)))

def _attend_dense(q, k, v):
    s = jnp.einsum('bqhd,bkhd->bhqk', q, k).astype(jnp.float32) * (q.shape[-1] ** -0.5)
    p = jax.nn.softmax(s, axis=-1).astype(q.dtype)
    o = jnp.einsum('bhqk,bkhd->bqhd', p, v)
    return o.reshape(o.shape[:2] + (-1,))

def _na_latent(q, k, v, k_ctx, v_ctx, rpb):
    b, s, h, d = q.shape
    rows = s // GRID_W
    kr = min(NA_WIN_R, rows)
    row_start = np.clip(np.arange(rows) - kr // 2, 0, rows - kr)
    row_idx = row_start[:, None] + np.arange(kr)
    col = np.arange(GRID_W)
    col_start = np.clip(col - NA_WIN_C // 2, 0, GRID_W - NA_WIN_C)
    col_ok = (col[None, :] >= col_start[:, None]) & (col[None, :] < col_start[:, None] + NA_WIN_C)
    d_row = row_idx - np.arange(rows)[:, None] + NA_WIN_R - 1
    d_col = np.clip(col[None, :] - col[:, None], -(NA_WIN_C - 1), NA_WIN_C - 1) + NA_WIN_C - 1
    bias = rpb.astype(jnp.float32)[:, d_row[:, None, :, None], d_col[None, :, None, :]]
    bias = jnp.where(col_ok[None, None, :, None, :], bias, NEG_INF)
    scale = d ** -0.5
    qg = q.reshape(b, rows, GRID_W, h, d)
    kg = k.reshape(b, rows, GRID_W, h, d)[:, row_idx]
    vg = v.reshape(b, rows, GRID_W, h, d)[:, row_idx]
    s_win = jnp.einsum('brqhd,brjkhd->bhrqjk', qg, kg).astype(jnp.float32) * scale + bias[None]
    s_ctx = jnp.einsum('brqhd,bchd->bhrqc', qg, k_ctx).astype(jnp.float32) * scale
    n_win = kr * GRID_W
    scores = jnp.concatenate([s_win.reshape(b, h, rows, GRID_W, n_win), s_ctx], axis=-1)
    p = jax.nn.softmax(scores, axis=-1).astype(q.dtype)
    p_win = p[..., :n_win].reshape(b, h, rows, GRID_W, kr, GRID_W)
    p_ctx = p[..., n_win:]
    o = jnp.einsum('bhrqjk,brjkhd->brqhd', p_win, vg) + jnp.einsum('bhrqc,bchd->brqhd', p_ctx, v_ctx)
    return o.reshape(b, s, h * d)

def _short_conv(b_gate, c_gate, x_in, w):
    u = c_gate * x_in
    up = jnp.pad(u, ((0, 0), (1, 1), (0, 0)))
    return b_gate * (up[:, :-2] * w[0] + up[:, 1:-1] * w[1] + up[:, 2:] * w[2])

def _gla_decay(gate_lr, w2, b2):
    outs = []
    for dr, lr in enumerate(jnp.split(gate_lr, 2, axis=-1)):
        logit = (lr @ w2[dr] + b2[dr]).astype(jnp.float32)
        outs.append(_heads(jax.nn.log_sigmoid(logit) / GLA_GATE_TAU, GLA_HEADS))
    return outs[0], outs[1]

def _gla_scan(q, k, v, g, s0, emit):
    b, l, h, _ = k.shape
    dv = v.shape[-1]
    n = l // GLA_CHUNK

    def chunks(t):
        return t.reshape(b, n, GLA_CHUNK, h, t.shape[-1]).transpose(1, 0, 3, 2, 4).astype(jnp.float32)

    lower = np.tril(np.ones((GLA_CHUNK, GLA_CHUNK), dtype=bool))

    def step(state, inp):
        kc, vc, gc = inp[0], inp[1], inp[2]
        cum = jnp.cumsum(gc, axis=2)
        last = cum[:, :, -1:, :]
        new_state = (jnp.exp(last[:, :, 0, :])[..., None] * state
                     + jnp.einsum('bhsd,bhsv->bhdv', kc * jnp.exp(last - cum), vc))
        if not emit:
            return new_state, None
        qc = inp[3]
        inter = jnp.einsum('bhtd,bhdv->bhtv', qc * jnp.exp(cum), state)
        diff = cum[:, :, :, None, :] - cum[:, :, None, :, :]
        decay = jnp.exp(jnp.where(lower[:, :, None], diff, -jnp.inf))
        attn = jnp.einsum('bhtd,bhsd,bhtsd->bhts', qc, kc, decay)
        intra = jnp.einsum('bhts,bhsv->bhtv', attn, vc)
        return new_state, inter + intra

    xs = (chunks(k), chunks(v), chunks(g)) + ((chunks(q),) if emit else ())
    state, o = lax.scan(step, s0, xs)
    if emit:
        o = o.transpose(1, 0, 3, 2, 4).reshape(b, l, h, dv)
    return o, state

def _gla_bidir(q, k, v, g_f, g_b, s_f, s_b, emit):
    o_f, st_f = _gla_scan(q, k, v, g_f, s_f, emit)
    rev = lambda t: None if t is None else jnp.flip(t, axis=1)
    o_b, st_b = _gla_scan(rev(q), rev(k), rev(v), rev(g_b), s_b, emit)
    o = o_f + jnp.flip(o_b, axis=1) if emit else None
    return o, st_f, st_b

def _gla_out(o, r, g):
    on = o * lax.rsqrt(jnp.mean(o * o, axis=-1, keepdims=True) + RMS_EPS) * g.astype(jnp.float32)
    y = on * jax.nn.silu(_heads(r, GLA_HEADS).astype(jnp.float32))
    return y.reshape(r.shape).astype(r.dtype)

def _merge(o_na, o_sc, o_gla, gates, w_na, w_sc, w_gla, w_out):
    g_na, g_sc, g_gla = jnp.split(jax.nn.sigmoid(gates), N_BRANCH, axis=-1)
    y = g_na * (o_na @ w_na) + g_sc * (o_sc @ w_sc) + g_gla * (o_gla @ w_gla)
    return y @ w_out

def _moe(h, w_router, b_router, w_gate, w_up, w_down, ws_gate, ws_up, ws_down):
    t, d = h.shape
    scores = jax.nn.sigmoid((h @ w_router).astype(jnp.float32))
    sel = scores + b_router.astype(jnp.float32)
    group_score = lax.top_k(sel.reshape(t, N_EXPERT_GROUPS, N_EXPERTS // N_EXPERT_GROUPS), 2)[0].sum(-1)
    _, top_groups = lax.top_k(group_score, TOPK_GROUPS)
    group_mask = (top_groups[:, :, None] == jnp.arange(N_EXPERT_GROUPS)[None, None, :]).any(axis=1)
    sel = jnp.where(jnp.repeat(group_mask, N_EXPERTS // N_EXPERT_GROUPS, axis=1), sel, -jnp.inf)
    _, eidx = lax.top_k(sel, TOP_K)
    gate_w = jnp.take_along_axis(scores, eidx, axis=1)
    gate_w = gate_w / gate_w.sum(-1, keepdims=True) * ROUTED_SCALE
    a = t * TOP_K
    e_flat = eidx.reshape(-1).astype(jnp.int32)
    tok_flat = jnp.repeat(jnp.arange(t, dtype=jnp.int32), TOP_K)
    w_flat = gate_w.reshape(-1)
    order = jnp.argsort(e_flat)
    e_sorted = e_flat[order]
    counts = jnp.zeros((N_EXPERTS,), jnp.int32).at[e_flat].add(1)
    padded = (counts + MOE_BLOCK - 1) // MOE_BLOCK * MOE_BLOCK
    pad_end = jnp.cumsum(padded)
    pad_start = pad_end - padded
    grp_start = jnp.cumsum(counts) - counts
    dest = pad_start[e_sorted] + jnp.arange(a, dtype=jnp.int32) - grp_start[e_sorted]
    n_blocks = -(-(a + N_EXPERTS * (MOE_BLOCK - 1)) // MOE_BLOCK)
    slots = n_blocks * MOE_BLOCK
    slot_tok = jnp.full((slots,), t, jnp.int32).at[dest].set(tok_flat[order])
    slot_w = jnp.zeros((slots,), h.dtype).at[dest].set(w_flat[order].astype(h.dtype))
    blk_e = jnp.minimum(jnp.searchsorted(pad_end, jnp.arange(n_blocks, dtype=jnp.int32) * MOE_BLOCK, side='right'), N_EXPERTS - 1)
    h_pad = jnp.concatenate([h, jnp.zeros((1, d), h.dtype)], axis=0)

    def step(acc, blk):
        tok, w, e = blk
        xb = h_pad[tok]
        hid = jax.nn.silu(xb @ w_gate[e]) * (xb @ w_up[e])
        return acc.at[tok].add((hid @ w_down[e]) * w[:, None]), None

    routed, _ = lax.scan(step, jnp.zeros((t + 1, d), h.dtype),
                         (slot_tok.reshape(n_blocks, MOE_BLOCK), slot_w.reshape(n_blocks, MOE_BLOCK), blk_e))
    shared = (jax.nn.silu(h @ ws_gate) * (h @ ws_up)) @ ws_down
    return shared + routed[:t]

def _layer(x, ctx_s, c, c_ctx, w_mod, b_mod, g_norm1, g_norm2, w_in, na_rpb, w_branch_na, conv_w, w_branch_sc,
           gla_gate_w, gla_gate_b, gla_norm_g, w_branch_gla, w_out, w_router, b_router, w_exp_gate, w_exp_up,
           w_exp_down, w_sh_gate, w_sh_up, w_sh_down, ctx_out):
    sh1, sc1, gt1, sh2, sc2, gt2 = jnp.split((jax.nn.silu(c) @ w_mod + b_mod)[:, None, :], N_MOD, axis=-1)
    csh1, csc1, cgt1, csh2, csc2, cgt2 = jnp.split(jax.nn.silu(c_ctx) @ w_mod + b_mod, N_MOD, axis=-1)

    lat = _split_cols(_modulate(x, g_norm1, sh1, sc1) @ w_in, IN_COLS)
    hc = _modulate(ctx_s, g_norm1, csh1, csc1)
    cx = _split_cols(hc @ w_in, IN_COLS) if ctx_out else _split_cols(hc @ w_in[:, :N_KV], KV_COLS)

    k_na_c = _heads(cx['k_na'], NA_HEADS)
    v_na_c = _heads(cx['v_na'], NA_HEADS)
    o_na = _na_latent(_heads(lat['q_na'], NA_HEADS), _heads(lat['k_na'], NA_HEADS), _heads(lat['v_na'], NA_HEADS),
                      k_na_c, v_na_c, na_rpb)
    o_sc = _short_conv(lat['b_sc'], lat['c_sc'], lat['x_sc'], conv_w)
    q_scale = GLA_DK ** -0.5
    s0 = jnp.zeros((x.shape[0], GLA_HEADS, GLA_DK, GLA_DV), jnp.float32)
    gcf, gcb = _gla_decay(cx['gate_gla'], gla_gate_w, gla_gate_b)
    q_gla_c = _heads(cx['q_gla'], GLA_HEADS) * q_scale if ctx_out else None
    o_gla_c, st_f, st_b = _gla_bidir(q_gla_c, _heads(cx['k_gla'], GLA_HEADS), _heads(cx['v_gla'], GLA_HEADS),
                                     gcf, gcb, s0, s0, ctx_out)
    glf, glb = _gla_decay(lat['gate_gla'], gla_gate_w, gla_gate_b)
    o_gla, _, _ = _gla_bidir(_heads(lat['q_gla'], GLA_HEADS) * q_scale, _heads(lat['k_gla'], GLA_HEADS),
                             _heads(lat['v_gla'], GLA_HEADS), glf, glb, st_f, st_b, True)
    o_gla = _gla_out(o_gla, lat['r_gla'], gla_norm_g)
    x = x + gt1 * _merge(o_na, o_sc, o_gla, lat['merge'], w_branch_na, w_branch_sc, w_branch_gla, w_out)
    if ctx_out:
        o_na_c = _attend_dense(_heads(cx['q_na'], NA_HEADS), k_na_c, v_na_c)
        o_sc_c = _short_conv(cx['b_sc'], cx['c_sc'], cx['x_sc'], conv_w)
        o_gla_c = _gla_out(o_gla_c, cx['r_gla'], gla_norm_g)
        ctx_s = ctx_s + cgt1 * _merge(o_na_c, o_sc_c, o_gla_c, cx['merge'], w_branch_na, w_branch_sc, w_branch_gla, w_out)

    d = x.shape[-1]
    tokens = _modulate(x, g_norm2, sh2, sc2).reshape(-1, d)
    if ctx_out:
        tokens = jnp.concatenate([tokens, _modulate(ctx_s, g_norm2, csh2, csc2).reshape(-1, d)], axis=0)
    y = _moe(tokens, w_router, b_router, w_exp_gate, w_exp_up, w_exp_down, w_sh_gate, w_sh_up, w_sh_down)
    n_lat = x.shape[0] * x.shape[1]
    x = x + gt2 * y[:n_lat].reshape(x.shape)
    if ctx_out:
        ctx_s = ctx_s + cgt2 * y[n_lat:].reshape(ctx_s.shape)
    return x, ctx_s

def setup_inputs(seed: int = 0) -> dict:
    key = jax.random.key(seed)
    ks = jax.random.split(key, 28)
    nrm = lambda k, shape, s: jax.random.normal(k, shape, jnp.float32) * s
    L = DEPTH
    return {
        'x': nrm(ks[0], (BATCH, SEQ, D_MODEL), 1.0),
        'c': nrm(ks[1], (BATCH, D_MODEL), 1.0),
        'ctx': nrm(ks[2], (BATCH, CTX_LEN, D_MODEL), 1.0),
        'c_ctx': nrm(ks[3], (D_MODEL,), 1.0),
        'w_mod': nrm(ks[4], (L, D_MODEL, N_MOD * D_MODEL), 0.5 * D_MODEL ** -0.5),
        'b_mod': nrm(ks[5], (L, N_MOD * D_MODEL), 0.02),
        'g_norm1': 1.0 + nrm(ks[6], (L, D_MODEL), 0.02),
        'g_norm2': 1.0 + nrm(ks[7], (L, D_MODEL), 0.02),
        'w_in': nrm(ks[8], (L, D_MODEL, N_IN), D_MODEL ** -0.5),
        'na_rpb': nrm(ks[9], (L, NA_HEADS, 2 * NA_WIN_R - 1, 2 * NA_WIN_C - 1), 0.1),
        'w_branch_na': nrm(ks[10], (L, NA_WIDTH, D_MODEL), NA_WIDTH ** -0.5),
        'conv_w': nrm(ks[11], (L, CONV_W, SC_WIDTH), CONV_W ** -0.5),
        'w_branch_sc': nrm(ks[12], (L, SC_WIDTH, D_MODEL), SC_WIDTH ** -0.5),
        'gla_gate_w': nrm(ks[13], (L, 2, GLA_GATE_RANK, GLA_KEY_WIDTH), GLA_GATE_RANK ** -0.5),
        'gla_gate_b': nrm(ks[14], (L, 2, GLA_KEY_WIDTH), 0.1),
        'gla_norm_g': 1.0 + nrm(ks[15], (L, GLA_DV), 0.02),
        'w_branch_gla': nrm(ks[16], (L, GLA_VAL_WIDTH, D_MODEL), GLA_VAL_WIDTH ** -0.5),
        'w_out': nrm(ks[17], (L, D_MODEL, D_MODEL), D_MODEL ** -0.5),
        'w_router': nrm(ks[18], (L, D_MODEL, N_EXPERTS), D_MODEL ** -0.5),
        'b_router': nrm(ks[19], (L, N_EXPERTS), 0.01),
        'w_exp_gate': nrm(ks[20], (L, N_EXPERTS, D_MODEL, EXPERT_FF), D_MODEL ** -0.5),
        'w_exp_up': nrm(ks[21], (L, N_EXPERTS, D_MODEL, EXPERT_FF), D_MODEL ** -0.5),
        'w_exp_down': nrm(ks[22], (L, N_EXPERTS, EXPERT_FF, D_MODEL), EXPERT_FF ** -0.5),
        'w_sh_gate': nrm(ks[23], (L, D_MODEL, EXPERT_FF), D_MODEL ** -0.5),
        'w_sh_up': nrm(ks[24], (L, D_MODEL, EXPERT_FF), D_MODEL ** -0.5),
        'w_sh_down': nrm(ks[25], (L, EXPERT_FF, D_MODEL), EXPERT_FF ** -0.5),
        'g_final': 1.0 + nrm(ks[26], (D_MODEL,), 0.02),
    }

def reference(x, c, ctx, c_ctx, w_mod, b_mod, g_norm1, g_norm2, w_in, na_rpb, w_branch_na, conv_w, w_branch_sc,
              gla_gate_w, gla_gate_b, gla_norm_g, w_branch_gla, w_out, w_router, b_router, w_exp_gate, w_exp_up,
              w_exp_down, w_sh_gate, w_sh_up, w_sh_down, g_final):
    ctx_s = ctx
    for i in range(DEPTH):
        x, ctx_s = _layer(x, ctx_s, c, c_ctx, w_mod[i], b_mod[i], g_norm1[i], g_norm2[i], w_in[i], na_rpb[i],
                          w_branch_na[i], conv_w[i], w_branch_sc[i], gla_gate_w[i], gla_gate_b[i], gla_norm_g[i],
                          w_branch_gla[i], w_out[i], w_router[i], b_router[i], w_exp_gate[i], w_exp_up[i],
                          w_exp_down[i], w_sh_gate[i], w_sh_up[i], w_sh_down[i], i < DEPTH - 1)
    return _rmsnorm(x, g_final)


_drawn_inputs = setup_inputs


def setup_inputs(seed=0):
    import zlib

    import numpy as np

    out = dict(_drawn_inputs(seed))
    spreads = {}
    factors = {'g_norm1': 2.712,
     'na_rpb': 29.546,
     'gla_gate_b': 3.863,
     'gla_norm_g': 37.166,
     'g_final': 7.981,
     'g_norm2': 8.0,
     'b_router': 5.507}
    for name, (base, spread) in spreads.items():
        noise = np.random.default_rng([zlib.crc32(name.encode()), seed]).standard_normal(out[name].shape)
        drawn = base * np.exp(spread * noise) if base else spread * noise
        out[name] = jnp.asarray(drawn.astype(out[name].dtype))
    for name, factor in factors.items():
        out[name] = (out[name] * factor).astype(out[name].dtype)
    return out
```

```python
from contextlib import ExitStack

import numpy as np
import concourse.bass as bass
from concourse import mybir

P = 128
D = 1024
KD = D // P
SEQ = 512
CTX = 256
TOK = SEQ + CTX
TT = SEQ // P
TC = CTX // P
NA_H, NA_D = 8, 64
GRID = 64
WIN_R, WIN_C = 8, 16
RPB_R, RPB_C = 2 * WIN_R - 1, 2 * WIN_C - 1
GL_H, GL_DK, GL_DV = 4, 128, 256
RANK = 16
TAU = 16.0
NE, NG, TOPG, TOPK, FF = 64, 8, 4, 8, 256
ROUTED_SCALE = 2.5
EPS = 1e-6
NEG = -1e30
ROUND = 2.0 ** 23
PAD = 65536.0
NBLK = (SEQ * TOPK + NE * (P - 1)) // P
NBLK += NBLK % 2
RPB_T = RPB_R * RPB_C

F = mybir.dt.float32
R = mybir.dt.float32r
I32 = mybir.dt.int32
U32 = mybir.dt.uint32
ALU = mybir.AluOpType
ACT = mybir.ActivationFunctionType
AX = mybir.AxisListType

K_NA, V_NA, K_GLA, V_GLA, GATE, Q_NA, B_SC, C_SC, X_SC, Q_GLA, R_GLA, MERGE = (
    0, 512, 1024, 1536, 2560, 2592, 3104, 3616, 4128, 4640, 5152, 6176)

KB = 1024
BASE = 18 * KB
NRAW, NSPLIT = 3, 2


class Chain:

    def __init__(self, sem):
        self.sem, self.n = sem, 0

    def __call__(self, eng, ins):
        self.n += 1
        ins.then_inc(self.sem, 1)
        eng.wait_ge(self.sem, self.n)


def plan_tiles():
    halves, chunks, tiles = [], {}, []
    counts = {"A": 0, "D": 0}

    def chunk(name, weight, col, outs, rows=2):
        first = len(halves)
        for k in range(rows):
            halves.append((weight, 4 * k, col))
        mine = []
        for n, (kind, t) in enumerate(outs):
            who = "A" if name[0] in ("r", "c", "gate") else "D" if name[0] in ("mod", "x", "b", "br", "out", "row", "sh", "down") else "AD"[n % 2]
            counts[who] += 1
            tile = dict(n=len(tiles), bank=len(tiles) % 8, who=who, nth=counts[who], kind=kind, t=t)
            mine.append(tile)
            tiles.append(tile)
        chunks[name] = dict(name=name, first=first, last=len(halves) - 1, tiles=mine)

    feat = [("feat", m) for m in range(4)]
    feat_ctx = [("featc", m) for m in range(4)]
    tok = [("tok", t) for t in range(TT)]
    tok_ctx = [("tokc", t) for t in range(TC)]
    row = [("row", 0)]
    for j in range(4):
        chunk(("mod", j), "w_mod", 512 * j, row)
    chunk(("k_na",), "w_in", K_NA, feat + feat_ctx)
    chunk(("v_na",), "w_in", V_NA, tok + tok_ctx)
    chunk(("q_na",), "w_in", Q_NA, feat)
    chunk(("k_gla",), "w_in", K_GLA, feat + feat_ctx)
    chunk(("v_gla", 0), "w_in", V_GLA, tok + tok_ctx)
    chunk(("v_gla", 1), "w_in", V_GLA + 512, tok + tok_ctx)
    chunk(("q_gla",), "w_in", Q_GLA, feat)
    chunk(("r", 0), "w_in", R_GLA, tok)
    chunk(("r", 1), "w_in", R_GLA + 512, tok)
    chunk(("c",), "w_in", C_SC, feat)
    chunk(("x",), "w_in", X_SC, feat)
    chunk(("b",), "w_in", B_SC, feat)
    for j in range(2):
        for br, (weight, rows) in enumerate((("w_branch_na", 1), ("w_branch_sc", 1), ("w_branch_gla", 2))):
            chunk(("gate", j, br), "w_in", MERGE + br * D + 512 * j, feat)
            chunk(("br", j, br), weight, 512 * j, [(f"b{br}", m) for m in range(4)], rows)
    for j in range(2):
        chunk(("row", "gt1", j), "w_mod", 2 * D + 512 * j, row)
    for j in range(2):
        chunk(("out", j), "w_out", 512 * j, [("y", t) for t in range(TT)])
    for i, name in enumerate(("sh2", "sc2", "gt2")):
        for j in range(2):
            chunk(("row", name, j), "w_mod", (3 + i) * D + 512 * j, row)
    chunk(("sh",), "w_sh", 0, tok)
    chunk(("down",), "w_sh_down", 0, [("down", t) for t in range(2 * TT)], 1)
    return halves, chunks, tiles


def build(nc, x, c, ctx, c_ctx, w_mod, b_mod, g_norm1, g_norm2, w_in, na_rpb, w_branch_na, conv_w, w_branch_sc,
          gla_gate_w, gla_gate_b, gla_norm_g, w_branch_gla, w_out, w_router, b_router, w_exp_gate, w_exp_up,
          w_exp_down, w_sh_gate, w_sh_up, w_sh_down, g_final, k_ident, k_tri, k_mask, k_iota, k_slot, out, dump=None):
    HALVES, CH, TILES = plan_tiles()
    es = ExitStack()
    weights = {"w_mod": w_mod[0], "w_in": w_in[0], "w_branch_na": w_branch_na[0], "w_branch_sc": w_branch_sc[0],
               "w_branch_gla": w_branch_gla[0], "w_out": w_out[0]}

    def at(name, shape, kb, dt=F):
        return nc.alloc_sbuf_tensor_at(name, shape, dt, offset=BASE + int(kb * KB))

    def sem(name):
        return es.enter_context(nc.semaphore(name))

    early = ExitStack()
    early_sems = []

    def esem(name):
        early_sems.append(early.enter_context(nc.semaphore(name)))
        return early_sems[-1]

    def dram(name, shape, dt=F):
        return nc.dram_tensor(name, shape, dt, kind="Internal").ap()

    with es:
        PS = es.enter_context(nc.psum_tensor("PS", [P, 8, 512], F))
        fence = es.enter_context(nc.sbuf_tensor("fence", [P, 4], F))
        ident = at("ident", [P, P], 0)
        tri = at("tri", [P, 3, P], 0.5)
        namask = at("namask", [P, GRID], 2, I32)
        small = at("small", [P, 256], 2.5)
        csil = small[:, 0:16].rearrange("p (k w) -> p k w", w=2)
        ccol = small[:, 16:32].rearrange("p (w k) -> p w k", w=2)
        ssum = small[:, 32:48]
        rstd = small[:, 48:64]
        mhalf = small[:, 64:80]
        rsum = small[:, 80:112]
        rinv = small[:, 112:144]
        nmax = small[:, 144:176]
        convw = small[:, 176:188].rearrange("p (w m) -> p w m", w=3)
        tiny = small[:, 188:256]
        csel_hi = at("csel_hi", [P, KD, P], 4, R)
        csel_lo = at("csel_lo", [P, KD, P], 8, R)
        raw = at("raw", [P, NRAW, 4, 512], 12)
        whi = at("whi", [P, NSPLIT, 4, 512], 36, R)
        wlo = at("wlo", [P, NSPLIT, 4, 512], 52, R)
        hT_hi = at("hT_hi", [P, KD, SEQ], 68, R)
        hT_lo = at("hT_lo", [P, KD, SEQ], 84, R)
        hc_hi = at("hc_hi", [P, KD, CTX], 100, R)
        hc_lo = at("hc_lo", [P, KD, CTX], 108, R)
        onaT_hi = at("onaT_hi", [P, 4, SEQ], 116, R)
        onaT_lo = at("onaT_lo", [P, 4, SEQ], 124, R)

        landed = [sem(f"weights_landed{i}") for i in range(NRAW)]
        hi_done, lo_done, used = sem("hi_done"), sem("lo_done"), sem("half_used")
        tile_done = sem("tile_done")
        emptied = {"A": sem("emptied_by_act"), "D": sem("emptied_by_dve")}
        dch, ach = Chain(sem("dve_chain")), Chain(sem("act_chain"))
        pch = Chain(sem("pool_chain"))

        arrive, per_slot = [], [0] * NRAW
        for i, (w, _, _) in enumerate(HALVES):
            per_slot[i % NRAW] += 32 if w == "w_sh" else 16
            arrive.append(per_slot[i % NRAW])
        freed, firsts = [None] * len(HALVES), 0
        for ch in CH.values():
            for i in range(ch["first"], ch["last"]):
                firsts += 1
                freed[i] = (used, firsts)
            freed[ch["last"]] = (tile_done, ch["tiles"][-1]["n"] + 1)
        splits_a, splits_d = [0], [0]
        nloads = [0]

        def load_to(eng, upto):
            while nloads[0] <= min(upto, len(HALVES) - 1):
                i = nloads[0]
                nloads[0] += 1
                if i >= NRAW:
                    eng.wait_ge(lo_done, i - NRAW + 1)
                w, k, col = HALVES[i]
                dst = raw[:, i % NRAW]
                if w == "w_sh":
                    for n, src in enumerate((w_sh_gate, w_sh_up)):
                        eng.dma_start(dst[:, :, n * FF:(n + 1) * FF],
                                      src[0].rearrange("(k p) n -> p k n", p=P)[:, k:k + 4, :]).then_inc(landed[i % NRAW], 16)
                elif w == "w_sh_down":
                    eng.dma_start(dst.rearrange("p (k h) n -> p k (h n)", h=2),
                                  w_sh_down[0].rearrange("(k p) n -> p k n", p=P)).then_inc(landed[i % NRAW], 16)
                else:
                    eng.dma_start(dst, weights[w].rearrange("(k p) n -> p k n", p=P)[:, k:k + 4, col:col + 512])\
                       .then_inc(landed[i % NRAW], 16)

        def split_hi(act, upto):
            while splits_a[0] <= min(upto, len(HALVES) - 1):
                i = splits_a[0]
                splits_a[0] += 1
                act.wait_ge(landed[i % NRAW], arrive[i])
                if i >= NSPLIT:
                    act.wait_ge(*freed[i - NSPLIT])
                act.activation(whi[:, i % NSPLIT], raw[:, i % NRAW], ACT.Copy).then_inc(hi_done, 1)

        def split_lo(dve, upto):
            while splits_d[0] <= min(upto, len(HALVES) - 1):
                i = splits_d[0]
                splits_d[0] += 1
                dve.wait_ge(hi_done, i + 1)
                dve.tensor_tensor(wlo[:, i % NSPLIT], raw[:, i % NRAW], whi[:, i % NSPLIT].bitcast(F), ALU.subtract)\
                   .then_inc(lo_done, 1)

        def mm3(pe, o, ahi, alo, bhi, blo, start, stop):
            pe.matmul(o, ahi, bhi, start=start, stop=False)
            pe.matmul(o, alo, bhi, start=False, stop=False)
            return pe.matmul(o, ahi, blo, start=False, stop=stop)

        def project(pe, name, acts):
            ch = CH[name]
            for i in range(ch["first"], ch["last"] + 1):
                pe.wait_ge(lo_done, i + 1)
                s, first, last = i % NSPLIT, i == ch["first"], i == ch["last"]
                for tile in ch["tiles"]:
                    if first and tile["n"] >= 8:
                        before = TILES[tile["n"] - 8]
                        pe.wait_ge(emptied[before["who"]], before["nth"])
                    kind, t = tile["kind"], tile["t"]
                    bank = PS[:, tile["bank"], :]
                    ahi, alo = acts(kind)
                    if kind == "down":
                        for k in range(2):
                            lhs = slice((t // 2) * P, (t // 2 + 1) * P)
                            w = 2 * k + t % 2
                            mm = mm3(pe, bank, ahi[:, k, lhs], alo[:, k, lhs], whi[:, s, w], wlo[:, s, w], k == 0, k == 1)
                        mm.then_inc(tile_done, 1)
                        continue
                    for k in range(4):
                        kk = k + 4 * (i - ch["first"])
                        st, sp = first and k == 0, last and k == 3
                        if kind in ("tok", "tokc", "y"):
                            lhs = slice(t * P, (t + 1) * P)
                            mm = mm3(pe, bank, ahi[:, kk, lhs], alo[:, kk, lhs], whi[:, s, k], wlo[:, s, k], st, sp)
                        elif kind == "row":
                            mm = mm3(pe, bank, ahi[:, kk], alo[:, kk], whi[:, s, k], wlo[:, s, k], st, sp)
                        else:
                            o = bank[:, 0:CTX] if kind == "featc" else bank
                            cols = slice(t * P, (t + 1) * P)
                            mm = mm3(pe, o, whi[:, s, k, cols], wlo[:, s, k, cols], ahi[:, kk], alo[:, kk], st, sp)
                    if last:
                        mm.then_inc(tile_done, 1)
                if not last:
                    mm.then_inc(used, 1)

        def mine(name, who):
            return [t for t in CH[name]["tiles"] if t["who"] == who]

        def wait_tiles(eng, name):
            for who in "AD":
                own = mine(name, who)
                if own:
                    eng.wait_ge(emptied[who], own[-1]["nth"])

        def build_csel(dve, halves):
            for n, (w, a, b) in enumerate(halves):
                src = csil[:, :, w:w + 1].to_broadcast([P, KD, b - a])
                dch(dve, dve.tensor_copy(csel_hi[:, :, a:b], src))
                dch(dve, dve.tensor_tensor(csel_lo[:, :, a:b], src, csel_hi[:, :, a:b].bitcast(F), ALU.subtract))

        def copy_tiles(eng, who, name, dst, scale=1.0):
            for tile in mine(name, who):
                eng.wait_ge(tile_done, tile["n"] + 1)
                o = dst(tile["kind"], tile["t"])
                src = PS[:, tile["bank"], 0:CTX] if tile["kind"] == "featc" else PS[:, tile["bank"], :]
                if who == "A":
                    eng.activation(o, src, ACT.Copy, scale=scale).then_inc(emptied["A"], 1)
                else:
                    eng.tensor_scalar(o, src, scale, None, ALU.mult).then_inc(emptied["D"], 1)

        xs = at("xs", [P, TT + TC, D], 132)
        mrow = at("mrow", [P, 2 * D], 156)
        brow = at("brow", [P, 2 * D], 164)
        junk = at("junk", [P, D], 172)
        hf = at("hf", [P, 2, TOK], 176)
        modc = at("modc", [P, 2 * KD, 2], 182)
        scale1 = at("scale1", [P, KD, 2], 182.25)
        g1c = at("g1c", [P, KD], 182.5)
        cpy = sem("rpb_padded")
        x_in, consts, c_in, b_in = (esem(n) for n in ("x_in", "consts", "c_in", "b_in"))
        csil_done, csel_done, mrow_done, mrowT, modc_done = (esem(n) for n in ("csil", "csel", "mrow", "mrowT", "modc"))
        sq_done, ms_done, pow_done, xn_done, xT, hf_done, hhi_done, hlo_done = (
            esem(n) for n in ("squares", "meansq", "rstd", "xn", "xT", "hf", "h_hi", "h_lo"))
        zero_done = sem("zeros")
        rpb_rep = dram("rpb_rep", [NA_H, GRID, RPB_T])
        LAST1 = CH[("mod", 3)]["last"]

        with nc.Block() as block:
            @block.sync
            def _(sp):
                sp.dma_start(ccol[:, 0, :], c[0].rearrange("(k p) -> p k", p=P), allow_slow_non_contiguous=True).then_inc(c_in, 16)
                sp.dma_start(ccol[:, 1, :], c_ctx.rearrange("(k p) -> p k", p=P), allow_slow_non_contiguous=True).then_inc(c_in, 16)
                load_to(sp, 2)
                sp.dma_start(brow[:, :], bass.AP(tensor=b_mod.tensor, offset=0, ap=[[0, P], [1, 2 * D]])).then_inc(b_in, 16)
                sp.dma_start(g1c[:, :], g_norm1[0].rearrange("(k p) -> p k", p=P), allow_slow_non_contiguous=True).then_inc(b_in, 16)
                load_to(sp, LAST1 + 3)

            @block.gpsimd
            def _(pool):
                pool.dma_start(ident[:, :], k_ident).then_inc(consts, 16)
                pool.dma_start(tri[:, :, :], k_tri.rearrange("m p t -> p m t")).then_inc(consts, 16)
                pool.dma_start(namask[:, :], k_mask).then_inc(consts, 16)
                pool.memset(mhalf[:, :], -0.5).then_inc(zero_done, 1)
                pool.dma_start(rpb_rep, bass.AP(tensor=na_rpb.tensor, offset=0, ap=[[RPB_T, NA_H], [0, GRID], [1, RPB_T]]))\
                    .then_inc(cpy, 16)
                pool.wait_ge(zero_done, 1)
                pool.wait_ge(cpy, 16)
                pool.wait_ge(consts, 48)
                pool.wait_ge(ms_done, 1)
                pool.tensor_tensor(rstd[:, 0:TT + TC], ssum[:, 0:TT + TC], mhalf[:, 0:TT + TC], ALU.pow).then_inc(pow_done, 1)

            @block.scalar
            def _(act):
                act.dma_start(xs[:, 0:TT, :], x[0].rearrange("(t p) d -> p t d", p=P)).then_inc(x_in, 16)
                act.dma_start(xs[:, TT:, :], ctx[0].rearrange("(t p) d -> p t d", p=P)).then_inc(x_in, 16)
                act.wait_ge(c_in, 32)
                act.activation(csil.rearrange("p k w -> p w k"), ccol, ACT.Silu).then_inc(csil_done, 1)
                split_hi(act, 1)
                act.wait_ge(x_in, 32)
                for t in range(TT + TC):
                    ach(act, act.activation(junk[:, :], xs[:, t, :], ACT.Square, accum_out=ssum[:, t:t + 1]))
                act.copy(tiny[:, 67:68], ssum[:, 0:1]).then_inc(sq_done, 1)
                split_hi(act, LAST1 + 2)
                for k in range(KD):
                    act.wait_ge(hf_done, k + 1)
                    act.activation(hT_hi[:, k, :], hf[:, k % 2, 0:SEQ], ACT.Copy).then_inc(hhi_done, 1)
                    act.activation(hc_hi[:, k, :], hf[:, k % 2, SEQ:], ACT.Copy).then_inc(hhi_done, 1)
                split_hi(act, LAST1 + 2)

            @block.vector
            def _(dve):
                dve.wait_ge(csil_done, 1)
                build_csel(dve, [(0, 0, 64), (1, 64, P)])
                dve.tensor_copy(tiny[:, 66:67], csil[:, 0, 0:1]).then_inc(csel_done, 1)
                split_lo(dve, 1)
                dve.wait_ge(sq_done, 1)
                dve.tensor_scalar(ssum[:, 0:TT + TC], ssum[:, 0:TT + TC], 1.0 / D, EPS, ALU.mult, ALU.add).then_inc(ms_done, 1)
                dve.wait_ge(pow_done, 1)
                for t in range(TT + TC):
                    dve.tensor_scalar(xs[:, t, :], xs[:, t, :], rstd[:, t:t + 1], None, ALU.mult).then_inc(xn_done, 1)
                dve.wait_ge(b_in, 32)
                for j in range(4):
                    split_lo(dve, 2 * j + 3)
                    tile = CH[("mod", j)]["tiles"][0]
                    dve.wait_ge(tile_done, tile["n"] + 1)
                    cols = slice(512 * j, 512 * j + 512)
                    dve.tensor_tensor(mrow[:, cols], PS[:, tile["bank"], :], brow[:, cols], ALU.add).then_inc(emptied["D"], 1)
                dve.wait_ge(mrowT, 1)
                dch(dve, dve.tensor_copy(modc[:, :, :].rearrange("p (b k) w -> p b k w", b=4),
                                         PS[:, 4:8, :].rearrange("p b (k t) -> p b k t", t=P)[:, :, :, 0:P:64]))
                dve.tensor_scalar(scale1[:, :, :], modc[:, KD:, :], 1.0, None, ALU.add).then_inc(modc_done, 1)
                dve.wait_ge(modc_done, 1)
                dch(dve, dve.tensor_tensor(scale1[:, :, :], scale1[:, :, :],
                                           g1c[:, :, None].to_broadcast([P, KD, 2]), ALU.mult))
                for k in range(KD):
                    dve.wait_ge(xT, k + 1)
                    if k >= 2:
                        dve.wait_ge(hhi_done, 2 * k - 2)
                        dve.wait_ge(hlo_done, 2 * k - 2)
                    b = 4 * (k % 2)
                    dve.tensor_scalar(hf[:, k % 2, 0:SEQ], PS[:, b, :], scale1[:, k, 0:1], modc[:, k, 0:1], ALU.mult, ALU.add)
                    dve.tensor_scalar(hf[:, k % 2, SEQ:], PS[:, b + 1, 0:CTX], scale1[:, k, 1:2], modc[:, k, 1:2], ALU.mult, ALU.add)\
                       .then_inc(hf_done, 1)
                    dve.wait_ge(hf_done, k + 1)
                    dve.wait_ge(hhi_done, 2 * k + 2)
                    dve.tensor_tensor(hT_lo[:, k, :], hf[:, k % 2, 0:SEQ], hT_hi[:, k, :].bitcast(F), ALU.subtract).then_inc(hlo_done, 1)
                    dve.tensor_tensor(hc_lo[:, k, :], hf[:, k % 2, SEQ:], hc_hi[:, k, :].bitcast(F), ALU.subtract).then_inc(hlo_done, 1)
                split_lo(dve, LAST1 + 2)

            @block.tensor
            def _(pe):
                pe.wait_ge(csel_done, 1)
                for j in range(4):
                    project(pe, ("mod", j), lambda kind: (csel_hi, csel_lo))
                pe.wait_ge(consts, 48)
                pe.wait_ge(emptied["D"], 4)
                for m in range(2 * KD):
                    mm = pe.transpose(PS[:, 4 + m // 4, (m % 4) * P:(m % 4 + 1) * P], mrow[:, m * P:(m + 1) * P], ident[:, :])
                mm.then_inc(mrowT, 1)
                pe.wait_ge(xn_done, TT + TC)
                pe.wait_ge(modc_done, 1)
                for k in range(KD):
                    b = 4 * (k % 2)
                    if k >= 2:
                        pe.wait_ge(hf_done, k - 1)
                    for t in range(TT + TC):
                        o = PS[:, b + t // TT, (t % TT) * P:(t % TT + 1) * P]
                        mm = pe.transpose(o, xs[:, t, k * P:(k + 1) * P], ident[:, :])
                    mm.then_inc(xT, 1)

        def acts(kind):
            return (hc_hi, hc_lo) if kind in ("featc", "tokc") else (hT_hi, hT_lo)

        kna = at("kna", [P, 4, TOK], 132)
        vna = at("vna", [P, TT + TC, 512], 144)
        qna = at("qna", [P, 4, SEQ], 156)
        prob = at("prob", [P, 2, TOK], 164)
        probT = at("probT", [P, 2, TOK], 170)
        braw = at("braw", [P, 14, GRID], 176)
        bias = at("bias", [P, 2, 14, GRID], 179.5)
        ona = at("ona", [P, TT, 512], 186.5)
        NI = NA_H * TT
        bias_in, bias_done, scores, scores_read, smax = (esem(n) for n in ("bias_in", "bias", "scores", "scores_read", "smax"))
        exped, probT_done, pT_a, pT_d, pv_done, ona_done = (esem(n) for n in ("exped", "probT", "pT_act", "pT_dve", "pv", "ona"))
        turned, turn_hi, turn_lo = sem("turned"), sem("turn_hi"), sem("turn_lo")
        nturn = [0, 0, 0]

        def turn(pe, src, n_tiles, banks, first_wait=None):
            for m in range(n_tiles):
                i = nturn[0]
                nturn[0] += 1
                if m >= len(banks):
                    pe.wait_ge(turn_lo, i - len(banks) + 1)
                for t in range(TT):
                    mm = pe.transpose(PS[:, banks[m % len(banks)], t * P:(t + 1) * P], src(t, m), ident[:, :])
                mm.then_inc(turned, 1)

        def turn_out_hi(act, dst, n_tiles, banks):
            for m in range(n_tiles):
                nturn[1] += 1
                act.wait_ge(turned, nturn[1])
                act.activation(dst[:, m, :], PS[:, banks[m % len(banks)], :], ACT.Copy).then_inc(turn_hi, 1)

        def turn_out_lo(dve, dst, hi, n_tiles, banks):
            for m in range(n_tiles):
                nturn[2] += 1
                dve.wait_ge(turn_hi, nturn[2])
                dve.tensor_tensor(dst[:, m, :], PS[:, banks[m % len(banks)], :], hi[:, m, :].bitcast(F), ALU.subtract)\
                   .then_inc(turn_lo, 1)

        def kna_at(kind, m):
            return kna[:, m, SEQ:] if kind == "featc" else kna[:, m, 0:SEQ]

        def vna_at(kind, t):
            return vna[:, TT + t, :] if kind == "tokc" else vna[:, t, :]

        na_names = [("k_na",), ("v_na",), ("q_na",)]
        LAST2 = CH[("q_na",)]["last"]
        with nc.Block() as block:
            @block.sync
            def _(sp):
                for h in range(NA_H):
                    if h:
                        sp.wait_ge(bias_done, h)
                    off = h * GRID * RPB_T + WIN_C - 1
                    for half in range(2):
                        sp.dma_start(braw[64 * half:64 * half + 64],
                                     bass.AP(tensor=rpb_rep.tensor, offset=off + (1 - half) * RPB_C,
                                             ap=[[RPB_T - 1, GRID], [RPB_C, 14], [1, GRID]])).then_inc(bias_in, 16)
                    if h == 0:
                        load_to(sp, LAST2 + 3)

            @block.scalar
            def _(act):
                for name, dst in zip(na_names, (kna_at, vna_at, lambda kind, m: qna[:, m, :])):
                    split_hi(act, CH[name]["last"] + 2)
                    copy_tiles(act, "A", name, dst)
                for i in range(NI + 1):
                    if i < NI:
                        act.wait_ge(smax, i + 1)
                        act.activation(prob[:, i % 2, :], prob[:, i % 2, :], ACT.Exp, bias=nmax[:, i:i + 1],
                                       accum_out=rsum[:, i:i + 1]).then_inc(exped, 1)
                    if i >= 1:
                        j = i - 1
                        act.wait_ge(probT_done, j + 1)
                        if j >= 2:
                            act.wait_ge(pv_done, j - 1)
                        act.activation(probT[:, j % 2, 0:512], PS[:, 3, :], ACT.Copy).then_inc(pT_a, 1)
                turn_out_hi(act, onaT_hi, 4, [0, 1, 2, 3])

            @block.vector
            def _(dve):
                for name, dst in zip(na_names, (kna_at, vna_at, lambda kind, m: qna[:, m, :])):
                    split_lo(dve, CH[name]["last"] + 2)
                    copy_tiles(dve, "D", name, dst)
                for i in range(NI + 2):
                    if i < NI:
                        h, qt = divmod(i, TT)
                        if qt == 0:
                            if h >= 2:
                                dve.wait_ge(smax, (h - 1) * TT)
                            dch(dve, dve.memset(bias[:, h % 2], NEG))
                            dve.wait_ge(bias_in, 32 * (h + 1))
                            dve.copy_predicated(bias[:, h % 2], namask[:, None, :].to_broadcast([P, 14, GRID]), braw[:, :, :])\
                               .then_inc(bias_done, 1)
                            dve.wait_ge(bias_done, h + 1)
                        dve.wait_ge(scores, i + 1)
                        if i >= 2:
                            dve.wait_ge(probT_done, i - 1)
                        dve.scalar_tensor_tensor(out=prob[:, i % 2, 0:512].rearrange("p (j k) -> p j k", k=GRID),
                                                 in0=PS[:, i % 2, :].rearrange("p (j k) -> p j k", k=GRID),
                                                 scalar=NA_D ** -0.5,
                                                 in1=bias[:, h % 2, 6 - 2 * qt:14 - 2 * qt, :],
                                                 op0=ALU.mult, op1=ALU.add)
                        dve.tensor_scalar(prob[:, i % 2, 512:], PS[:, 2 + 5 * (i % 2), 0:CTX], NA_D ** -0.5, None,
                                          ALU.mult).then_inc(scores_read, 1)
                        dve.wait_ge(scores_read, i + 1)
                        dve.tensor_reduce(nmax[:, i:i + 1], prob[:, i % 2, :], AX.X, ALU.max, negate=True).then_inc(smax, 1)
                    if 1 <= i <= NI:
                        j = i - 1
                        dve.wait_ge(probT_done, j + 1)
                        if j >= 2:
                            dve.wait_ge(pv_done, j - 1)
                        dve.tensor_copy(probT[:, j % 2, 512:], PS[:, 4, 0:CTX]).then_inc(pT_d, 1)
                        dve.wait_ge(exped, j + 1)
                        dch(dve, dve.reciprocal(rinv[:, j:j + 1], rsum[:, j:j + 1]))
                    if i >= 2:
                        j = i - 2
                        h, qt = divmod(j, TT)
                        dve.wait_ge(pv_done, j + 1)
                        dve.tensor_scalar(ona[:, qt, h * NA_D:(h + 1) * NA_D], PS[:, 5 + j % 2, 0:NA_D], rinv[:, j:j + 1], None,
                                          ALU.mult).then_inc(ona_done, 1)
                turn_out_lo(dve, onaT_lo, onaT_hi, 4, [0, 1, 2, 3])

            @block.tensor
            def _(pe):
                for name in na_names:
                    project(pe, name, acts)
                for name in na_names:
                    wait_tiles(pe, name)

                def score(i):
                    h, qt = divmod(i, TT)
                    rows = slice(64 * (h % 2), 64 * (h % 2) + 64)
                    if i >= 2:
                        pe.wait_ge(scores_read, i - 1)
                    q = qna[rows, h // 2, qt * P:(qt + 1) * P]
                    pe.matmul(PS[:, i % 2, :], q, kna[rows, h // 2, 0:SEQ], start=True, stop=True)
                    pe.matmul(PS[:, 2 + 5 * (i % 2), 0:CTX], q, kna[rows, h // 2, SEQ:], start=True, stop=True)\
                      .then_inc(scores, 1)

                def values(j):
                    h = j // TT
                    pe.wait_ge(pT_a, j + 1)
                    pe.wait_ge(pT_d, j + 1)
                    if j >= 2:
                        pe.wait_ge(ona_done, j - 1)
                    for t in range(TT + TC):
                        mm = pe.matmul(PS[:, 5 + j % 2, 0:NA_D], probT[:, j % 2, t * P:(t + 1) * P],
                                       vna[:, t, h * NA_D:(h + 1) * NA_D], start=(t == 0), stop=(t == TT + TC - 1))
                    mm.then_inc(pv_done, 1)

                score(0)
                for i in range(NI):
                    if i + 1 < NI:
                        score(i + 1)
                    if i >= 1:
                        values(i - 1)
                    pe.wait_ge(exped, i + 1)
                    for t in range(TT + TC):
                        mm = pe.transpose(PS[:, 3 + t // 4, (t % 4) * P:(t % 4 + 1) * P],
                                          prob[:, i % 2, t * P:(t + 1) * P], ident[:, :])
                    mm.then_inc(probT_done, 1)
                values(NI - 1)
                pe.wait_ge(ona_done, NI)
                turn(pe, lambda t, m: ona[:, t, m * P:(m + 1) * P], 4, [0, 1, 2, 3])

        if dump == "na":
            return finish(nc, out, es, sem, onaT_hi, onaT_lo)

        kgl = at("kgl", [P, GL_H, TOK], 132)
        vgl = at("vgl", [P, TT + TC, D], 144)
        qgl = at("qgl", [P, GL_H, SEQ], 168)
        lrT = at("lrT", [64, TOK], 176)
        ogl = at("ogl", [P, TT, D], 189)
        wgp = at("wgp", [P, KD, P], 189)
        wg_hi = at("wg_hi", [P, KD, P], 193, R)
        wg_lo = at("wg_lo", [P, KD, P], 197, R)
        wgr = at("wgr", [P, KD, 2 * RANK], 201)
        w2 = at("w2", [64, 512], 179)
        gate_in, w2_in, wgp_done, wg_done, lr_done, lr_out = (esem(n) for n in ("gate_in", "w2_in", "wgp", "wg", "lr", "lr_out"))
        gl_names = [("k_gla",), ("v_gla", 0), ("v_gla", 1), ("q_gla",)]
        LAST3 = CH[("q_gla",)]["last"]

        def kgl_at(kind, m):
            return kgl[:, m, SEQ:] if kind == "featc" else kgl[:, m, 0:SEQ]

        def vgl_at(j):
            return lambda kind, t: vgl[:, (TT if kind == "tokc" else 0) + t, 512 * j:512 * j + 512]

        gl_dst = [kgl_at, vgl_at(0), vgl_at(1), lambda kind, m: qgl[:, m, :]]
        with nc.Block() as block:
            @block.sync
            def _(sp):
                sp.dma_start(wgr[:, :, :], w_in[0].rearrange("(k p) n -> p k n", p=P)[:, :, GATE:GATE + 2 * RANK]).then_inc(gate_in, 16)
                for d in range(2):
                    sp.dma_start(w2[32 * d:32 * d + RANK, :], gla_gate_w[0, d]).then_inc(w2_in, 16)
                    sp.dma_start(w2[32 * d + RANK:32 * d + RANK + 1, :], gla_gate_b[:, d, :]).then_inc(w2_in, 16)
                sp.wait_ge(w2_in, 64)
                load_to(sp, LAST3 + 3)

            @block.scalar
            def _(act):
                for name, dst in zip(gl_names, gl_dst):
                    split_hi(act, CH[name]["last"] + 2)
                    copy_tiles(act, "A", name, dst, GL_DK ** -0.5 if name == ("q_gla",) else 1.0)
                act.wait_ge(wgp_done, 4)
                act.activation(wg_hi[:, :, :], wgp[:, :, :], ACT.Copy).then_inc(wg_done, 1)

            @block.vector
            def _(dve):
                dch(dve, dve.memset(wgp[:, :, :], 0.0))
                dve.memset(lrT[:, :], 1.0).then_inc(wgp_done, 1)
                dve.wait_ge(gate_in, 16)
                for d in range(2):
                    dve.tensor_copy(wgp[:, :, 32 * d:32 * d + RANK], wgr[:, :, RANK * d:RANK * d + RANK]).then_inc(wgp_done, 1)
                dve.wait_ge(wgp_done, 3)
                dve.tensor_copy(tiny[:, 0:1], wgp[:, 0, 0:1]).then_inc(wgp_done, 1)
                for name, dst in zip(gl_names, gl_dst):
                    split_lo(dve, CH[name]["last"] + 2)
                    copy_tiles(dve, "D", name, dst, GL_DK ** -0.5 if name == ("q_gla",) else 1.0)
                dve.wait_ge(wg_done, 1)
                dve.tensor_tensor(wg_lo[:, :, :], wgp[:, :, :], wg_hi[:, :, :].bitcast(F), ALU.subtract).then_inc(wg_done, 1)
                dve.wait_ge(lr_done, 1)
                for d in range(2):
                    rows = slice(32 * d, 32 * d + RANK)
                    dve.tensor_copy(lrT[rows, 0:SEQ], PS[rows, 0, :]).then_inc(lr_out, 1)
                    dve.tensor_copy(lrT[rows, SEQ:], PS[rows, 1, 0:CTX]).then_inc(lr_out, 1)

            @block.tensor
            def _(pe):
                for name in gl_names:
                    project(pe, name, acts)
                for name in gl_names:
                    wait_tiles(pe, name)
                pe.wait_ge(wg_done, 2)
                for b, (hi, lo, n) in enumerate(((hT_hi, hT_lo, SEQ), (hc_hi, hc_lo, CTX))):
                    for k in range(KD):
                        mm = mm3(pe, PS[:, b, 0:n], wg_hi[:, k], wg_lo[:, k], hi[:, k], lo[:, k], k == 0, k == KD - 1)
                mm.then_inc(lr_done, 1)

        state = at("state", [P, 2, GL_H, GL_DV], 100)
        smid = at("smid", [P, GL_H, GL_DV], 108)
        eq = at("eq", [P, GL_H, P], 112)
        ek = at("ek", [P, GL_H, P], 114)
        lgate = at("lgate", [P, 512], 181)
        tneg = at("tneg", [P, 512], 183)
        attn = at("attn", [P, GL_H, P], 185)
        kdec = at("kdec", [P, GL_H, P], 187)
        edges = tiny[:, 0:24].rearrange("p (w h e) -> p w h e", w=2, e=3)
        one = tiny[:, 24:25]
        (logit_done, absd, expd, lnd, gdone, cumd, dsub, kexp, kfd, qfd, smidd, kT_done, kT_out, atd, atm, od, oout, ud, sdone) = (
            esem("gl_" + n) for n in "logit abs exp ln gate cum diff decays kf qf smid kT kT_out attn attn_out o o_out update state".split())
        units = []
        order = {0: [("c", 0), ("c", 1)] + [("l", t) for t in range(TT)],
                 1: [("c", 1), ("c", 0)] + [("l", TT - 1 - t) for t in range(TT)]}
        seen = set()
        for j in range(TC + TT):
            for d in range(2):
                kind, t = order[d][j]
                lat = kind == "l"
                units.append(dict(d=d, j=j, lat=lat, t=t, tok=(0 if lat else SEQ) + t * P, vt=t if lat else TT + t,
                                  add=lat and t in seen, last=j == TC + TT - 1, nlat=sum(u["lat"] for u in units),
                                  nup=sum(not u["last"] for u in units)))
                if lat:
                    seen.add(t)
        NU = len(units)
        with nc.Block() as block:
            @block.sync
            def _(sp):
                pass

            @block.scalar
            def _(act):
                act.wait_ge(absd, 1)
                for u, un in enumerate(units):
                    d = un["d"]
                    act.wait_ge(logit_done, u + 1)
                    if u:
                        act.wait_ge(gdone, u)
                    act.activation(tneg[:, :], PS[:, 0, :], ACT.Abs).then_inc(absd, 1)
                    act.wait_ge(absd, u + 2)
                    act.activation(tneg[:, :], tneg[:, :], ACT.Exp, scale=-1.0).then_inc(expd, 1)
                    act.wait_ge(expd, u + 1)
                    act.activation(tneg[:, :], tneg[:, :], ACT.Ln, bias=one).then_inc(lnd, 1)
                    act.wait_ge(dsub, u + 1)
                    act.activation(ek[:, :, :], eq[:, :, :], ACT.Exp, scale=-1.0 / TAU).then_inc(kexp, 1)
                    act.wait_ge(kexp, 3 * u + 1)
                    act.activation(eq[:, :, :], eq[:, :, :], ACT.Exp, scale=1.0 / TAU).then_inc(kexp, 1)
                    act.activation(edges[:, d], edges[:, d], ACT.Exp, scale=1.0 / TAU).then_inc(kexp, 1)
                    if not un["last"]:
                        act.wait_ge(kT_done, un["nup"] + 1)
                        if un["nup"]:
                            act.wait_ge(ud, un["nup"])
                        act.activation(kdec[:, :, :], PS[:, 3, :], ACT.Copy).then_inc(kT_out, 1)

            @block.vector
            def _(dve):
                dve.memset(one, 1.0).then_inc(absd, 1)
                for u, un in enumerate(units):
                    d, t = un["d"], un["t"]
                    if u:
                        dve.wait_ge(cumd, u)
                    dve.wait_ge(lnd, u + 1)
                    dve.scalar_tensor_tensor(out=lgate[:, :], in0=PS[:, 0, :], scalar=0.0, in1=tneg[:, :],
                                             op0=ALU.min, op1=ALU.subtract).then_inc(gdone, 1)
                    dve.wait_ge(cumd, u + 1)
                    cum = PS[:, 1, :].rearrange("p (h t) -> p h t", h=GL_H)
                    mid, last = (63, P - 1) if d == 0 else (64, 0)
                    dve.tensor_copy(edges[:, d, :, 0:1], cum[:, :, mid:mid + 1])
                    dch(dve, dve.tensor_copy(edges[:, d, :, 1:2], cum[:, :, last:last + 1]))
                    dch(dve, dve.tensor_tensor(edges[:, d, :, 2:3], edges[:, d, :, 1:2], edges[:, d, :, 0:1], ALU.subtract))
                    if u:
                        dve.wait_ge(kT_done, units[u]["nup"])
                        if un["nlat"]:
                            dve.wait_ge(atd, un["nlat"])
                    dve.tensor_tensor(eq[:, :, :], cum, edges[:, d, :, 0:1].to_broadcast([P, GL_H, P]), ALU.subtract).then_inc(dsub, 1)
                    dve.wait_ge(kexp, 3 * u + 3)
                    dve.tensor_tensor(ek[:, :, :], kgl[:, :, un["tok"]:un["tok"] + P], ek[:, :, :], ALU.mult).then_inc(kfd, 1)
                    if un["lat"]:
                        dve.tensor_tensor(eq[:, :, :], qgl[:, :, un["tok"]:un["tok"] + P], eq[:, :, :], ALU.mult).then_inc(qfd, 1)
                        if un["nlat"]:
                            dve.wait_ge(od, un["nlat"])
                        dve.tensor_tensor(smid[:, :, :], state[:, d], edges[:, d, :, 0:1].to_broadcast([P, GL_H, GL_DV]), ALU.mult)\
                           .then_inc(smidd, 1)
                        dve.wait_ge(atd, un["nlat"] + 1)
                        dve.tensor_tensor(attn[:, :, :], PS[:, 2, :].rearrange("p (h t) -> p h t", h=GL_H),
                                          tri[:, d:d + 1, :].to_broadcast([P, GL_H, P]), ALU.mult).then_inc(atm, 1)
                    if un["lat"]:
                        dve.wait_ge(od, un["nlat"] + 1)
                        o = PS[:, 4:6, :].rearrange("p b n -> p (b n)")
                        if un["add"]:
                            dve.tensor_tensor(ogl[:, t, :], ogl[:, t, :], o, ALU.add).then_inc(oout, 1)
                        else:
                            dve.tensor_copy(ogl[:, t, :], o).then_inc(oout, 1)
                        dve.wait_ge(oout, un["nlat"] + 1)
                    if not un["last"]:
                        if un["j"]:
                            dch(dve, dve.tensor_tensor(state[:, d], state[:, d],
                                                       edges[:, d, :, 1:2].to_broadcast([P, GL_H, GL_DV]), ALU.mult))
                        dve.wait_ge(ud, un["nup"] + 1)
                        for h in range(GL_H):
                            upd = PS[:, 6 + h // 2, (h % 2) * GL_DV:(h % 2 + 1) * GL_DV]
                            if un["j"]:
                                ins = dve.scalar_tensor_tensor(out=state[:, d, h], in0=upd, scalar=edges[:, d, h, 2:3],
                                                               in1=state[:, d, h], op0=ALU.mult, op1=ALU.add)
                            else:
                                ins = dve.tensor_scalar(state[:, d, h], upd, edges[:, d, h, 2:3], None, ALU.mult)
                        ins.then_inc(sdone, 1)
                        dve.wait_ge(sdone, un["nup"] + 1)

            @block.tensor
            def _(pe):
                def logits(u):
                    un = units[u]
                    d, rows = un["d"], slice(32 * un["d"], 32 * un["d"] + RANK + 1)
                    if u:
                        pe.wait_ge(gdone, u)
                    pe.matmul(PS[:, 0, :], lrT[rows, un["tok"]:un["tok"] + P], w2[rows, :], start=True, stop=True).then_inc(logit_done, 1)

                logits(0)
                for u, un in enumerate(units):
                    d = un["d"]
                    pe.wait_ge(gdone, u + 1)
                    if u:
                        pe.wait_ge(dsub, u)
                    for h in range(GL_H):
                        mm = pe.matmul(PS[:, 1, h * P:(h + 1) * P], lgate[:, h * P:(h + 1) * P], tri[:, d, :], start=True, stop=True)
                    mm.then_inc(cumd, 1)
                    if u + 1 < NU:
                        logits(u + 1)
                    pe.wait_ge(kfd, u + 1)
                    if not un["last"]:
                        if un["nup"]:
                            pe.wait_ge(kT_out, un["nup"])
                        for h in range(GL_H):
                            mm = pe.transpose(PS[:, 3, h * P:(h + 1) * P], ek[:, h, :], ident[:, :])
                        mm.then_inc(kT_done, 1)
                    if un["lat"]:
                        pe.wait_ge(qfd, un["nlat"] + 1)
                        if un["nlat"]:
                            pe.wait_ge(atm, un["nlat"])
                        for h in range(GL_H):
                            mm = pe.matmul(PS[:, 2, h * P:(h + 1) * P], ek[:, h, :], eq[:, h, :], start=True, stop=True)
                        mm.then_inc(atd, 1)
                        pe.wait_ge(smidd, un["nlat"] + 1)
                        pe.wait_ge(atm, un["nlat"] + 1)
                        if un["nlat"]:
                            pe.wait_ge(oout, un["nlat"])
                        for h in range(GL_H):
                            o = PS[:, 4 + h // 2, (h % 2) * GL_DV:(h % 2 + 1) * GL_DV]
                            pe.matmul(o, attn[:, h, :], vgl[:, un["vt"], h * GL_DV:(h + 1) * GL_DV], start=True, stop=False)
                            mm = pe.matmul(o, eq[:, h, :], smid[:, h, :], start=False, stop=True)
                        mm.then_inc(od, 1)
                    if not un["last"]:
                        pe.wait_ge(kT_out, un["nup"] + 1)
                        if un["nup"]:
                            pe.wait_ge(sdone, un["nup"])
                        for h in range(GL_H):
                            mm = pe.matmul(PS[:, 6 + h // 2, (h % 2) * GL_DV:(h % 2 + 1) * GL_DV], kdec[:, h, :],
                                           vgl[:, un["vt"], h * GL_DV:(h + 1) * GL_DV], start=True, stop=True)
                        mm.then_inc(ud, 1)

        if dump == "gla":
            return finish(nc, out, es, sem, ogl)

        oglT_hi = at("oglT_hi", [P, KD, SEQ], 132, R)
        oglT_lo = at("oglT_lo", [P, KD, SEQ], 148, R)
        oscT_hi = at("oscT_hi", [P, 4, SEQ], 100, R)
        oscT_lo = at("oscT_lo", [P, 4, SEQ], 108, R)
        cT = at("cT", [P, 4, SEQ], 164)
        uT = at("uT", [P, 4, SEQ + 2], 172)
        sr = at("sr", [P, 2, 512], 181)
        gnr = at("gnr", [P, GL_DV], 185)
        jk = at("jk", [P, GL_DV], 186)
        bsc = sr
        gn_in, cw_in, osq, oms, opow, onrm, srd, srm, u0, ud2, cvd, bsd, bhi = (
            esem(n) for n in "gn_in cw_in o_squares o_ms o_rstd o_normed silu_r gated u_edges u_done conv b_times sc_hi".split())
        LAST5 = CH[("b",)]["last"]
        with nc.Block() as block:
            @block.sync
            def _(sp):
                sp.dma_start(gnr[:, :], bass.AP(tensor=gla_norm_g.tensor, offset=0, ap=[[0, P], [1, GL_DV]])).then_inc(gn_in, 16)
                for w in range(3):
                    sp.dma_start(convw[:, w, :], conv_w[0, w].rearrange("(m p) -> p m", p=P), allow_slow_non_contiguous=True)\
                      .then_inc(cw_in, 16)
                load_to(sp, LAST5 + 3)

            @block.gpsimd
            def _(pool):
                pool.wait_ge(oms, 1)
                pool.tensor_tensor(rstd[:, 0:16], ssum[:, 0:16], mhalf[:, 0:16], ALU.pow).then_inc(opow, 1)

            @block.scalar
            def _(act):
                for t in range(TT):
                    for h in range(GL_H):
                        ach(act, act.activation(jk[:, :], ogl[:, t, h * GL_DV:(h + 1) * GL_DV], ACT.Square,
                                                accum_out=ssum[:, GL_H * t + h:GL_H * t + h + 1]))
                act.copy(tiny[:, 67:68], ssum[:, 0:1]).then_inc(osq, 1)
                for j in range(2):
                    split_hi(act, CH[("r", j)]["last"] + 2)
                    for tile in CH[("r", j)]["tiles"]:
                        act.wait_ge(tile_done, tile["n"] + 1)
                        n = TT * j + tile["t"]
                        if n >= 2:
                            act.wait_ge(srm, n - 1)
                        act.activation(sr[:, n % 2, :], PS[:, tile["bank"], :], ACT.Silu).then_inc(emptied["A"], 1)
                split_hi(act, CH[("c",)]["last"] + 2)
                copy_tiles(act, "A", ("c",), lambda kind, m: cT[:, m, :])
                split_hi(act, CH[("x",)]["last"] + 2)
                split_hi(act, CH[("b",)]["last"] + 2)
                for m in range(4):
                    act.wait_ge(bsd, m + 1)
                    act.activation(oscT_hi[:, m, :], bsc[:, m % 2, :], ACT.Copy).then_inc(bhi, 1)
                turn_out_hi(act, oglT_hi, KD, [0, 1, 2, 3])

            @block.vector
            def _(dve):
                dve.wait_ge(osq, 1)
                dve.tensor_scalar(ssum[:, 0:16], ssum[:, 0:16], 1.0 / GL_DV, EPS, ALU.mult, ALU.add).then_inc(oms, 1)
                dve.memset(uT[:, :, 0:SEQ + 2:SEQ + 1], 0.0).then_inc(u0, 1)
                dve.wait_ge(opow, 1)
                dve.wait_ge(gn_in, 16)
                for t in range(TT):
                    for h in range(GL_H):
                        n = GL_H * t + h
                        o = ogl[:, t, h * GL_DV:(h + 1) * GL_DV]
                        ins = dve.scalar_tensor_tensor(out=o, in0=o, scalar=rstd[:, n:n + 1], in1=gnr[:, :],
                                                       op0=ALU.mult, op1=ALU.mult)
                ins.then_inc(onrm, 1)
                dve.wait_ge(onrm, 1)
                for j in range(2):
                    split_lo(dve, CH[("r", j)]["last"] + 2)
                    for tile in CH[("r", j)]["tiles"]:
                        n = TT * j + tile["t"]
                        dve.wait_ge(emptied["A"], tile["nth"])
                        o = ogl[:, tile["t"], 512 * j:512 * j + 512]
                        dve.tensor_tensor(o, o, sr[:, n % 2, :], ALU.mult).then_inc(srm, 1)
                split_lo(dve, CH[("x",)]["last"] + 2)
                for tile in CH[("x",)]["tiles"]:
                    m = tile["t"]
                    dve.wait_ge(tile_done, tile["n"] + 1)
                    wait_tiles(dve, ("c",))
                    dve.tensor_tensor(uT[:, m, 1:SEQ + 1], PS[:, tile["bank"], :], cT[:, m, :], ALU.mult).then_inc(emptied["D"], 1)
                wait_tiles(dve, ("x",))
                dve.wait_ge(cw_in, 48)
                dve.wait_ge(u0, 1)
                for w in range(3):
                    for m in range(4):
                        if w == 0:
                            ins = dve.tensor_scalar(cT[:, m, :], uT[:, m, 0:SEQ], convw[:, 0, m:m + 1], None, ALU.mult)
                        else:
                            ins = dve.scalar_tensor_tensor(out=cT[:, m, :], in0=uT[:, m, w:SEQ + w], scalar=convw[:, w, m:m + 1],
                                                           in1=cT[:, m, :], op0=ALU.mult, op1=ALU.add)
                    dch(dve, ins)
                split_lo(dve, CH[("b",)]["last"] + 2)
                dve.wait_ge(srm, 2 * TT)
                for tile in CH[("b",)]["tiles"]:
                    m = tile["t"]
                    dve.wait_ge(tile_done, tile["n"] + 1)
                    dve.tensor_tensor(bsc[:, m % 2, :], PS[:, tile["bank"], :], cT[:, m, :], ALU.mult).then_inc(bsd, 1)
                    dve.wait_ge(bhi, m + 1)
                    dve.tensor_tensor(oscT_lo[:, m, :], bsc[:, m % 2, :], oscT_hi[:, m, :].bitcast(F), ALU.subtract).then_inc(emptied["D"], 1)
                    dve.wait_ge(emptied["D"], tile["nth"])
                turn_out_lo(dve, oglT_lo, oglT_hi, KD, [0, 1, 2, 3])

            @block.tensor
            def _(pe):
                for name in (("r", 0), ("r", 1), ("c",), ("x",), ("b",)):
                    project(pe, name, acts)
                wait_tiles(pe, ("b",))
                wait_tiles(pe, ("c",))
                pe.wait_ge(srm, 2 * TT)
                turn(pe, lambda t, m: ogl[:, t, m * P:(m + 1) * P], KD, [0, 1, 2, 3])

        yT_hi = at("yT_hi", [P, KD, SEQ], 164, R)
        yT_lo = at("yT_lo", [P, KD, SEQ], 180, R)
        yacc = at("yacc", [P, 4, SEQ], 196)
        sgate = at("sgate", [P, 4, SEQ], 4)
        ymul, yhi = sem("y_times"), sem("y_hi")
        branch = {"b0": (onaT_hi, onaT_lo), "b1": (oscT_hi, oscT_lo), "b2": (oglT_hi, oglT_lo)}
        LAST6 = CH[("br", 1, 2)]["last"]
        jb = [(j, br) for j in range(2) for br in range(3)]
        with nc.Block() as block:
            @block.sync
            def _(sp):
                load_to(sp, LAST6 + 3)

            @block.gpsimd
            def _(pool):
                for s in early_sems:
                    pool.sem_clear(s)

            @block.scalar
            def _(act):
                for n, (j, br) in enumerate(jb):
                    split_hi(act, CH[("gate", j, br)]["last"] + 2)
                    for tile in CH[("gate", j, br)]["tiles"]:
                        act.wait_ge(tile_done, tile["n"] + 1)
                        if n:
                            act.wait_ge(emptied["D"], CH[("br", *jb[n - 1])]["tiles"][tile["t"]]["nth"])
                        act.activation(sgate[:, tile["t"], :], PS[:, tile["bank"], :], ACT.Sigmoid).then_inc(emptied["A"], 1)
                    split_hi(act, CH[("br", j, br)]["last"] + 2)
                    if br == 2:
                        for tile in CH[("br", j, br)]["tiles"]:
                            act.wait_ge(emptied["D"], tile["nth"])
                            act.activation(yT_hi[:, 4 * j + tile["t"], :], yacc[:, tile["t"], :], ACT.Copy).then_inc(yhi, 1)

            @block.vector
            def _(dve):
                for n, (j, br) in enumerate(jb):
                    split_lo(dve, CH[("gate", j, br)]["last"] + 2)
                    split_lo(dve, CH[("br", j, br)]["last"] + 2)
                    for tile in CH[("br", j, br)]["tiles"]:
                        m = tile["t"]
                        dve.wait_ge(tile_done, tile["n"] + 1)
                        dve.wait_ge(emptied["A"], CH[("gate", j, br)]["tiles"][m]["nth"])
                        if br == 0:
                            dve.tensor_tensor(yacc[:, m, :], PS[:, tile["bank"], :], sgate[:, m, :], ALU.mult).then_inc(emptied["D"], 1)
                        else:
                            dch(dve, dve.tensor_tensor(sgate[:, m, :], PS[:, tile["bank"], :], sgate[:, m, :], ALU.mult))
                            dve.tensor_tensor(yacc[:, m, :], yacc[:, m, :], sgate[:, m, :], ALU.add).then_inc(emptied["D"], 1)
                    dve.wait_ge(emptied["D"], CH[("br", j, br)]["tiles"][-1]["nth"])
                    if br == 2:
                        for m in range(4):
                            dve.wait_ge(yhi, 4 * j + m + 1)
                            ins = dve.tensor_tensor(yT_lo[:, 4 * j + m, :], yacc[:, m, :], yT_hi[:, 4 * j + m, :].bitcast(F), ALU.subtract)
                        dch(dve, ins)

            @block.tensor
            def _(pe):
                for j, br in jb:
                    project(pe, ("gate", j, br), acts)
                    project(pe, ("br", j, br), lambda kind: branch[kind])

        early.close()
        if dump == "y":
            return finish(nc, out, es, sem, yT_hi)

        x1 = at("x1", [P, TT, D], 68)
        shacc = at("shacc", [P, TT, D], 84)
        gt2 = at("gt2", [P, D], 100)
        gt1 = at("gt1", [P, D], 104)
        sh2 = at("sh2", [P, D], 108)
        sc2 = at("sc2", [P, D], 112)
        bm4 = at("bm4", [P, 4, D], 116)
        g2r = at("g2r", [P, D], 132)
        ptmp = at("ptmp", [P, 2, 512], 136)
        brt = at("brt", [P, NE], 140)
        h2 = at("h2", [P, TT, D], 148)
        wr = at("wr", [P, KD, NE], 196)
        wr_hi = at("wr_hi", [P, KD, NE], 198, R)
        wr_lo = at("wr_lo", [P, KD, NE], 200, R)
        h2T_hi = at("h2T_hi", [P, KD, SEQ], 164, R)
        h2T_lo = at("h2T_lo", [P, KD, SEQ], 180, R)
        rows_in, cs2, x1d, h2d, g1rows, sqd2, ms2, pw2, wrd = (sem(n) for n in "rows_in csel2 x1 h2 rows squares2 ms2 rstd2 wr".split())
        h2_out, rt_done = sem("h2_out"), sem("router")
        h2_dram = dram("h2_dram", [SEQ, D])
        LASTM = CH[("out", 1)]["last"]
        with nc.Block() as block:
            @block.sync
            def _(sp):
                sp.dma_start(x1[:, :, :], x[0].rearrange("(t p) d -> p t d", p=P)).then_inc(rows_in, 16)
                sp.dma_start(bm4[:, :, :], bass.AP(tensor=b_mod.tensor, offset=2 * D, ap=[[0, P], [D, 4], [1, D]])).then_inc(rows_in, 16)
                load_to(sp, CH[("row", "gt2", 1)]["last"] + 3)

            @block.gpsimd
            def _(pool):
                pool.dma_start(g2r[:, :], bass.AP(tensor=g_norm2.tensor, offset=0, ap=[[0, P], [1, D]])).then_inc(cpy, 16)
                pool.wait_ge(cpy, 32)
                pool.wait_ge(ms2, 1)
                pool.tensor_tensor(rstd[:, 0:TT], ssum[:, 0:TT], mhalf[:, 0:TT], ALU.pow).then_inc(pw2, 1)

            @block.scalar
            def _(act):
                for name in (("row", "gt1", 0), ("row", "gt1", 1), ("out", 0), ("out", 1)):
                    split_hi(act, CH[name]["last"] + 2)
                act.wait_ge(x1d, 2 * TT)
                for t in range(TT):
                    ach(act, act.activation(ptmp[:, :, :], x1[:, t, :], ACT.Square, accum_out=ssum[:, t:t + 1]))
                act.copy(tiny[:, 67:68], ssum[:, 0:1]).then_inc(sqd2, 1)
                for n in ("sh2", "sc2", "gt2"):
                    for j in range(2):
                        split_hi(act, CH[("row", n, j)]["last"] + 2)

            @block.vector
            def _(dve):
                build_csel(dve, [(0, 0, P)])
                dve.tensor_copy(tiny[:, 66:67], csil[:, 0, 0:1]).then_inc(cs2, 1)
                dve.wait_ge(rows_in, 32)

                def rows(n, idx, dst):
                    for j in range(2):
                        split_lo(dve, CH[("row", n, j)]["last"] + 2)
                        tile = CH[("row", n, j)]["tiles"][0]
                        dve.wait_ge(tile_done, tile["n"] + 1)
                        dve.tensor_tensor(dst[:, 512 * j:512 * j + 512], PS[:, tile["bank"], :], bm4[:, idx, 512 * j:512 * j + 512],
                                          ALU.add).then_inc(emptied["D"], 1)
                    dve.wait_ge(emptied["D"], tile["nth"])

                rows("gt1", 0, gt1)
                for j in range(2):
                    split_lo(dve, CH[("out", j)]["last"] + 2)
                    for tile in CH[("out", j)]["tiles"]:
                        t = tile["t"]
                        dve.wait_ge(tile_done, tile["n"] + 1)
                        dve.tensor_tensor(ptmp[:, t % 2, :], PS[:, tile["bank"], :], gt1[:, 512 * j:512 * j + 512], ALU.mult)\
                           .then_inc(emptied["D"], 1)
                        dve.wait_ge(emptied["D"], tile["nth"])
                        o = x1[:, t, 512 * j:512 * j + 512]
                        dve.tensor_tensor(o, o, ptmp[:, t % 2, :], ALU.add).then_inc(x1d, 1)
                dve.wait_ge(sqd2, 1)
                dve.tensor_scalar(ssum[:, 0:TT], ssum[:, 0:TT], 1.0 / D, EPS, ALU.mult, ALU.add).then_inc(ms2, 1)
                rows("sh2", 1, sh2)
                rows("sc2", 2, sc2)
                rows("gt2", 3, gt2)
                dve.wait_ge(cpy, 32)
                dch(dve, dve.scalar_tensor_tensor(out=sc2[:, :], in0=sc2[:, :], scalar=1.0, in1=g2r[:, :], op0=ALU.add, op1=ALU.mult))
                dve.wait_ge(pw2, 1)
                for t in range(TT):
                    dch(dve, dve.scalar_tensor_tensor(out=h2[:, t, :], in0=x1[:, t, :], scalar=rstd[:, t:t + 1], in1=sc2[:, :],
                                                      op0=ALU.mult, op1=ALU.mult))
                    dve.tensor_tensor(h2[:, t, :], h2[:, t, :], sh2[:, :], ALU.add).then_inc(h2d, 1)

            @block.tensor
            def _(pe):
                pe.wait_ge(cs2, 1)
                cs = lambda kind: (csel_hi, csel_lo)
                for j in range(2):
                    project(pe, ("row", "gt1", j), cs)
                for j in range(2):
                    project(pe, ("out", j), lambda kind: (yT_hi, yT_lo))
                for n in ("sh2", "sc2", "gt2"):
                    for j in range(2):
                        project(pe, ("row", n, j), cs)

        if dump == "h2":
            return finish(nc, out, es, sem, h2)
        wk = at("wk", [P, TT, TOPK], 202)
        dest = at("dest", [P, TT, TOPK], 202.25, U32)
        tokidx = at("tokidx", [P, NBLK], 202.5, U32)
        blkrow = at("blkrow", [1, P], 203, I32)
        blkcol = at("blkcol", [P, 4], 203.5)
        blkint = at("blkint", [P, 4], 203.625, I32)
        iota = at("iota", [P, TT], 203.75)
        slot = at("slot", [P, TT * TOPK], 203.875)
        pad = at("pad", [P, P], 204)
        ones = at("ones", [P, P], 204.5)
        shid = at("shid", [P, TT, FF], 104)
        sgl = at("sgl", [P, TT, FF], 108)
        sT_hi = at("sT_hi", [P, 2, SEQ], 112, R)
        sT_lo = at("sT_lo", [P, 2, SEQ], 116, R)

        def pk(name, shape, kb):
            return at(name, [P] + shape, kb)

        score, sel, selm, rep = (pk(n, [TT, NE], 120 + i) for i, n in enumerate(("score", "sel", "selm", "rep")))
        chosen, gw, vpos = (pk(n, [TT, NE], 124 + i) for i, n in enumerate(("chosen", "gw", "vpos")))
        g8 = pk("g8", [TT, NG, 8], 127)
        gs, gtop, gmask, top8, d1 = (pk(n, [TT, 8], 128 + 0.125 * i) for i, n in enumerate(("gs", "gtop", "gmask", "top8", "d1")))
        wsum = pk("wsum", [TT], 128.75)
        cnt, nbl, bend, bst, jle = (pk(n, [NE], 129 + 0.25 * i) for i, n in enumerate(("cnt", "nbl", "bend", "bst", "jle")))
        eqk = pk("eqk", [TOPK, NE], 131)
        (wr_in, h2T_done, scored, sgd, hidd, chosen_done, rank_done, rank_read, dest_done, blk_done, zeros2, sc_out,
         tok0, tokd, blk_out, blk_in, ones_done, shd) = (sem(n) for n in (
             "wr_in h2T scored sh_silu sh_hid chosen ranks ranks_read dest blocks zeros2 lists_out lists_zero "
             "lists_in blk_out blk_in ones sh_down").split())
        tok_dram = dram("tok_dram", [NBLK * P, 1])
        blk_dram = dram("blk_dram", [P, 1], I32)
        sh_tiles = CH[("sh",)]["tiles"]
        nb = [(sh_tiles[0]["bank"] + i) % 8 for i in range(8)]
        B_RT, B_RK, B_CT, B_T2 = nb[4], nb[5], nb[6], nb[7]
        turn_banks = [b for b in range(4)]
        with nc.Block() as block:
            @block.sync
            def _(sp):
                sp.dma_start(wr[:, :, :], w_router[0].rearrange("(k p) n -> p k n", p=P)).then_inc(wr_in, 16)
                sp.dma_start(brt[:, :], bass.AP(tensor=b_router.tensor, offset=0, ap=[[0, P], [1, NE]])).then_inc(wr_in, 16)
                sp.dma_start(iota[:, :], k_iota).then_inc(wr_in, 16)
                sp.dma_start(slot[:, :], k_slot).then_inc(wr_in, 16)
                sp.dma_start(h2_dram.rearrange("(t p) d -> p t d", p=P), h2[:, :, :]).then_inc(h2_out, 16)
                load_to(sp, len(HALVES))
                sp.wait_ge(blk_done, 1)
                sp.dma_start(blk_dram[:, :], blkint[:, 0:1], allow_slow_non_contiguous=True).then_inc(blk_out, 16)
                sp.wait_ge(blk_out, 16)
                sp.dma_start(blkrow[:, :], blk_dram.rearrange("p a -> a p")).then_inc(blk_in, 16)
                sp.wait_ge(h2_out, 16)
                sp.wait_ge(blk_in, 16)

            @block.gpsimd
            def _(pool):
                pool.memset(pad[:, :], PAD).then_inc(zeros2, 1)
                pool.memset(ones[:, :], 1.0).then_inc(ones_done, 1)
                pool.wait_ge(zeros2, 1)
                pool.dma_start(tok_dram.rearrange("(b p) a -> b (p a)", p=P), pad[0:NBLK, :]).then_inc(tok0, 16)
                pool.wait_ge(tok0, 16)
                pool.wait_ge(wr_in, 64)
                pool.wait_ge(dest_done, 1)
                for t in range(TT):
                    for k in range(TOPK):
                        pool.indirect_dma_start(tok_dram, bass.IndirectOffsetOnAxis(ap=dest[:, t, k:k + 1], axis=0),
                                                slot[:, t * TOPK + k:t * TOPK + k + 1], None).then_inc(sc_out, 16)
                pool.wait_ge(sc_out, 16 * TT * TOPK)

            @block.scalar
            def _(act):
                act.wait_ge(wr_in, 64)
                act.activation(wr_hi[:, :, :], wr[:, :, :], ACT.Copy).then_inc(wrd, 1)
                turn_out_hi(act, h2T_hi, KD, turn_banks)
                act.wait_ge(h2T_done, 1)
                act.activation(score[:, :, :], PS[:, B_RT, 0:TT * NE], ACT.Sigmoid).then_inc(scored, 1)
                split_hi(act, CH[("sh",)]["last"] + 2)
                for tile in sh_tiles:
                    act.wait_ge(tile_done, tile["n"] + 1)
                    act.activation(sgl[:, tile["t"], :], PS[:, tile["bank"], 0:FF], ACT.Silu).then_inc(sgd, 1)
                turn_out_hi(act, sT_hi, 2, [B_T2, B_RT])

            @block.vector
            def _(dve):
                dve.wait_ge(wrd, 1)
                dve.tensor_tensor(wr_lo[:, :, :], wr[:, :, :], wr_hi[:, :, :].bitcast(F), ALU.subtract).then_inc(wrd, 1)
                turn_out_lo(dve, h2T_lo, h2T_hi, KD, turn_banks)
                split_lo(dve, CH[("sh",)]["last"] + 2)
                dve.wait_ge(scored, 1)
                dch(dve, dve.tensor_tensor(sel[:, :, :], score[:, :, :], brt[:, None, :].to_broadcast([P, TT, NE]), ALU.add))
                for t in range(TT):
                    for g in range(NG):
                        ins = dve.max(g8[:, t, g, :], sel[:, t, g * 8:(g + 1) * 8])
                dch(dve, ins)
                dch(dve, dve.tensor_tensor(gs[:, :, :], g8[:, :, :, 0], g8[:, :, :, 1], ALU.add))
                for t in range(TT):
                    ins = dve.max(gtop[:, t, :], gs[:, t, :])
                dch(dve, ins)
                dch(dve, dve.tensor_tensor(gmask[:, :, :], gs[:, :, :], gtop[:, :, TOPG - 1:TOPG].to_broadcast([P, TT, NG]), ALU.is_ge))
                gm = gmask[:, :, :, None].to_broadcast([P, TT, NG, NE // NG])
                r4 = lambda a: a[:, :, :].rearrange("p t (g e) -> p t g e", g=NG)
                dch(dve, dve.tensor_tensor(r4(selm), r4(sel), gm, ALU.mult))
                dch(dve, dve.tensor_scalar(gmask[:, :, :], gmask[:, :, :], 1.0, -NEG, ALU.subtract, ALU.mult))
                dch(dve, dve.tensor_tensor(r4(selm), r4(selm), gm, ALU.add))
                for t in range(TT):
                    ins = dve.max(top8[:, t, :], selm[:, t, :])
                dch(dve, ins)
                for t in range(TT):
                    ins = dve.match_replace(rep[:, t, :], top8[:, t, :], selm[:, t, :], -3e38)
                dch(dve, ins)
                dve.tensor_tensor(chosen[:, :, :], rep[:, :, :], selm[:, :, :], ALU.not_equal).then_inc(chosen_done, 1)
                dve.wait_ge(chosen_done, 1)
                dch(dve, dve.tensor_tensor(gw[:, :, :], score[:, :, :], chosen[:, :, :], ALU.mult))
                dch(dve, dve.tensor_reduce(wsum[:, :], gw[:, :, :], AX.X, ALU.add))
                dch(dve, dve.reciprocal(wsum[:, :], wsum[:, :]))
                dch(dve, dve.scalar_tensor_tensor(out=gw[:, :, :], in0=gw[:, :, :], scalar=ROUTED_SCALE,
                                                  in1=wsum[:, :, None].to_broadcast([P, TT, NE]), op0=ALU.mult, op1=ALU.mult))
                dve.wait_ge(rank_done, 1)
                dch(dve, dve.tensor_copy(cnt[:, :], PS[:, B_CT, 0:NE]))
                dch(dve, dve.tensor_scalar(nbl[:, :], cnt[:, :], 0.0, None, ALU.is_gt))
                for m in range(1, TT):
                    dch(dve, dve.scalar_tensor_tensor(out=nbl[:, :], in0=cnt[:, :], scalar=float(m * P), in1=nbl[:, :],
                                                      op0=ALU.is_gt, op1=ALU.add))
                dch(dve, dve.tensor_tensor_scan(bend[:, :], ones[:, 0:NE], nbl[:, :], 0.0, ALU.mult, ALU.add))
                dch(dve, dve.tensor_tensor(bst[:, :], bend[:, :], nbl[:, :], ALU.subtract))
                dve.scalar_tensor_tensor(out=vpos[:, :, :], in0=bst[:, None, :].to_broadcast([P, TT, NE]), scalar=float(P),
                                         in1=PS[:, B_RK, 0:TT * NE].rearrange("p (t e) -> p t e", t=TT),
                                         op0=ALU.mult, op1=ALU.add).then_inc(rank_read, 1)
                dve.wait_ge(rank_read, 1)
                dch(dve, dve.scalar_tensor_tensor(out=vpos[:, :, :], in0=vpos[:, :, :], scalar=1.0, in1=chosen[:, :, :],
                                                  op0=ALU.add, op1=ALU.mult))
                for t in range(TT):
                    ins = dve.max(d1[:, t, :], vpos[:, t, :])
                dch(dve, ins)
                dve.tensor_scalar(dest[:, :, :], d1[:, :, :], 1.0, None, ALU.subtract).then_inc(dest_done, 1)
                dch(dve, dve.tensor_scalar(jle[:, :], bend[:, :], iota[:, 0:1], None, ALU.is_le))
                dch(dve, dve.tensor_reduce(blkcol[:, 0:1], jle[:, :], AX.X, ALU.add))
                dch(dve, dve.tensor_scalar(blkcol[:, 1:2], bend[:, NE - 1:NE], 0.5, 0.25 - 2, ALU.mult, ALU.add))
                dch(dve, dve.tensor_scalar(blkint[:, 1:2], blkcol[:, 1:2], ROUND, ROUND, ALU.add, ALU.subtract))
                dve.tensor_scalar(blkint[:, 0:1], blkcol[:, 0:1], float(NE - 1), None, ALU.min).then_inc(blk_done, 1)
                for t in range(TT):
                    vb = vpos[:, t:t + 1, :].to_broadcast([P, TOPK, NE])
                    dch(dve, dve.tensor_tensor(eqk[:, :, :], vb, d1[:, t, :, None].to_broadcast([P, TOPK, NE]), ALU.is_equal))
                    dch(dve, dve.tensor_tensor(eqk[:, :, :], eqk[:, :, :], gw[:, t:t + 1, :].to_broadcast([P, TOPK, NE]), ALU.mult))
                    dch(dve, dve.tensor_reduce(wk[:, t, :], eqk[:, :, :], AX.X, ALU.add))
                for tile in sh_tiles:
                    dve.wait_ge(sgd, tile["t"] + 1)
                    dve.tensor_tensor(shid[:, tile["t"], :], PS[:, tile["bank"], FF:], sgl[:, tile["t"], :], ALU.mult).then_inc(emptied["D"], 1)
                split_lo(dve, len(HALVES))
                turn_out_lo(dve, sT_lo, sT_hi, 2, [B_T2, B_RT])
                for tile in CH[("down",)]["tiles"]:
                    dve.wait_ge(tile_done, tile["n"] + 1)
                    t, h = divmod(tile["t"], 2)
                    dve.tensor_copy(shacc[:, t, 512 * h:512 * h + 512], PS[:, tile["bank"], :]).then_inc(emptied["D"], 1)

            @block.tensor
            def _(pe):
                turn(pe, lambda t, m: h2[:, t, m * P:(m + 1) * P], KD, turn_banks)
                pe.wait_ge(turn_lo, nturn[0])
                pe.wait_ge(wrd, 2)
                for t in range(TT):
                    for k in range(KD):
                        lhs = slice(t * P, (t + 1) * P)
                        mm = mm3(pe, PS[:, B_RT, t * NE:(t + 1) * NE], h2T_hi[:, k, lhs], h2T_lo[:, k, lhs], wr_hi[:, k], wr_lo[:, k],
                                 k == 0, k == KD - 1)
                mm.then_inc(h2T_done, 1)
                project(pe, ("sh",), lambda kind: (h2T_hi, h2T_lo))
                pe.wait_ge(chosen_done, 1)
                pe.wait_ge(ones_done, 1)
                for t in range(TT):
                    for j in range(t + 1):
                        pe.matmul(PS[:, B_RK, t * NE:(t + 1) * NE], tri[:, 2, :] if j == t else ones[:, :], chosen[:, j, :],
                                  start=(j == 0), stop=(j == t))
                for j in range(TT):
                    mm = pe.matmul(PS[:, B_CT, 0:NE], ones[:, :], chosen[:, j, :], start=(j == 0), stop=(j == TT - 1))
                mm.then_inc(rank_done, 1)
                pe.wait_ge(emptied["D"], sh_tiles[-1]["nth"])
                turn(pe, lambda t, m: shid[:, t, m * P:(m + 1) * P], 2, [B_T2, B_RT])
                pe.wait_ge(turn_lo, nturn[0])
                project(pe, ("down",), lambda kind: (sT_hi, sT_lo))

        wraw = at("wraw", [P, 6, 2048], 104)
        mhi = at("mhi", [P, 3, 2048], 152, R)
        mlo = at("mlo", [P, 3, 2048], 176, R)
        tokT = at("tokT", [NBLK, P], 200)
        xg = at("xg", [P, 2, D], 12)
        xT_hi = at("xT_hi", [P, 2, KD, P], 20, R)
        xT_lo = at("xT_lo", [P, 2, KD, P], 28, R)
        mhid = at("mhid", [P, 2, FF], 36)
        hT2_hi = at("hT2_hi", [P, 2, 2, P], 38, R)
        hT2_lo = at("hT2_lo", [P, 2, 2, P], 40, R)
        ysb = at("ysb", [P, 2, D], 42)
        msg = at("msg", [P, 2, FF], 50)
        idxcur = at("idxcur", [P, 2], 52, U32)
        slotcur = at("slotcur", [P, 2], 52.125, U32)
        slotidx = at("slotidx", [P, NBLK], 52.5, U32)
        tokf = at("tokf", [P, NBLK], 53)
        y_dram = dram("y_dram", [SEQ * TOPK, D])
        wland = [sem(f"expert_landed{i}") for i in range(6)]
        (tokT_in, tokT_t, tokidx_done, mhi_done, mlo_done, piece_free, idx_done, idx_seen, xT_t, xT_hid, xT_lod,
         gu_done, silud, mhidd, hT_t, hT_hid, hT_lod, dn_done, y_a, y_d, slot_done, xg_zero) = (sem(n) for n in (
             "lists_back lists_turned tokidx ex_hi ex_lo piece_used idx_col idx_seen ex_xT ex_xT_hi ex_xT_lo "
            "ex_gate_up ex_silu ex_hid ex_hidT ex_hidT_hi ex_hidT_lo ex_down y_act y_dve slot_col ex_x_zero".split()))
        xg_in, y_out = ([sem(f"{n}{u}") for u in range(2)] for n in ("expert_x_in", "y_out"))
        DS = bass.ds
        NP_ = NBLK // 2
        MINBLK = SEQ * TOPK // P

        def pairs(eng, body):
            n_pairs = eng.value_load(blkint[0:1, 1:2], min_val=MINBLK // 2 - 2, max_val=NP_ - 2) + 2
            for b in range(4):
                body(b // 2, b % 2, b == 0)
            with eng.Fori(2, NP_) as i:
                with eng.If(i < n_pairs):
                    for u in range(2):
                        body(i, u, False)
            return n_pairs

        with nc.Block() as block:
            @block.sync
            def _(sp):
                sp.dma_start(tokT[:, :], tok_dram.rearrange("(b p) a -> b (p a)", p=P)).then_inc(tokT_in, 16)

                def body(i, u, first):
                    e = sp.value_load(blkrow[0:1, DS(i * 2 + u, 1)], min_val=0, max_val=NE - 1)
                    for pc in range(3):
                        s = 3 * u + pc
                        if not (isinstance(i, int) and i == 0):
                            sp.wait_ge(mlo_done, i * 6 + (s - 5))
                        if pc < 2:
                            dst = wraw[:, s].rearrange("p (c g f) -> p c g f", c=4, g=2)
                            for g, w in enumerate((w_exp_gate, w_exp_up)):
                                src = w[0][DS(e, 1)].rearrange("a (p c) f -> p (a c) f", p=P)[:, 4 * pc:4 * pc + 4, :]
                                sp.dma_start(dst[:, :, g, :], src).then_inc(wland[s], 16)
                        else:
                            src = w_exp_down[0][DS(e, 1)].rearrange("a (p c) n -> p (a c n)", p=P)
                            sp.dma_start(wraw[:, s], src).then_inc(wland[s], 16)
                pairs(sp, body)

            @block.gpsimd
            def _(pool):
                pool.memset(xg[:, :, :], 0.0).then_inc(xg_zero, 1)
                pool.wait_ge(xg_zero, 1)
                pool.wait_ge(tokidx_done, 1)

                def store(i, u, back):
                    b = i * 2 + (u - back)
                    if not (isinstance(b, int) and b < 2):
                        pool.wait_ge(y_out[(u - back) % 2], i * 16 - 16)
                    pool.wait_ge(y_a, b + 1)
                    pool.wait_ge(y_d, b + 1)
                    v = (u - back) % 2
                    pool.tensor_copy(slotcur[:, v:v + 1], slotidx[:, DS(b, 1)]).then_inc(slot_done, 1)
                    pool.wait_ge(slot_done, b + 1)
                    pool.sem_inc(idx_seen, 1)
                    pool.indirect_dma_start(y_dram, bass.IndirectOffsetOnAxis(ap=slotcur[:, v:v + 1], axis=0), ysb[:, v, :], None,
                                            bounds_check=SEQ * TOPK - 1, oob_is_err=False).then_inc(y_out[v], 16)

                def body(i, u, first):
                    b = i * 2 + u
                    late = not (isinstance(i, int) and i == 0)
                    if late:
                        pool.wait_ge(xg_in[u], i * 16)
                        pool.wait_ge(xT_t, b - 1)
                    pool.tensor_copy(idxcur[:, u:u + 1], tokidx[:, DS(b, 1)]).then_inc(idx_done, 1)
                    pool.wait_ge(idx_done, b + 1)
                    pool.sem_inc(idx_seen, 1)
                    pool.indirect_dma_start(xg[:, u, :], None, h2_dram, bass.IndirectOffsetOnAxis(ap=idxcur[:, u:u + 1], axis=0),
                                            bounds_check=SEQ - 1, oob_is_err=False).then_inc(xg_in[u], 16)
                    if late:
                        store(i, u, 2)
                n_pairs = pairs(pool, body)
                store(n_pairs, 0, 2)
                store(n_pairs, 1, 2)
                for s in y_out:
                    pool.wait_ge(s, n_pairs * 16)

            @block.scalar
            def _(act):
                def post(i, u, back):
                    b = i * 2 + (u - back)
                    par = (u - back) % 2
                    act.wait_ge(gu_done, b + 1)
                    act.activation(msg[:, par, :], PS[:, par, 0:FF], ACT.Silu).then_inc(silud, 1)

                def post2(i, u, back, steady):
                    b = i * 2 + (u - back)
                    par = (u - back) % 2
                    act.wait_ge(hT_t, b + 1)
                    act.activation(hT2_hi[:, par], PS[:, 4, 0:2 * P], ACT.Copy).then_inc(hT_hid, 1)

                def post3(i, u, back, steady):
                    b = i * 2 + (u - back)
                    par = (u - back) % 2
                    act.wait_ge(dn_done, b + 1)
                    if not (isinstance(b, int) and b < 2):
                        act.wait_ge(y_out[par], i * 16 + 16 * u - 16)
                    act.activation(ysb[:, par, 0:512], PS[:, 5, :], ACT.Copy).then_inc(y_a, 1)

                def hi(i, u, pc):
                    s = 3 * u + pc
                    act.wait_ge(wland[s], (i + 1) * (32 if pc < 2 else 16))
                    if not (isinstance(i, int) and i == 0 and u == 0):
                        act.wait_ge((piece_free, gu_done, dn_done)[pc], i * 2 + u)
                    act.activation(mhi[:, pc, :], wraw[:, s, :], ACT.Copy).then_inc(mhi_done, 1)

                def body(i, u, first):
                    b = i * 2 + u
                    late = not (isinstance(i, int) and i == 0)
                    hi(i, u, 0)
                    if not first:
                        post(i, u, 1)
                    act.wait_ge(xT_t, b + 1)
                    if late:
                        act.wait_ge(gu_done, b - 1)
                    for h in range(2):
                        act.activation(xT_hi[:, u, 4 * h:4 * h + 4, :], PS[:, 2 + h, :], ACT.Copy).then_inc(xT_hid, 1)
                    if not first:
                        post2(i, u, 1, late)
                    hi(i, u, 1)
                    if not first:
                        post3(i, u, 1, late)
                    hi(i, u, 2)
                n_pairs = pairs(act, body)
                post(n_pairs, 0, 1)
                post2(n_pairs, 0, 1, True)
                post3(n_pairs, 0, 1, True)

            @block.vector
            def _(dve):
                dve.wait_ge(tokT_t, 1)
                dch(dve, dve.tensor_copy(slotidx[:, :], PS[:, 7, 0:NBLK]))
                dch(dve, dve.tensor_scalar(tokf[:, :], PS[:, 7, 0:NBLK], 1.0 / TOPK, 0.5 * (TOPK - 1) / TOPK, ALU.mult, ALU.subtract))
                dve.tensor_scalar(tokidx[:, :], tokf[:, :], ROUND, ROUND, ALU.add, ALU.subtract).then_inc(tokidx_done, 1)

                def lo(i, u, pc):
                    dve.wait_ge(mhi_done, i * 6 + (3 * u + pc + 1))
                    dve.tensor_tensor(mlo[:, pc, :], wraw[:, 3 * u + pc, :], mhi[:, pc, :].bitcast(F), ALU.subtract).then_inc(mlo_done, 1)

                def post(i, u, back):
                    b = i * 2 + (u - back)
                    par = (u - back) % 2
                    dve.wait_ge(silud, b + 1)
                    dve.tensor_tensor(mhid[:, par, :], PS[:, par, FF:], msg[:, par, :], ALU.mult).then_inc(mhidd, 1)

                def post2(i, u, back, steady):
                    b = i * 2 + (u - back)
                    par = (u - back) % 2
                    dve.wait_ge(hT_hid, b + 1)
                    dve.tensor_tensor(hT2_lo[:, par], PS[:, 4, 0:2 * P], hT2_hi[:, par].bitcast(F), ALU.subtract).then_inc(hT_lod, 1)

                def post3(i, u, back, steady):
                    b = i * 2 + (u - back)
                    par = (u - back) % 2
                    dve.wait_ge(dn_done, b + 1)
                    if not (isinstance(b, int) and b < 2):
                        dve.wait_ge(y_out[par], i * 16 + 16 * u - 16)
                    dve.tensor_copy(ysb[:, par, 512:], PS[:, 6, :]).then_inc(y_d, 1)

                def body(i, u, first):
                    b = i * 2 + u
                    late = not (isinstance(i, int) and i == 0)
                    lo(i, u, 0)
                    if not first:
                        post(i, u, 1)
                    for h in range(2):
                        dve.wait_ge(xT_hid, b * 2 + h + 1)
                        dve.tensor_tensor(xT_lo[:, u, 4 * h:4 * h + 4, :], PS[:, 2 + h, :], xT_hi[:, u, 4 * h:4 * h + 4, :].bitcast(F),
                                          ALU.subtract).then_inc(xT_lod, 1)
                    if not first:
                        post2(i, u, 1, late)
                    lo(i, u, 1)
                    if not first:
                        post3(i, u, 1, late)
                    lo(i, u, 2)
                n_pairs = pairs(dve, body)
                post(n_pairs, 0, 1)
                post2(n_pairs, 0, 1, True)
                post3(n_pairs, 0, 1, True)

            @block.tensor
            def _(pe):
                pe.wait_ge(tokT_in, 16)
                pe.transpose(PS[:, 7, 0:NBLK], tokT[:, :], ident[0:NBLK, 0:NBLK]).then_inc(tokT_t, 1)

                def down(i, u, back, steady):
                    b = i * 2 + (u - back)
                    par = (u - back) % 2
                    pe.wait_ge(mhidd, b + 1)
                    if steady:
                        pe.wait_ge(hT_lod, b)
                    for c in range(2):
                        mm = pe.transpose(PS[:, 4, c * P:(c + 1) * P], mhid[:, par, c:FF:2], ident[:, :])
                    mm.then_inc(hT_t, 1)
                    pe.wait_ge(hT_lod, b + 1)
                    pe.wait_ge(mlo_done, b * 3 + 3)
                    if steady:
                        pe.wait_ge(y_a, b)
                        pe.wait_ge(y_d, b)
                    for c in range(2):
                        for n in range(2):
                            w = slice((2 * c + n) * 512, (2 * c + n + 1) * 512)
                            mm = mm3(pe, PS[:, 5 + n, :], hT2_hi[:, par, c], hT2_lo[:, par, c], mhi[:, 2, w], mlo[:, 2, w],
                                     c == 0, c == 1)
                    mm.then_inc(dn_done, 1)

                def body(i, u, first):
                    b = i * 2 + u
                    late = not (isinstance(i, int) and i == 0)
                    pe.wait_ge(xg_in[u], i * 16 + 16)
                    if not first:
                        pe.wait_ge(xT_lod, b * 2)
                    for c in range(KD):
                        mm = pe.transpose(PS[:, 2 + c // 4, (c % 4) * P:(c % 4 + 1) * P], xg[:, u, c:D:KD], ident[:, :])
                    mm.then_inc(xT_t, 1)
                    if not first:
                        down(i, u, 1, late)
                    pe.wait_ge(xT_lod, b * 2 + 2)
                    if late:
                        pe.wait_ge(mhidd, b - 1)
                    for pc in range(2):
                        pe.wait_ge(mlo_done, b * 3 + (pc + 1))
                        for c in range(4):
                            w = slice(c * 512, (c + 1) * 512)
                            mm = mm3(pe, PS[:, u, :], xT_hi[:, u, 4 * pc + c], xT_lo[:, u, 4 * pc + c], mhi[:, pc, w], mlo[:, pc, w],
                                     pc == 0 and c == 0, pc == 1 and c == 3)
                        if pc == 0:
                            mm.then_inc(piece_free, 1)
                    mm.then_inc(gu_done, 1)
                n_pairs = pairs(pe, body)
                down(n_pairs, 0, 1, True)

        NYB = 3
        HK = TOPK // 2
        yb = at("yb", [P, NYB, HK, D], 104)
        gfr = at("gfr", [P, D], 12)
        fin = at("fin", [P, TT, D], 16)
        jf = at("jf", [P, D], 32)
        y_in = [sem(f"rows_in{i}") for i in range(NYB)]
        summed, gf_in, x2d, sq3, ms3, pw3, find, out_done = (sem(n) for n in "summed gf_in x2 squares3 ms3 rstd3 final out_done".split())
        with nc.Block() as block:
            @block.sync
            def _(sp):
                rows = y_dram.rearrange("(t p k) d -> t p k d", t=TT, p=P)
                for n in range(2 * TT):
                    t, h = divmod(n, 2)
                    if n >= NYB:
                        sp.wait_ge(summed, (n - NYB + 1) * HK)
                    sp.dma_start(yb[:, n % NYB], rows[t, :, h * HK:(h + 1) * HK, :]).then_inc(y_in[n % NYB], 16)
                    if n == 0:
                        sp.dma_start(gfr[:, :], bass.AP(tensor=g_final.tensor, offset=0, ap=[[0, P], [1, D]])).then_inc(gf_in, 16)
                for t in range(TT):
                    sp.wait_ge(find, t + 1)
                    sp.dma_start(out[t * P:(t + 1) * P, :], fin[:, t, :]).then_inc(out_done, 16)
                sp.wait_ge(out_done, 16 * TT)

            @block.gpsimd
            def _(pool):
                for t in range(TT):
                    pool.wait_ge(ms3, t + 1)
                    pool.tensor_tensor(rstd[:, t:t + 1], ssum[:, t:t + 1], mhalf[:, t:t + 1], ALU.pow).then_inc(pw3, 1)

            @block.scalar
            def _(act):
                for t in range(TT):
                    act.wait_ge(x2d, t + 1)
                    act.activation(jf[:, :], fin[:, t, :], ACT.Square, accum_out=ssum[:, t:t + 1]).then_inc(sq3, 1)
                    act.wait_ge(sq3, t + 1)

            @block.vector
            def _(dve):
                for n in range(TT * TOPK):
                    t, k = divmod(n, TOPK)
                    part = n // HK
                    dve.wait_ge(y_in[part % NYB], 16 * (part // NYB + 1))
                    if n:
                        dve.wait_ge(summed, n)
                    dve.scalar_tensor_tensor(out=shacc[:, t, :], in0=yb[:, part % NYB, k % HK, :], scalar=wk[:, t, k:k + 1], in1=shacc[:, t, :],
                                             op0=ALU.mult, op1=ALU.add).then_inc(summed, 1)
                    if k == TOPK - 1:
                        dve.wait_ge(summed, n + 1)
                        dch(dve, dve.tensor_tensor(shacc[:, t, :], shacc[:, t, :], gt2[:, :], ALU.mult))
                        dve.tensor_tensor(fin[:, t, :], x1[:, t, :], shacc[:, t, :], ALU.add).then_inc(x2d, 1)
                        dve.wait_ge(sq3, t + 1)
                        dve.tensor_scalar(ssum[:, t:t + 1], ssum[:, t:t + 1], 1.0 / D, EPS, ALU.mult, ALU.add).then_inc(ms3, 1)
                dve.wait_ge(gf_in, 16)
                for t in range(TT):
                    dve.wait_ge(pw3, t + 1)
                    dve.scalar_tensor_tensor(out=fin[:, t, :], in0=fin[:, t, :], scalar=rstd[:, t:t + 1], in1=gfr[:, :],
                                             op0=ALU.mult, op1=ALU.mult).then_inc(find, 1)
    return nc


def finish(nc, out, es, sem, *ts):
    s = sem("dump")
    with nc.Block() as block:
        @block.sync
        def _(sp):
            n = 0
            for t in ts:
                f = int(np.prod(t.shape[1:]))
                fl = t[:] if len(t.shape) == 2 else t[:].rearrange("p a b -> p (a b)")
                sp.dma_start(bass.AP(tensor=out.tensor, offset=n, ap=[[f, P], [1, f]]), fl.bitcast(F)).then_inc(s, 16)
                n += P * f
            sp.wait_ge(s, 16 * len(ts))
    return nc


_INS = ['x', 'c', 'ctx', 'c_ctx', 'w_mod', 'b_mod', 'g_norm1', 'g_norm2', 'w_in', 'na_rpb', 'w_branch_na', 'conv_w',
        'w_branch_sc', 'gla_gate_w', 'gla_gate_b', 'gla_norm_g', 'w_branch_gla', 'w_out', 'w_router', 'b_router',
        'w_exp_gate', 'w_exp_up', 'w_exp_down', 'w_sh_gate', 'w_sh_up', 'w_sh_down', 'g_final']


def shape_constants():
    s, t = np.arange(P)[:, None], np.arange(P)[None, :]
    tri = np.stack([s <= t, s >= t, s < t]).astype(np.float32)
    q, k = (np.arange(P) % GRID)[:, None], np.arange(GRID)[None, :]
    start = np.clip(q - WIN_C // 2, 0, GRID - WIN_C)
    mask = ((k >= start) & (k < start + WIN_C)).astype(np.int32)
    iota = np.arange(SEQ, dtype=np.float32).reshape(TT, P).T.copy()
    slot = iota[:, :, None] * TOPK + np.arange(TOPK, dtype=np.float32)
    return {"k_ident": np.eye(P, dtype=np.float32), "k_tri": tri, "k_mask": mask, "k_iota": iota,
            "k_slot": slot.reshape(P, TT * TOPK).astype(np.float32)}


def kernel(**inputs):
    import concourse.bacc as _bacc
    from concourse.bass_utils import run_bass_kernel_spmd as _run

    nc = _bacc.Bacc("TRN2", target_bir_lowering=False, num_devices=1)
    arrays, args = {}, []
    tables = shape_constants()
    for name in _INS + list(tables):
        a = np.ascontiguousarray(inputs[name] if name in inputs else tables[name])
        arrays[f"in_{name}_dram"] = a
        args.append(nc.dram_tensor(f"in_{name}_dram", a.shape, mybir.dt.from_np(a.dtype), kind="ExternalInput").ap())
    out = nc.dram_tensor("out_0_dram", (SEQ, D), F, kind="ExternalOutput").ap()
    build(nc, *args, out)
    r = _run(nc, [arrays], core_ids=[0])
    return r.results[0]["out_0_dram"].reshape(1, SEQ, D)
```

```python
from contextlib import ExitStack

import numpy as np
import concourse.bass as bass
from concourse import mybir

P = 128
D = 1024
KD = D // P
SEQ = 512
CTX = 256
TOK = SEQ + CTX
TT = SEQ // P
TC = CTX // P
NA_H, NA_D = 8, 64
GRID = 64
WIN_R, WIN_C = 8, 16
RPB_R, RPB_C = 2 * WIN_R - 1, 2 * WIN_C - 1
GL_H, GL_DK, GL_DV = 4, 128, 256
RANK = 16
TAU = 16.0
NE, NG, TOPG, TOPK, FF = 64, 8, 4, 8, 256
ROUTED_SCALE = 2.5
EPS = 1e-6
NEG = -1e30
ROUND = 1.5 * 2.0 ** 23
PEEL = 3
PAD = 65536.0
NBLK = (SEQ * TOPK + NE * (P - 1)) // P
NBLK += NBLK % 2
RPB_T = RPB_R * RPB_C

F = mybir.dt.float32
R = mybir.dt.float32r
I32 = mybir.dt.int32
U32 = mybir.dt.uint32
ALU = mybir.AluOpType
ACT = mybir.ActivationFunctionType
AX = mybir.AxisListType

K_NA, V_NA, K_GLA, V_GLA, GATE, Q_NA, B_SC, C_SC, X_SC, Q_GLA, R_GLA, MERGE = (
    0, 512, 1024, 1536, 2560, 2592, 3104, 3616, 4128, 4640, 5152, 6176)

NROW = 8
ROW_BANK = 2
KB = 1024
BASE = 18 * KB
NRAW, NSPLIT = 3, 2


class Chain:

    def __init__(self, sem):
        self.sem, self.n = sem, 0

    def __call__(self, eng, ins):
        self.n += 1
        ins.then_inc(self.sem, 1)
        eng.wait_ge(self.sem, self.n)


def plan_tiles():
    halves, chunks, tiles = [], {}, []
    counts = {"A": 0, "D": 0}

    def chunk(name, weight, col, outs, rows=2):
        first = len(halves)
        for k in range(rows):
            halves.append((weight, 4 * k, col))
        mine = []
        for n, (kind, t) in enumerate(outs):
            who = "A" if name[0] in ("r", "c", "gate") else "D" if name[0] in ("mod", "x", "b", "br", "out", "row", "sh", "down") else "AD"[n % 2]
            counts[who] += 1
            tile = dict(n=len(tiles), bank=len(tiles) % 8, who=who, nth=counts[who], kind=kind, t=t)
            mine.append(tile)
            tiles.append(tile)
        chunks[name] = dict(name=name, first=first, last=len(halves) - 1, tiles=mine)

    feat = [("feat", m) for m in range(4)]
    feat_ctx = [("featc", m) for m in range(4)]
    tok = [("tok", t) for t in range(TT)]
    tok_ctx = [("tokc", t) for t in range(TC)]
    row = [("row", 0)]
    for j in range(4):
        chunk(("mod", j), "w_mod", 512 * j, row)
    chunk(("k_na",), "w_in", K_NA, feat + feat_ctx)
    chunk(("v_na",), "w_in", V_NA, tok + tok_ctx)
    chunk(("q_na",), "w_in", Q_NA, feat)
    chunk(("k_gla",), "w_in", K_GLA, feat + feat_ctx)
    chunk(("v_gla", 0), "w_in", V_GLA, tok + tok_ctx)
    chunk(("v_gla", 1), "w_in", V_GLA + 512, tok + tok_ctx)
    chunk(("q_gla",), "w_in", Q_GLA, feat)
    for j in range(NROW):
        chunk(("row", j), "w_mod", 2 * D + 512 * j, row)
        chunks["row", j]["tiles"][0]["bank"] = ROW_BANK
    chunk(("r", 0), "w_in", R_GLA, tok)
    chunk(("r", 1), "w_in", R_GLA + 512, tok)
    chunk(("c",), "w_in", C_SC, feat)
    chunk(("x",), "w_in", X_SC, feat)
    chunk(("b",), "w_in", B_SC, feat)
    for j in range(2):
        for br, (weight, rows) in enumerate((("w_branch_na", 1), ("w_branch_sc", 1), ("w_branch_gla", 2))):
            chunk(("gate", j, br), "w_in", MERGE + br * D + 512 * j, feat)
            chunk(("br", j, br), weight, 512 * j, [(f"b{br}", m) for m in range(4)], rows)
    for j in range(2):
        chunk(("out", j), "w_out", 512 * j, [("y", t) for t in range(TT)])
    chunk(("sh",), "w_sh", 0, tok)
    chunk(("down",), "w_sh_down", 0, [("down", t) for t in range(2 * TT)], 1)
    return halves, chunks, tiles


def build(nc, x, c, ctx, c_ctx, w_mod, b_mod, g_norm1, g_norm2, w_in, na_rpb, w_branch_na, conv_w, w_branch_sc,
          gla_gate_w, gla_gate_b, gla_norm_g, w_branch_gla, w_out, w_router, b_router, w_exp_gate, w_exp_up,
          w_exp_down, w_sh_gate, w_sh_up, w_sh_down, g_final, k_ident, k_tri, k_mask, k_iota, k_slot, k_cols, out, dump=None):
    HALVES, CH, TILES = plan_tiles()
    es = ExitStack()
    weights = {"w_mod": w_mod[0], "w_in": w_in[0], "w_branch_na": w_branch_na[0], "w_branch_sc": w_branch_sc[0],
               "w_branch_gla": w_branch_gla[0], "w_out": w_out[0]}

    def at(name, shape, kb, dt=F):
        return nc.alloc_sbuf_tensor_at(name, shape, dt, offset=BASE + int(kb * KB))

    def sem(name):
        return es.enter_context(nc.semaphore(name))

    early = ExitStack()
    early_sems = []

    def esem(name):
        early_sems.append(early.enter_context(nc.semaphore(name)))
        return early_sems[-1]

    def dram(name, shape, dt=F):
        return nc.dram_tensor(name, shape, dt, kind="Internal").ap()

    with es:
        PS = es.enter_context(nc.psum_tensor("PS", [P, 8, 512], F))
        fence = es.enter_context(nc.sbuf_tensor("fence", [P, 4], F))
        ident = at("ident", [P, P], 0)
        tri = at("tri", [P, 3, P], 0.5)
        namask = at("namask", [P, GRID], 2, I32)
        small = at("small", [P, 256], 2.5)
        csil = small[:, 0:16].rearrange("p (k w) -> p k w", w=2)
        ccol = small[:, 16:32].rearrange("p (w k) -> p w k", w=2)
        ssum = small[:, 32:48]
        rstd = small[:, 48:64]
        mhalf = small[:, 64:80]
        rsum = small[:, 80:112]
        rinv = small[:, 112:144]
        nmax = small[:, 144:176]
        convw = small[:, 176:188].rearrange("p (w m) -> p w m", w=3)
        tiny = small[:, 188:256]
        csel_hi = at("csel_hi", [P, KD, P], 4, R)
        csel_lo = at("csel_lo", [P, KD, P], 8, R)
        raw = at("raw", [P, NRAW, 4, 512], 12)
        whi = at("whi", [P, NSPLIT, 4, 512], 36, R)
        wlo = at("wlo", [P, NSPLIT, 4, 512], 52, R)
        hT_hi = at("hT_hi", [P, KD, SEQ], 68, R)
        hT_lo = at("hT_lo", [P, KD, SEQ], 84, R)
        hc_hi = at("hc_hi", [P, KD, CTX], 100, R)
        hc_lo = at("hc_lo", [P, KD, CTX], 108, R)
        onaT_hi = at("onaT_hi", [P, 4, SEQ], 116, R)
        onaT_lo = at("onaT_lo", [P, 4, SEQ], 124, R)
        onaT = at("onaT", [P, 4, SEQ], 124)

        landed = [sem(f"weights_landed{i}") for i in range(NRAW)]
        hi_done, lo_done, used = sem("hi_done"), sem("lo_done"), sem("half_used")
        tile_done = sem("tile_done")
        emptied = {"A": sem("emptied_by_act"), "D": sem("emptied_by_dve")}
        dch, ach = Chain(sem("dve_chain")), Chain(sem("act_chain"))
        pch = Chain(sem("pool_chain"))

        arrive, per_slot = [], [0] * NRAW
        for i, (w, _, _) in enumerate(HALVES):
            per_slot[i % NRAW] += 32 if w == "w_sh" else 16
            arrive.append(per_slot[i % NRAW])
        freed, firsts = [None] * len(HALVES), 0
        for ch in CH.values():
            for i in range(ch["first"], ch["last"]):
                firsts += 1
                freed[i] = (used, firsts)
            freed[ch["last"]] = (tile_done, ch["tiles"][-1]["n"] + 1)
        splits_a, splits_d = [0], [0]
        nloads = [0]

        def load_to(eng, upto):
            while nloads[0] <= min(upto, len(HALVES) - 1):
                i = nloads[0]
                nloads[0] += 1
                if i >= NRAW:
                    eng.wait_ge(lo_done, i - NRAW + 1)
                w, k, col = HALVES[i]
                dst = raw[:, i % NRAW]
                if w == "w_sh":
                    for n, src in enumerate((w_sh_gate, w_sh_up)):
                        eng.dma_start(dst[:, :, n * FF:(n + 1) * FF],
                                      src[0].rearrange("(k p) n -> p k n", p=P)[:, k:k + 4, :]).then_inc(landed[i % NRAW], 16)
                elif w == "w_sh_down":
                    eng.dma_start(dst.rearrange("p (k h) n -> p k (h n)", h=2),
                                  w_sh_down[0].rearrange("(k p) n -> p k n", p=P)).then_inc(landed[i % NRAW], 16)
                else:
                    eng.dma_start(dst, weights[w].rearrange("(k p) n -> p k n", p=P)[:, k:k + 4, col:col + 512])\
                       .then_inc(landed[i % NRAW], 16)

        def split_hi(act, upto):
            while splits_a[0] <= min(upto, len(HALVES) - 1):
                i = splits_a[0]
                splits_a[0] += 1
                act.wait_ge(landed[i % NRAW], arrive[i])
                if i >= NSPLIT:
                    act.wait_ge(*freed[i - NSPLIT])
                act.activation(whi[:, i % NSPLIT], raw[:, i % NRAW], ACT.Copy).then_inc(hi_done, 1)

        def split_lo(dve, upto):
            while splits_d[0] <= min(upto, len(HALVES) - 1):
                i = splits_d[0]
                splits_d[0] += 1
                dve.wait_ge(hi_done, i + 1)
                dve.tensor_tensor(wlo[:, i % NSPLIT], raw[:, i % NRAW], whi[:, i % NSPLIT].bitcast(F), ALU.subtract)\
                   .then_inc(lo_done, 1)

        def mm3(pe, o, ahi, alo, bhi, blo, start, stop):
            pe.matmul(o, ahi, bhi, start=start, stop=False)
            pe.matmul(o, alo, bhi, start=False, stop=False)
            return pe.matmul(o, ahi, blo, start=False, stop=stop)

        def project(pe, name, acts, part=None):
            ch = CH[name]
            for i in range(ch["first"], ch["last"] + 1) if part is None else [ch["first"] + part]:
                pe.wait_ge(lo_done, i + 1)
                s, first, last = i % NSPLIT, i == ch["first"], i == ch["last"]
                for tile in ch["tiles"]:
                    if first and tile["n"] >= 8:
                        before = TILES[tile["n"] - 8]
                        pe.wait_ge(emptied[before["who"]], before["nth"])
                    kind, t = tile["kind"], tile["t"]
                    bank = PS[:, tile["bank"], :]
                    ahi, alo = acts(kind)
                    if kind == "down":
                        for k in range(2):
                            lhs = slice((t // 2) * P, (t // 2 + 1) * P)
                            w = 2 * k + t % 2
                            mm = mm3(pe, bank, ahi[:, k, lhs], alo[:, k, lhs], whi[:, s, w], wlo[:, s, w], k == 0, k == 1)
                        mm.then_inc(tile_done, 1)
                        continue
                    for k in range(4):
                        kk = k + 4 * (i - ch["first"])
                        st, sp = first and k == 0, last and k == 3
                        if kind in ("tok", "tokc", "y"):
                            lhs = slice(t * P, (t + 1) * P)
                            mm = mm3(pe, bank, ahi[:, kk, lhs], alo[:, kk, lhs], whi[:, s, k], wlo[:, s, k], st, sp)
                        elif kind == "row":
                            mm = mm3(pe, bank, ahi[:, kk], alo[:, kk], whi[:, s, k], wlo[:, s, k], st, sp)
                        else:
                            o = bank[:, 0:CTX] if kind == "featc" else bank
                            cols = slice(t * P, (t + 1) * P)
                            mm = mm3(pe, o, whi[:, s, k, cols], wlo[:, s, k, cols], ahi[:, kk], alo[:, kk], st, sp)
                    if last:
                        mm.then_inc(tile_done, 1)
                if not last:
                    mm.then_inc(used, 1)

        def mine(name, who):
            return [t for t in CH[name]["tiles"] if t["who"] == who]

        def wait_tiles(eng, name):
            for who in "AD":
                own = mine(name, who)
                if own:
                    eng.wait_ge(emptied[who], own[-1]["nth"])

        def build_csel(dve, halves):
            for n, (w, a, b) in enumerate(halves):
                src = csil[:, :, w:w + 1].to_broadcast([P, KD, b - a])
                dch(dve, dve.tensor_copy(csel_hi[:, :, a:b], src))
                dch(dve, dve.tensor_tensor(csel_lo[:, :, a:b], src, csel_hi[:, :, a:b].bitcast(F), ALU.subtract))

        def copy_tiles(eng, who, name, dst, scale=1.0):
            for tile in mine(name, who):
                eng.wait_ge(tile_done, tile["n"] + 1)
                o = dst(tile["kind"], tile["t"])
                src = PS[:, tile["bank"], 0:CTX] if tile["kind"] == "featc" else PS[:, tile["bank"], :]
                if who == "A":
                    eng.activation(o, src, ACT.Copy, scale=scale).then_inc(emptied["A"], 1)
                else:
                    eng.tensor_scalar(o, src, scale, None, ALU.mult).then_inc(emptied["D"], 1)

        xs = at("xs", [P, TT + TC, D], 132)
        mrow = at("mrow", [P, 2 * D], 156)
        brow = at("brow", [P, 2 * D], 164)
        junk = at("junk", [P, D], 172)
        hf = at("hf", [P, 2, TOK], 176)
        modc = at("modc", [P, 2 * KD, 2], 182)
        scale1 = at("scale1", [P, KD, 2], 182.25)
        g1c = at("g1c", [P, KD], 182.5)
        cpy = sem("rpb_padded")
        x_in, consts, c_in, b_in = (esem(n) for n in ("x_in", "consts", "c_in", "b_in"))
        csil_done, csel_done, mrow_done, mrowT, modc_done = (esem(n) for n in ("csil", "csel", "mrow", "mrowT", "modc"))
        sq_done, ms_done, pow_done, xn_done, xT, hf_done, hhi_done, hlo_done = (
            esem(n) for n in ("squares", "meansq", "rstd", "xn", "xT", "hf", "h_hi", "h_lo"))
        zero_done = sem("zeros")
        rpb_rep = dram("rpb_rep", [NA_H, GRID, RPB_T])
        LAST1 = CH[("mod", 3)]["last"]

        with nc.Block() as block:
            @block.sync
            def _(sp):
                sp.dma_start(ccol[:, 0, :], c[0].rearrange("(k p) -> p k", p=P), allow_slow_non_contiguous=True).then_inc(c_in, 16)
                sp.dma_start(ccol[:, 1, :], c_ctx.rearrange("(k p) -> p k", p=P), allow_slow_non_contiguous=True).then_inc(c_in, 16)
                load_to(sp, 2)
                sp.dma_start(brow[:, :], bass.AP(tensor=b_mod.tensor, offset=0, ap=[[0, P], [1, 2 * D]])).then_inc(b_in, 16)
                sp.dma_start(g1c[:, :], g_norm1[0].rearrange("(k p) -> p k", p=P), allow_slow_non_contiguous=True).then_inc(b_in, 16)
                load_to(sp, LAST1 + 3)

            @block.gpsimd
            def _(pool):
                pool.dma_start(ident[:, :], k_ident).then_inc(consts, 16)
                pool.dma_start(tri[:, :, :], k_tri.rearrange("m p t -> p m t")).then_inc(consts, 16)
                pool.dma_start(namask[:, :], k_mask).then_inc(consts, 16)
                pool.memset(mhalf[:, :], -0.5).then_inc(zero_done, 1)
                pool.dma_start(rpb_rep, bass.AP(tensor=na_rpb.tensor, offset=0, ap=[[RPB_T, NA_H], [0, GRID], [1, RPB_T]]))\
                    .then_inc(cpy, 16)
                pool.wait_ge(zero_done, 1)
                pool.wait_ge(cpy, 16)
                pool.wait_ge(consts, 48)
                pool.wait_ge(ms_done, 1)
                pool.tensor_tensor(rstd[:, 0:TT + TC], ssum[:, 0:TT + TC], mhalf[:, 0:TT + TC], ALU.pow).then_inc(pow_done, 1)

            @block.scalar
            def _(act):
                act.dma_start(xs[:, 0:TT, :], x[0].rearrange("(t p) d -> p t d", p=P)).then_inc(x_in, 16)
                act.dma_start(xs[:, TT:, :], ctx[0].rearrange("(t p) d -> p t d", p=P)).then_inc(x_in, 16)
                act.wait_ge(c_in, 32)
                act.activation(csil.rearrange("p k w -> p w k"), ccol, ACT.Silu).then_inc(csil_done, 1)
                split_hi(act, 1)
                act.wait_ge(x_in, 32)
                for t in range(TT + TC):
                    ach(act, act.activation(junk[:, :], xs[:, t, :], ACT.Square, accum_out=ssum[:, t:t + 1]))
                act.copy(tiny[:, 67:68], ssum[:, 0:1]).then_inc(sq_done, 1)
                split_hi(act, LAST1 + 2)
                for k in range(KD):
                    act.wait_ge(hf_done, k + 1)
                    act.activation(hT_hi[:, k, :], hf[:, k % 2, 0:SEQ], ACT.Copy).then_inc(hhi_done, 1)
                    act.activation(hc_hi[:, k, :], hf[:, k % 2, SEQ:], ACT.Copy).then_inc(hhi_done, 1)
                split_hi(act, LAST1 + 2)

            @block.vector
            def _(dve):
                dve.wait_ge(csil_done, 1)
                build_csel(dve, [(0, 0, 64), (1, 64, P)])
                dve.tensor_copy(tiny[:, 66:67], csil[:, 0, 0:1]).then_inc(csel_done, 1)
                split_lo(dve, 1)
                dve.wait_ge(sq_done, 1)
                dve.tensor_scalar(ssum[:, 0:TT + TC], ssum[:, 0:TT + TC], 1.0 / D, EPS, ALU.mult, ALU.add).then_inc(ms_done, 1)
                dve.wait_ge(pow_done, 1)
                for t in range(TT + TC):
                    dve.tensor_scalar(xs[:, t, :], xs[:, t, :], rstd[:, t:t + 1], None, ALU.mult).then_inc(xn_done, 1)
                dve.wait_ge(b_in, 32)
                for j in range(4):
                    split_lo(dve, 2 * j + 3)
                    tile = CH[("mod", j)]["tiles"][0]
                    dve.wait_ge(tile_done, tile["n"] + 1)
                    cols = slice(512 * j, 512 * j + 512)
                    dve.tensor_tensor(mrow[:, cols], PS[:, tile["bank"], :], brow[:, cols], ALU.add).then_inc(emptied["D"], 1)
                dve.wait_ge(mrowT, 1)
                dch(dve, dve.tensor_copy(modc[:, :, :].rearrange("p (b k) w -> p b k w", b=4),
                                         PS[:, 4:8, :].rearrange("p b (k t) -> p b k t", t=P)[:, :, :, 0:P:64]))
                dve.tensor_scalar(scale1[:, :, :], modc[:, KD:, :], 1.0, None, ALU.add).then_inc(modc_done, 1)
                dve.wait_ge(modc_done, 1)
                dch(dve, dve.tensor_tensor(scale1[:, :, :], scale1[:, :, :],
                                           g1c[:, :, None].to_broadcast([P, KD, 2]), ALU.mult))
                for k in range(KD):
                    dve.wait_ge(xT, k + 1)
                    if k >= 2:
                        dve.wait_ge(hhi_done, 2 * k - 2)
                        dve.wait_ge(hlo_done, 2 * k - 2)
                    b = 4 * (k % 2)
                    dve.tensor_scalar(hf[:, k % 2, 0:SEQ], PS[:, b, :], scale1[:, k, 0:1], modc[:, k, 0:1], ALU.mult, ALU.add)
                    dve.tensor_scalar(hf[:, k % 2, SEQ:], PS[:, b + 1, 0:CTX], scale1[:, k, 1:2], modc[:, k, 1:2], ALU.mult, ALU.add)\
                       .then_inc(hf_done, 1)
                    dve.wait_ge(hf_done, k + 1)
                    dve.wait_ge(hhi_done, 2 * k + 2)
                    dve.tensor_tensor(hT_lo[:, k, :], hf[:, k % 2, 0:SEQ], hT_hi[:, k, :].bitcast(F), ALU.subtract).then_inc(hlo_done, 1)
                    dve.tensor_tensor(hc_lo[:, k, :], hf[:, k % 2, SEQ:], hc_hi[:, k, :].bitcast(F), ALU.subtract).then_inc(hlo_done, 1)
                split_lo(dve, LAST1 + 2)

            @block.tensor
            def _(pe):
                pe.wait_ge(csel_done, 1)
                for j in range(4):
                    project(pe, ("mod", j), lambda kind: (csel_hi, csel_lo))
                pe.wait_ge(consts, 48)
                pe.wait_ge(emptied["D"], 4)
                for m in range(2 * KD):
                    mm = pe.transpose(PS[:, 4 + m // 4, (m % 4) * P:(m % 4 + 1) * P], mrow[:, m * P:(m + 1) * P], ident[:, :])
                mm.then_inc(mrowT, 1)
                pe.wait_ge(xn_done, TT + TC)
                pe.wait_ge(modc_done, 1)
                for k in range(KD):
                    b = 4 * (k % 2)
                    if k >= 2:
                        pe.wait_ge(hf_done, k - 1)
                    for t in range(TT + TC):
                        o = PS[:, b + t // TT, (t % TT) * P:(t % TT + 1) * P]
                        mm = pe.transpose(o, xs[:, t, k * P:(k + 1) * P], ident[:, :])
                    mm.then_inc(xT, 1)

        def acts(kind):
            return (hc_hi, hc_lo) if kind in ("featc", "tokc") else (hT_hi, hT_lo)

        kna = at("kna", [P, 4, TOK], 132)
        vna = at("vna", [P, TT + TC, 512], 144)
        qna = at("qna", [P, 4, SEQ], 156)
        prob = at("prob", [P, 2, TOK], 164)
        probT = at("probT", [P, 2, TOK], 170)
        braw = at("braw", [P, 14, GRID], 176)
        bias = at("bias", [P, 2, 14, GRID], 179.5)
        ona = at("ona", [P, TT, 512], 186.5)
        NI = NA_H * TT
        bias_in, bias_done, scores, scores_read, smax = (esem(n) for n in ("bias_in", "bias", "scores", "scores_read", "smax"))
        exped, probT_done, pT_a, pT_d, pv_done, ona_done = (esem(n) for n in ("exped", "probT", "pT_act", "pT_dve", "pv", "ona"))
        turned, turn_hi, turn_lo = sem("turned"), sem("turn_hi"), sem("turn_lo")
        nturn = [0, 0, 0]

        def turn(pe, src, n_tiles, banks, first_wait=None):
            for m in range(n_tiles):
                i = nturn[0]
                nturn[0] += 1
                if m >= len(banks):
                    pe.wait_ge(turn_lo, i - len(banks) + 1)
                for t in range(TT):
                    mm = pe.transpose(PS[:, banks[m % len(banks)], t * P:(t + 1) * P], src(t, m), ident[:, :])
                mm.then_inc(turned, 1)

        def turn_out_hi(act, dst, n_tiles, banks):
            for m in range(n_tiles):
                nturn[1] += 1
                act.wait_ge(turned, nturn[1])
                act.activation(dst[:, m, :], PS[:, banks[m % len(banks)], :], ACT.Copy).then_inc(turn_hi, 1)

        def turn_out_lo(dve, dst, hi, n_tiles, banks):
            for m in range(n_tiles):
                nturn[2] += 1
                dve.wait_ge(turn_hi, nturn[2])
                dve.tensor_tensor(dst[:, m, :], PS[:, banks[m % len(banks)], :], hi[:, m, :].bitcast(F), ALU.subtract)\
                   .then_inc(turn_lo, 1)

        def kna_at(kind, m):
            return kna[:, m, SEQ:] if kind == "featc" else kna[:, m, 0:SEQ]

        def vna_at(kind, t):
            return vna[:, TT + t, :] if kind == "tokc" else vna[:, t, :]

        na_names = [("k_na",), ("v_na",), ("q_na",)]
        LAST2 = CH[("q_na",)]["last"]
        with nc.Block() as block:
            @block.sync
            def _(sp):
                for h in range(NA_H):
                    if h:
                        sp.wait_ge(bias_done, h)
                    off = h * GRID * RPB_T + WIN_C - 1
                    for half in range(2):
                        sp.dma_start(braw[64 * half:64 * half + 64],
                                     bass.AP(tensor=rpb_rep.tensor, offset=off + (1 - half) * RPB_C,
                                             ap=[[RPB_T - 1, GRID], [RPB_C, 14], [1, GRID]])).then_inc(bias_in, 16)
                    if h == 0:
                        load_to(sp, LAST2 + 3)

            @block.scalar
            def _(act):
                for name, dst in zip(na_names, (kna_at, vna_at, lambda kind, m: qna[:, m, :])):
                    split_hi(act, CH[name]["last"] + 2)
                    copy_tiles(act, "A", name, dst)
                for i in range(NI + 1):
                    if i < NI:
                        act.wait_ge(smax, i + 1)
                        act.activation(prob[:, i % 2, :], prob[:, i % 2, :], ACT.Exp, bias=nmax[:, i:i + 1],
                                       accum_out=rsum[:, i:i + 1]).then_inc(exped, 1)
                    if i >= 1:
                        j = i - 1
                        act.wait_ge(probT_done, j + 1)
                        if j >= 2:
                            act.wait_ge(pv_done, j - 1)
                        act.activation(probT[:, j % 2, 0:512], PS[:, 3, :], ACT.Copy).then_inc(pT_a, 1)
                for m in range(4):
                    nturn[1] += 1
                    act.wait_ge(turned, nturn[1])
                    act.activation(onaT[:, m, 0:SEQ // 2], PS[:, m, 0:SEQ // 2], ACT.Copy).then_inc(turn_hi, 1)

            @block.vector
            def _(dve):
                for name, dst in zip(na_names, (kna_at, vna_at, lambda kind, m: qna[:, m, :])):
                    split_lo(dve, CH[name]["last"] + 2)
                    copy_tiles(dve, "D", name, dst)
                for i in range(NI + 2):
                    if i < NI:
                        h, qt = divmod(i, TT)
                        if qt == 0:
                            if h >= 2:
                                dve.wait_ge(smax, (h - 1) * TT)
                            dch(dve, dve.memset(bias[:, h % 2], NEG))
                            dve.wait_ge(bias_in, 32 * (h + 1))
                            dve.copy_predicated(bias[:, h % 2], namask[:, None, :].to_broadcast([P, 14, GRID]), braw[:, :, :])\
                               .then_inc(bias_done, 1)
                            dve.wait_ge(bias_done, h + 1)
                        dve.wait_ge(scores, i + 1)
                        if i >= 2:
                            dve.wait_ge(probT_done, i - 1)
                        dve.scalar_tensor_tensor(out=prob[:, i % 2, 0:512].rearrange("p (j k) -> p j k", k=GRID),
                                                 in0=PS[:, i % 2, :].rearrange("p (j k) -> p j k", k=GRID),
                                                 scalar=NA_D ** -0.5,
                                                 in1=bias[:, h % 2, 6 - 2 * qt:14 - 2 * qt, :],
                                                 op0=ALU.mult, op1=ALU.add)
                        dve.tensor_scalar(prob[:, i % 2, 512:], PS[:, 2 + 5 * (i % 2), 0:CTX], NA_D ** -0.5, None,
                                          ALU.mult).then_inc(scores_read, 1)
                        dve.wait_ge(scores_read, i + 1)
                        dve.tensor_reduce(nmax[:, i:i + 1], prob[:, i % 2, :], AX.X, ALU.max, negate=True).then_inc(smax, 1)
                    if 1 <= i <= NI:
                        j = i - 1
                        dve.wait_ge(probT_done, j + 1)
                        if j >= 2:
                            dve.wait_ge(pv_done, j - 1)
                        dve.tensor_copy(probT[:, j % 2, 512:], PS[:, 4, 0:CTX]).then_inc(pT_d, 1)
                        dve.wait_ge(exped, j + 1)
                        dch(dve, dve.reciprocal(rinv[:, j:j + 1], rsum[:, j:j + 1]))
                    if i >= 2:
                        j = i - 2
                        h, qt = divmod(j, TT)
                        dve.wait_ge(pv_done, j + 1)
                        dve.tensor_scalar(ona[:, qt, h * NA_D:(h + 1) * NA_D], PS[:, 5 + j % 2, 0:NA_D], rinv[:, j:j + 1], None,
                                          ALU.mult).then_inc(ona_done, 1)
                for m in range(4):
                    nturn[2] += 1
                    dve.wait_ge(turn_hi, nturn[2])
                    dve.tensor_copy(onaT[:, m, SEQ // 2:], PS[:, m, SEQ // 2:]).then_inc(turn_lo, 1)

            @block.tensor
            def _(pe):
                for name in na_names:
                    project(pe, name, acts)
                for name in na_names:
                    wait_tiles(pe, name)

                def score(i):
                    h, qt = divmod(i, TT)
                    rows = slice(64 * (h % 2), 64 * (h % 2) + 64)
                    if i >= 2:
                        pe.wait_ge(scores_read, i - 1)
                    q = qna[rows, h // 2, qt * P:(qt + 1) * P]
                    pe.matmul(PS[:, i % 2, :], q, kna[rows, h // 2, 0:SEQ], start=True, stop=True)
                    pe.matmul(PS[:, 2 + 5 * (i % 2), 0:CTX], q, kna[rows, h // 2, SEQ:], start=True, stop=True)\
                      .then_inc(scores, 1)

                def values(j):
                    h = j // TT
                    pe.wait_ge(pT_a, j + 1)
                    pe.wait_ge(pT_d, j + 1)
                    if j >= 2:
                        pe.wait_ge(ona_done, j - 1)
                    for t in range(TT + TC):
                        mm = pe.matmul(PS[:, 5 + j % 2, 0:NA_D], probT[:, j % 2, t * P:(t + 1) * P],
                                       vna[:, t, h * NA_D:(h + 1) * NA_D], start=(t == 0), stop=(t == TT + TC - 1))
                    mm.then_inc(pv_done, 1)

                score(0)
                for i in range(NI):
                    if i + 1 < NI:
                        score(i + 1)
                    if i >= 1:
                        values(i - 1)
                    pe.wait_ge(exped, i + 1)
                    for t in range(TT + TC):
                        mm = pe.transpose(PS[:, 3 + t // 4, (t % 4) * P:(t % 4 + 1) * P],
                                          prob[:, i % 2, t * P:(t + 1) * P], ident[:, :])
                    mm.then_inc(probT_done, 1)
                values(NI - 1)
                pe.wait_ge(ona_done, NI)
                turn(pe, lambda t, m: ona[:, t, m * P:(m + 1) * P], 4, [0, 1, 2, 3])

        if dump == "na":
            return finish(nc, out, es, sem, onaT)

        kgl = at("kgl", [P, GL_H, TOK], 132)
        vgl = at("vgl", [P, TT + TC, D], 144)
        qgl = at("qgl", [P, GL_H, SEQ], 168)
        lrT = at("lrT", [64, TOK], 176)
        ogl = at("ogl", [P, TT, D], 189)
        wgp = at("wgp", [P, KD, P], 189)
        wg_hi = at("wg_hi", [P, KD, P], 193, R)
        wg_lo = at("wg_lo", [P, KD, P], 197, R)
        wgr = at("wgr", [P, KD, 2 * RANK], 201)
        w2 = at("w2", [64, 512], 179)
        gate_in, w2_in, wgp_done, wg_done, lr_done, lr_out = (esem(n) for n in ("gate_in", "w2_in", "wgp", "wg", "lr", "lr_out"))
        gl_names = [("k_gla",), ("v_gla", 0), ("v_gla", 1), ("q_gla",)]
        LAST3 = CH[("q_gla",)]["last"]

        def kgl_at(kind, m):
            return kgl[:, m, SEQ:] if kind == "featc" else kgl[:, m, 0:SEQ]

        def vgl_at(j):
            return lambda kind, t: vgl[:, (TT if kind == "tokc" else 0) + t, 512 * j:512 * j + 512]

        gl_dst = [kgl_at, vgl_at(0), vgl_at(1), lambda kind, m: qgl[:, m, :]]
        with nc.Block() as block:
            @block.sync
            def _(sp):
                sp.dma_start(wgr[:, :, :], w_in[0].rearrange("(k p) n -> p k n", p=P)[:, :, GATE:GATE + 2 * RANK]).then_inc(gate_in, 16)
                for d in range(2):
                    sp.dma_start(w2[32 * d:32 * d + RANK, :], gla_gate_w[0, d]).then_inc(w2_in, 16)
                    sp.dma_start(w2[32 * d + RANK:32 * d + RANK + 1, :], gla_gate_b[:, d, :]).then_inc(w2_in, 16)
                sp.wait_ge(w2_in, 64)
                load_to(sp, LAST3 + 3)

            @block.scalar
            def _(act):
                for name, dst in zip(gl_names, gl_dst):
                    split_hi(act, CH[name]["last"] + 2)
                    copy_tiles(act, "A", name, dst, GL_DK ** -0.5 if name == ("q_gla",) else 1.0)
                act.wait_ge(wgp_done, 4)
                act.activation(wg_hi[:, :, :], wgp[:, :, :], ACT.Copy).then_inc(wg_done, 1)

            @block.vector
            def _(dve):
                dch(dve, dve.memset(wgp[:, :, :], 0.0))
                dve.memset(lrT[:, :], 1.0).then_inc(wgp_done, 1)
                dve.wait_ge(gate_in, 16)
                for d in range(2):
                    dve.tensor_copy(wgp[:, :, 32 * d:32 * d + RANK], wgr[:, :, RANK * d:RANK * d + RANK]).then_inc(wgp_done, 1)
                dve.wait_ge(wgp_done, 3)
                dve.tensor_copy(tiny[:, 0:1], wgp[:, 0, 0:1]).then_inc(wgp_done, 1)
                for name, dst in zip(gl_names, gl_dst):
                    split_lo(dve, CH[name]["last"] + 2)
                    copy_tiles(dve, "D", name, dst, GL_DK ** -0.5 if name == ("q_gla",) else 1.0)
                dve.wait_ge(wg_done, 1)
                dve.tensor_tensor(wg_lo[:, :, :], wgp[:, :, :], wg_hi[:, :, :].bitcast(F), ALU.subtract).then_inc(wg_done, 1)
                dve.wait_ge(lr_done, 1)
                for d in range(2):
                    rows = slice(32 * d, 32 * d + RANK)
                    dve.tensor_copy(lrT[rows, 0:SEQ], PS[rows, 0, :]).then_inc(lr_out, 1)
                    dve.tensor_copy(lrT[rows, SEQ:], PS[rows, 1, 0:CTX]).then_inc(lr_out, 1)

            @block.tensor
            def _(pe):
                for name in gl_names:
                    project(pe, name, acts)
                for name in gl_names:
                    wait_tiles(pe, name)
                pe.wait_ge(wg_done, 2)
                for b, (hi, lo, n) in enumerate(((hT_hi, hT_lo, SEQ), (hc_hi, hc_lo, CTX))):
                    for k in range(KD):
                        mm = mm3(pe, PS[:, b, 0:n], wg_hi[:, k], wg_lo[:, k], hi[:, k], lo[:, k], k == 0, k == KD - 1)
                mm.then_inc(lr_done, 1)

        state = at("state", [P, 2, GL_H, GL_DV], 100)
        smid = at("smid", [P, GL_H, GL_DV], 108)
        eq = at("eq", [P, 2, GL_H, P], 112)
        ek = at("ek", [P, 2, GL_H, P], 116)
        rowbuf = at("rowbuf", [1, 2, 512], 120)
        lgate = at("lgate", [P, 512], 181)
        tneg = at("tneg", [P, 512], 183)
        attn = at("attn", [P, GL_H, P], 185)
        kdec = at("kdec", [P, GL_H, P], 187)
        edges = tiny[:, 0:24].rearrange("p (w h e) -> p w h e", w=2, e=3)
        one = tiny[:, 24:25]
        (logit_done, absd, expd, lnd, gdone, cumd, dsub, kexp, kfd, qfd, smidd, kT_done, kT_out, atd, atm, od, oout, ud, sdone) = (
            esem("gl_" + n) for n in "logit abs exp ln gate cum diff decays kf qf smid kT kT_out attn attn_out o o_out update state".split())
        units = []
        order = {0: [("c", 0), ("c", 1)] + [("l", t) for t in range(TT)],
                 1: [("c", 1), ("c", 0)] + [("l", TT - 1 - t) for t in range(TT)]}
        seen = set()
        for j in range(TC + TT):
            for d in range(2):
                kind, t = order[d][j]
                lat = kind == "l"
                units.append(dict(d=d, j=j, lat=lat, t=t, tok=(0 if lat else SEQ) + t * P, vt=t if lat else TT + t,
                                  add=lat and t in seen, last=j == TC + TT - 1, nlat=sum(u["lat"] for u in units),
                                  nup=sum(not u["last"] for u in units)))
                if lat:
                    seen.add(t)
        NU = len(units)
        rows_dram = dram("rows_dram", [1, NROW * 512])
        row_out = [sem(f"row_out{i}") for i in range(2)]
        row_halves = [(j, part) for j in range(NROW) for part in range(2)]
        bursts = [row_halves[len(row_halves) * u // NU:len(row_halves) * (u + 1) // NU] for u in range(NU)]

        def row_half(j, part):
            return CH[("row", j)]["first"] + part

        with nc.Block() as block:
            @block.sync
            def _(sp):
                for j in range(NROW):
                    load_to(sp, row_half(j, 1) + 3)
                    sp.wait_ge(emptied["D"], CH[("row", j)]["tiles"][0]["nth"])
                    sp.dma_start(rows_dram[0:1, 512 * j:512 * j + 512], rowbuf[0:1, j % 2, :]).then_inc(row_out[j % 2], 16)
                for w in row_out:
                    sp.wait_ge(w, 16 * NROW // 2)

            @block.scalar
            def _(act):
                def gate_logs(u):
                    act.wait_ge(logit_done, u + 1)
                    if u:
                        act.wait_ge(gdone, u)
                    act.activation(tneg[:, :], PS[:, 0, :], ACT.Abs).then_inc(absd, 1)
                    act.wait_ge(absd, u + 2)
                    act.activation(tneg[:, :], tneg[:, :], ACT.Exp, scale=-1.0).then_inc(expd, 1)
                    act.wait_ge(expd, u + 1)
                    act.activation(tneg[:, :], tneg[:, :], ACT.Ln, bias=one).then_inc(lnd, 1)

                def decays(u):
                    d = units[u]["d"]
                    act.wait_ge(dsub, u + 1)
                    act.activation(ek[:, u % 2], eq[:, u % 2], ACT.Exp, scale=-1.0 / TAU).then_inc(kexp, 1)
                    act.wait_ge(kexp, 3 * u + 1)
                    act.activation(eq[:, u % 2], eq[:, u % 2], ACT.Exp, scale=1.0 / TAU).then_inc(kexp, 1)
                    act.activation(edges[:, d], edges[:, d], ACT.Exp, scale=1.0 / TAU).then_inc(kexp, 1)

                act.wait_ge(absd, 1)
                gate_logs(0)
                decays(0)
                gate_logs(1)
                for u, un in enumerate(units):
                    if not un["last"]:
                        act.wait_ge(kT_done, un["nup"] + 1)
                        if un["nup"]:
                            act.wait_ge(ud, un["nup"])
                        act.activation(kdec[:, :, :], PS[:, 3, :], ACT.Copy).then_inc(kT_out, 1)
                    if u + 1 < NU:
                        decays(u + 1)
                    if u + 2 < NU:
                        gate_logs(u + 2)
                    for j, part in bursts[min(u + 1, NU - 1)]:
                        split_hi(act, row_half(j, part))
                split_hi(act, row_half(NROW - 1, 1) + 2)

            @block.vector
            def _(dve):
                def gates(u):
                    if u:
                        dve.wait_ge(cumd, u)
                    dve.wait_ge(lnd, u + 1)
                    dve.scalar_tensor_tensor(out=lgate[:, :], in0=PS[:, 0, :], scalar=0.0, in1=tneg[:, :],
                                             op0=ALU.min, op1=ALU.subtract).then_inc(gdone, 1)

                def differences(u):
                    un = units[u]
                    d = un["d"]
                    dve.wait_ge(cumd, u + 1)
                    cum = PS[:, 1, :].rearrange("p (h t) -> p h t", h=GL_H)
                    mid, last = (63, P - 1) if d == 0 else (64, 0)
                    dve.tensor_copy(edges[:, d, :, 0:1], cum[:, :, mid:mid + 1])
                    dch(dve, dve.tensor_copy(edges[:, d, :, 1:2], cum[:, :, last:last + 1]))
                    dch(dve, dve.tensor_tensor(edges[:, d, :, 2:3], edges[:, d, :, 1:2], edges[:, d, :, 0:1], ALU.subtract))
                    if u >= 2:
                        dve.wait_ge(kT_done, units[u - 1]["nup"])
                        if units[u - 1]["nlat"]:
                            dve.wait_ge(od, units[u - 1]["nlat"])
                    dve.tensor_tensor(eq[:, u % 2], cum, edges[:, d, :, 0:1].to_broadcast([P, GL_H, P]), ALU.subtract).then_inc(dsub, 1)

                def factors(u):
                    un = units[u]
                    dve.wait_ge(kexp, 3 * u + 3)
                    dve.tensor_tensor(ek[:, u % 2], kgl[:, :, un["tok"]:un["tok"] + P], ek[:, u % 2], ALU.mult).then_inc(kfd, 1)
                    if un["lat"]:
                        dve.tensor_tensor(eq[:, u % 2], qgl[:, :, un["tok"]:un["tok"] + P], eq[:, u % 2], ALU.mult).then_inc(qfd, 1)

                def row_copy(u):
                    for j, part in bursts[u]:
                        if part == 1:
                            tile = CH[("row", j)]["tiles"][0]
                            dve.wait_ge(tile_done, tile["n"] + 1)
                            if j >= 2:
                                dve.wait_ge(row_out[j % 2], 16 * (j // 2))
                            dve.tensor_copy(rowbuf[0:1, j % 2, :], PS[0:1, tile["bank"], :]).then_inc(emptied["D"], 1)

                dve.memset(one, 1.0).then_inc(absd, 1)
                gates(0)
                differences(0)
                factors(0)
                gates(1)
                for u, un in enumerate(units):
                    d, t = un["d"], un["t"]
                    if un["lat"]:
                        if un["nlat"]:
                            dve.wait_ge(od, un["nlat"])
                        dve.tensor_tensor(smid[:, :, :], state[:, d], edges[:, d, :, 0:1].to_broadcast([P, GL_H, GL_DV]), ALU.mult)\
                           .then_inc(smidd, 1)
                        dve.wait_ge(atd, un["nlat"] + 1)
                        dve.tensor_tensor(attn[:, :, :], PS[:, 0, :].rearrange("p (h t) -> p h t", h=GL_H),
                                          tri[:, d:d + 1, :].to_broadcast([P, GL_H, P]), ALU.mult).then_inc(atm, 1)
                    if u:
                        row_copy(u - 1)
                    if u + 1 < NU:
                        differences(u + 1)
                    for j, part in bursts[u]:
                        split_lo(dve, row_half(j, part))
                    if u + 1 < NU:
                        factors(u + 1)
                    if un["lat"]:
                        dve.wait_ge(od, un["nlat"] + 1)
                        o = PS[:, 4:6, :].rearrange("p b n -> p (b n)")
                        if un["add"]:
                            dve.tensor_tensor(ogl[:, t, :], ogl[:, t, :], o, ALU.add).then_inc(oout, 1)
                        else:
                            dve.tensor_copy(ogl[:, t, :], o).then_inc(oout, 1)
                        dve.wait_ge(oout, un["nlat"] + 1)
                    if u + 2 < NU:
                        gates(u + 2)
                    if not un["last"]:
                        if un["j"]:
                            dch(dve, dve.tensor_tensor(state[:, d], state[:, d],
                                                       edges[:, d, :, 1:2].to_broadcast([P, GL_H, GL_DV]), ALU.mult))
                        dve.wait_ge(ud, un["nup"] + 1)
                        for h in range(GL_H):
                            upd = PS[:, 6 + h // 2, (h % 2) * GL_DV:(h % 2 + 1) * GL_DV]
                            if un["j"]:
                                ins = dve.scalar_tensor_tensor(out=state[:, d, h], in0=upd, scalar=edges[:, d, h, 2:3],
                                                               in1=state[:, d, h], op0=ALU.mult, op1=ALU.add)
                            else:
                                ins = dve.tensor_scalar(state[:, d, h], upd, edges[:, d, h, 2:3], None, ALU.mult)
                        ins.then_inc(sdone, 1)
                        dve.wait_ge(sdone, un["nup"] + 1)
                row_copy(NU - 1)
                split_lo(dve, row_half(NROW - 1, 1) + 2)

            @block.tensor
            def _(pe):
                def logits(u):
                    un = units[u]
                    d, rows = un["d"], slice(32 * un["d"], 32 * un["d"] + RANK + 1)
                    if u:
                        pe.wait_ge(gdone, u)
                    pe.matmul(PS[:, 0, :], lrT[rows, un["tok"]:un["tok"] + P], w2[rows, :], start=True, stop=True).then_inc(logit_done, 1)

                def sums(u):
                    pe.wait_ge(gdone, u + 1)
                    if u:
                        pe.wait_ge(dsub, u)
                    for h in range(GL_H):
                        mm = pe.matmul(PS[:, 1, h * P:(h + 1) * P], lgate[:, h * P:(h + 1) * P], tri[:, units[u]["d"], :], start=True, stop=True)
                    mm.then_inc(cumd, 1)

                logits(0)
                sums(0)
                logits(1)
                for u, un in enumerate(units):
                    pe.wait_ge(kfd, u + 1)
                    if not un["last"]:
                        if un["nup"]:
                            pe.wait_ge(kT_out, un["nup"])
                        for h in range(GL_H):
                            mm = pe.transpose(PS[:, 3, h * P:(h + 1) * P], ek[:, u % 2, h, :], ident[:, :])
                        mm.then_inc(kT_done, 1)
                    if un["lat"]:
                        pe.wait_ge(qfd, un["nlat"] + 1)
                        pe.wait_ge(gdone, min(u + 2, NU))
                        for h in range(GL_H):
                            mm = pe.matmul(PS[:, 0, h * P:(h + 1) * P], ek[:, u % 2, h, :], eq[:, u % 2, h, :], start=True, stop=True)
                        mm.then_inc(atd, 1)
                    if u + 1 < NU:
                        sums(u + 1)
                    if un["lat"]:
                        pe.wait_ge(atm, un["nlat"] + 1)
                    if u + 2 < NU:
                        logits(u + 2)
                    if un["lat"]:
                        pe.wait_ge(smidd, un["nlat"] + 1)
                        if un["nlat"]:
                            pe.wait_ge(oout, un["nlat"])
                        for h in range(GL_H):
                            o = PS[:, 4 + h // 2, (h % 2) * GL_DV:(h % 2 + 1) * GL_DV]
                            pe.matmul(o, attn[:, h, :], vgl[:, un["vt"], h * GL_DV:(h + 1) * GL_DV], start=True, stop=False)
                            mm = pe.matmul(o, eq[:, u % 2, h, :], smid[:, h, :], start=False, stop=True)
                        mm.then_inc(od, 1)
                    if not un["last"]:
                        pe.wait_ge(kT_out, un["nup"] + 1)
                        if un["nup"]:
                            pe.wait_ge(sdone, un["nup"])
                        for h in range(GL_H):
                            mm = pe.matmul(PS[:, 6 + h // 2, (h % 2) * GL_DV:(h % 2 + 1) * GL_DV], kdec[:, h, :],
                                           vgl[:, un["vt"], h * GL_DV:(h + 1) * GL_DV], start=True, stop=True)
                        mm.then_inc(ud, 1)
                    for j, part in bursts[u]:
                        if part == 0 and j:
                            pe.wait_ge(emptied["D"], CH[("row", j - 1)]["tiles"][0]["nth"])
                        project(pe, ("row", j), lambda kind: (csel_hi, csel_lo), part=part)

        if dump == "gla":
            return finish(nc, out, es, sem, ogl)

        oglT_hi = at("oglT_hi", [P, KD, SEQ], 132, R)
        oglT_lo = at("oglT_lo", [P, KD, SEQ], 148, R)
        oscT_hi = at("oscT_hi", [P, 4, SEQ], 100, R)
        oscT_lo = at("oscT_lo", [P, 4, SEQ], 108, R)
        cT = at("cT", [P, 4, SEQ], 164)
        uT = at("uT", [P, 4, SEQ + 2], 172)
        sr = at("sr", [P, 2, 512], 181)
        gnr = at("gnr", [P, GL_DV], 185)
        jk = at("jk", [P, GL_DV], 186)
        bsc = sr
        gn_in, cw_in, osq, oms, opow, onrm, srd, srm, u0, ud2, cvd, bsd, bhi, ona_hi = (
            esem(n) for n in "gn_in cw_in o_squares o_ms o_rstd o_normed silu_r gated u_edges u_done conv b_times sc_hi ona_hi".split())
        LAST5 = CH[("b",)]["last"]
        with nc.Block() as block:
            @block.sync
            def _(sp):
                sp.dma_start(gnr[:, :], bass.AP(tensor=gla_norm_g.tensor, offset=0, ap=[[0, P], [1, GL_DV]])).then_inc(gn_in, 16)
                for w in range(3):
                    sp.dma_start(convw[:, w, :], conv_w[0, w].rearrange("(m p) -> p m", p=P), allow_slow_non_contiguous=True)\
                      .then_inc(cw_in, 16)
                load_to(sp, LAST5 + 3)

            @block.gpsimd
            def _(pool):
                pool.wait_ge(oms, 1)
                pool.tensor_tensor(rstd[:, 0:16], ssum[:, 0:16], mhalf[:, 0:16], ALU.pow).then_inc(opow, 1)

            @block.scalar
            def _(act):
                act.activation(onaT_hi[:, :, :], onaT[:, :, :], ACT.Copy).then_inc(ona_hi, 1)
                for t in range(TT):
                    for h in range(GL_H):
                        ach(act, act.activation(jk[:, :], ogl[:, t, h * GL_DV:(h + 1) * GL_DV], ACT.Square,
                                                accum_out=ssum[:, GL_H * t + h:GL_H * t + h + 1]))
                act.copy(tiny[:, 67:68], ssum[:, 0:1]).then_inc(osq, 1)
                for j in range(2):
                    split_hi(act, CH[("r", j)]["last"] + 2)
                    for tile in CH[("r", j)]["tiles"]:
                        act.wait_ge(tile_done, tile["n"] + 1)
                        n = TT * j + tile["t"]
                        if n >= 2:
                            act.wait_ge(srm, n - 1)
                        act.activation(sr[:, n % 2, :], PS[:, tile["bank"], :], ACT.Silu).then_inc(emptied["A"], 1)
                split_hi(act, CH[("c",)]["last"] + 2)
                copy_tiles(act, "A", ("c",), lambda kind, m: cT[:, m, :])
                split_hi(act, CH[("x",)]["last"] + 2)
                split_hi(act, CH[("b",)]["last"] + 2)
                for m in range(4):
                    act.wait_ge(bsd, m + 1)
                    act.activation(oscT_hi[:, m, :], bsc[:, m % 2, :], ACT.Copy).then_inc(bhi, 1)
                turn_out_hi(act, oglT_hi, KD, [0, 1, 2, 3])

            @block.vector
            def _(dve):
                dve.wait_ge(osq, 1)
                dve.tensor_scalar(ssum[:, 0:16], ssum[:, 0:16], 1.0 / GL_DV, EPS, ALU.mult, ALU.add).then_inc(oms, 1)
                dve.memset(uT[:, :, 0:SEQ + 2:SEQ + 1], 0.0).then_inc(u0, 1)
                dve.wait_ge(opow, 1)
                dve.wait_ge(gn_in, 16)
                for t in range(TT):
                    for h in range(GL_H):
                        n = GL_H * t + h
                        o = ogl[:, t, h * GL_DV:(h + 1) * GL_DV]
                        ins = dve.scalar_tensor_tensor(out=o, in0=o, scalar=rstd[:, n:n + 1], in1=gnr[:, :],
                                                       op0=ALU.mult, op1=ALU.mult)
                ins.then_inc(onrm, 1)
                dve.wait_ge(onrm, 1)
                dve.wait_ge(ona_hi, 1)
                dve.tensor_tensor(onaT_lo[:, :, :], onaT[:, :, :], onaT_hi[:, :, :].bitcast(F), ALU.subtract)
                for j in range(2):
                    split_lo(dve, CH[("r", j)]["last"] + 2)
                    for tile in CH[("r", j)]["tiles"]:
                        n = TT * j + tile["t"]
                        dve.wait_ge(emptied["A"], tile["nth"])
                        o = ogl[:, tile["t"], 512 * j:512 * j + 512]
                        dve.tensor_tensor(o, o, sr[:, n % 2, :], ALU.mult).then_inc(srm, 1)
                split_lo(dve, CH[("x",)]["last"] + 2)
                for tile in CH[("x",)]["tiles"]:
                    m = tile["t"]
                    dve.wait_ge(tile_done, tile["n"] + 1)
                    wait_tiles(dve, ("c",))
                    dve.tensor_tensor(uT[:, m, 1:SEQ + 1], PS[:, tile["bank"], :], cT[:, m, :], ALU.mult).then_inc(emptied["D"], 1)
                wait_tiles(dve, ("x",))
                dve.wait_ge(cw_in, 48)
                dve.wait_ge(u0, 1)
                for w in range(3):
                    for m in range(4):
                        if w == 0:
                            ins = dve.tensor_scalar(cT[:, m, :], uT[:, m, 0:SEQ], convw[:, 0, m:m + 1], None, ALU.mult)
                        else:
                            ins = dve.scalar_tensor_tensor(out=cT[:, m, :], in0=uT[:, m, w:SEQ + w], scalar=convw[:, w, m:m + 1],
                                                           in1=cT[:, m, :], op0=ALU.mult, op1=ALU.add)
                    dch(dve, ins)
                split_lo(dve, CH[("b",)]["last"] + 2)
                dve.wait_ge(srm, 2 * TT)
                for tile in CH[("b",)]["tiles"]:
                    m = tile["t"]
                    dve.wait_ge(tile_done, tile["n"] + 1)
                    dve.tensor_tensor(bsc[:, m % 2, :], PS[:, tile["bank"], :], cT[:, m, :], ALU.mult).then_inc(bsd, 1)
                    dve.wait_ge(bhi, m + 1)
                    dve.tensor_tensor(oscT_lo[:, m, :], bsc[:, m % 2, :], oscT_hi[:, m, :].bitcast(F), ALU.subtract).then_inc(emptied["D"], 1)
                    dve.wait_ge(emptied["D"], tile["nth"])
                turn_out_lo(dve, oglT_lo, oglT_hi, KD, [0, 1, 2, 3])

            @block.tensor
            def _(pe):
                for name in (("r", 0), ("r", 1), ("c",), ("x",), ("b",)):
                    project(pe, name, acts)
                wait_tiles(pe, ("b",))
                wait_tiles(pe, ("c",))
                pe.wait_ge(srm, 2 * TT)
                turn(pe, lambda t, m: ogl[:, t, m * P:(m + 1) * P], KD, [0, 1, 2, 3])

        yT_hi = at("yT_hi", [P, KD, SEQ], 164, R)
        yT_lo = at("yT_lo", [P, KD, SEQ], 180, R)
        yacc = at("yacc", [P, 4, SEQ], 196)
        sgate = at("sgate", [P, 4, SEQ], 4)
        ymul, yhi = sem("y_times"), sem("y_hi")
        branch = {"b0": (onaT_hi, onaT_lo), "b1": (oscT_hi, oscT_lo), "b2": (oglT_hi, oglT_lo)}
        LAST6 = CH[("br", 1, 2)]["last"]
        jb = [(j, br) for j in range(2) for br in range(3)]
        with nc.Block() as block:
            @block.sync
            def _(sp):
                load_to(sp, LAST6 + 3)

            @block.gpsimd
            def _(pool):
                for s in early_sems:
                    pool.sem_clear(s)

            @block.scalar
            def _(act):
                for n, (j, br) in enumerate(jb):
                    split_hi(act, CH[("gate", j, br)]["last"] + 2)
                    for tile in CH[("gate", j, br)]["tiles"]:
                        act.wait_ge(tile_done, tile["n"] + 1)
                        if n:
                            act.wait_ge(emptied["D"], CH[("br", *jb[n - 1])]["tiles"][tile["t"]]["nth"])
                        act.activation(sgate[:, tile["t"], :], PS[:, tile["bank"], :], ACT.Sigmoid).then_inc(emptied["A"], 1)
                    split_hi(act, CH[("br", j, br)]["last"] + 2)
                    if br == 2:
                        for tile in CH[("br", j, br)]["tiles"]:
                            act.wait_ge(emptied["D"], tile["nth"])
                            act.activation(yT_hi[:, 4 * j + tile["t"], :], yacc[:, tile["t"], :], ACT.Copy).then_inc(yhi, 1)

            @block.vector
            def _(dve):
                for n, (j, br) in enumerate(jb):
                    split_lo(dve, CH[("gate", j, br)]["last"] + 2)
                    split_lo(dve, CH[("br", j, br)]["last"] + 2)
                    for tile in CH[("br", j, br)]["tiles"]:
                        m = tile["t"]
                        dve.wait_ge(tile_done, tile["n"] + 1)
                        dve.wait_ge(emptied["A"], CH[("gate", j, br)]["tiles"][m]["nth"])
                        if br == 0:
                            dve.tensor_tensor(yacc[:, m, :], PS[:, tile["bank"], :], sgate[:, m, :], ALU.mult).then_inc(emptied["D"], 1)
                        else:
                            dch(dve, dve.tensor_tensor(sgate[:, m, :], PS[:, tile["bank"], :], sgate[:, m, :], ALU.mult))
                            dve.tensor_tensor(yacc[:, m, :], yacc[:, m, :], sgate[:, m, :], ALU.add).then_inc(emptied["D"], 1)
                    dve.wait_ge(emptied["D"], CH[("br", j, br)]["tiles"][-1]["nth"])
                    if br == 2:
                        for m in range(4):
                            dve.wait_ge(yhi, 4 * j + m + 1)
                            ins = dve.tensor_tensor(yT_lo[:, 4 * j + m, :], yacc[:, m, :], yT_hi[:, 4 * j + m, :].bitcast(F), ALU.subtract)
                        dch(dve, ins)

            @block.tensor
            def _(pe):
                for j, br in jb:
                    project(pe, ("gate", j, br), acts)
                    project(pe, ("br", j, br), lambda kind: branch[kind])

        early.close()
        if dump == "y":
            return finish(nc, out, es, sem, yT_hi)

        x1 = at("x1", [P, TT, D], 68)
        shacc = at("shacc", [P, TT, D], 84)
        gt2 = at("gt2", [P, D], 100)
        gt1 = at("gt1", [P, D], 104)
        sh2 = at("sh2", [P, D], 108)
        sc2 = at("sc2", [P, D], 112)
        bm4 = at("bm4", [P, 4, D], 116)
        g2r = at("g2r", [P, D], 132)
        ptmp = at("ptmp", [P, 2, 512], 136)
        brt = at("brt", [P, NE], 140)
        h2 = at("h2", [P, TT, D], 148)
        wr = at("wr", [P, KD, P], 196)
        wr_hi = at("wr_hi", [P, KD, P], 134, R)
        wr_lo = at("wr_lo", [P, KD, P], 142, R)
        h2T_hi = at("h2T_hi", [P, KD, SEQ], 164, R)
        h2T_lo = at("h2T_lo", [P, KD, SEQ], 180, R)
        rows_in, x1d, h2d, g1rows, sqd2, ms2, pw2, wrd = (sem(n) for n in "rows_in x1 h2 rows squares2 ms2 rstd2 wr".split())
        h2_out, rt_done = sem("h2_out"), sem("router")
        h2_dram = dram("h2_dram", [SEQ, D])
        LASTM = CH[("out", 1)]["last"]
        with nc.Block() as block:
            @block.sync
            def _(sp):
                sp.dma_start(x1[:, :, :], x[0].rearrange("(t p) d -> p t d", p=P)).then_inc(rows_in, 16)
                sp.dma_start(bm4[:, :, :], bass.AP(tensor=b_mod.tensor, offset=2 * D, ap=[[0, P], [D, 4], [1, D]])).then_inc(rows_in, 16)
                for n, (dst, w) in enumerate(zip((gt1, sh2, sc2, gt2), range(4))):
                    sp.dma_start(dst[:, :], bass.AP(tensor=rows_dram.tensor, offset=w * D, ap=[[0, P], [1, D]])).then_inc(rows_in, 16)
                load_to(sp, CH[("out", 1)]["last"] + 3)

            @block.gpsimd
            def _(pool):
                pool.dma_start(g2r[:, :], bass.AP(tensor=g_norm2.tensor, offset=0, ap=[[0, P], [1, D]])).then_inc(cpy, 16)
                pool.wait_ge(cpy, 32)
                pool.wait_ge(ms2, 1)
                pool.tensor_tensor(rstd[:, 0:TT], ssum[:, 0:TT], mhalf[:, 0:TT], ALU.pow).then_inc(pw2, 1)

            @block.scalar
            def _(act):
                for name in (("out", 0), ("out", 1)):
                    split_hi(act, CH[name]["last"] + 2)
                act.wait_ge(x1d, 2 * TT)
                for t in range(TT):
                    ach(act, act.activation(ptmp[:, :, :], x1[:, t, :], ACT.Square, accum_out=ssum[:, t:t + 1]))
                act.copy(tiny[:, 67:68], ssum[:, 0:1]).then_inc(sqd2, 1)

            @block.vector
            def _(dve):
                dve.wait_ge(rows_in, 96)
                for n, row in enumerate((gt1, sh2, sc2, gt2)):
                    ins = dve.tensor_tensor(row[:, :], row[:, :], bm4[:, n, :], ALU.add)
                dch(dve, ins)
                for j in range(2):
                    split_lo(dve, CH[("out", j)]["last"] + 2)
                    for tile in CH[("out", j)]["tiles"]:
                        t = tile["t"]
                        dve.wait_ge(tile_done, tile["n"] + 1)
                        dve.tensor_tensor(ptmp[:, t % 2, :], PS[:, tile["bank"], :], gt1[:, 512 * j:512 * j + 512], ALU.mult)\
                           .then_inc(emptied["D"], 1)
                        dve.wait_ge(emptied["D"], tile["nth"])
                        o = x1[:, t, 512 * j:512 * j + 512]
                        dve.tensor_tensor(o, o, ptmp[:, t % 2, :], ALU.add).then_inc(x1d, 1)
                dve.wait_ge(sqd2, 1)
                dve.tensor_scalar(ssum[:, 0:TT], ssum[:, 0:TT], 1.0 / D, EPS, ALU.mult, ALU.add).then_inc(ms2, 1)
                dve.wait_ge(cpy, 32)
                dch(dve, dve.scalar_tensor_tensor(out=sc2[:, :], in0=sc2[:, :], scalar=1.0, in1=g2r[:, :], op0=ALU.add, op1=ALU.mult))
                dve.wait_ge(pw2, 1)
                for t in range(TT):
                    dch(dve, dve.scalar_tensor_tensor(out=h2[:, t, :], in0=x1[:, t, :], scalar=rstd[:, t:t + 1], in1=sc2[:, :],
                                                      op0=ALU.mult, op1=ALU.mult))
                    dve.tensor_tensor(h2[:, t, :], h2[:, t, :], sh2[:, :], ALU.add).then_inc(h2d, 1)

            @block.tensor
            def _(pe):
                for j in range(2):
                    project(pe, ("out", j), lambda kind: (yT_hi, yT_lo))

        if dump == "h2":
            return finish(nc, out, es, sem, h2)
        wk = at("wk", [P, TT, TOPK], 202)
        tokidx = at("tokidx", [P, NBLK], 202.5, U32)
        blkrow = at("blkrow", [1, P], 203, I32)
        blkcol = at("blkcol", [P, 4], 203.5)
        blkint = at("blkint", [P, 4], 203.625, I32)
        iota = at("iota", [P, TT], 203.75)
        slot = at("slot", [P, TT, TOPK], 203.875)
        cols = at("cols", [P, P], 204)
        slotidx = at("slotidx", [P, NBLK], 205, U32)
        rowhot = at("rowhot", [P, 2, TOPK, P], 148)
        blkhot = at("blkhot", [P, 2, TOPK, NBLK], 156)
        scoreT = at("scoreT", [NE, SEQ], 146)
        ones = at("ones", [P, P], 204.5)
        shid = at("shid", [P, TT, FF], 104)
        sgl = at("sgl", [P, TT, FF], 108)
        sT_hi = at("sT_hi", [P, 2, SEQ], 112, R)
        sT_lo = at("sT_lo", [P, 2, SEQ], 116, R)

        def pk(name, shape, kb):
            return at(name, [P] + shape, kb)

        sel, selm, rep = (pk(n, [TT, NE], 121 + i) for i, n in enumerate(("sel", "selm", "rep")))
        chosen, gw, vpos = (pk(n, [TT, NE], 124 + i) for i, n in enumerate(("chosen", "gw", "vpos")))
        g8 = pk("g8", [TT, NG, 8], 127)
        gs, gtop, gmask, top8, d1 = (pk(n, [TT, 8], 128 + 0.125 * i) for i, n in enumerate(("gs", "gtop", "gmask", "top8", "d1")))
        wsum = pk("wsum", [TT], 128.75)
        cnt, nbl, bend, bst, jle = (pk(n, [NE], 129 + 0.25 * i) for i, n in enumerate(("cnt", "nbl", "bend", "bst", "jle")))
        eqk = pk("eqk", [TOPK, NE], 131)
        dest, dblk, drow = (pk(n, [TT, TOPK], 130.25 + 0.125 * i) for i, n in enumerate(("dest", "dblk", "drow")))
        lists, nolist = (pk(n, [NBLK], 133 + 0.375 * i) for i, n in enumerate(("lists", "nolist")))
        (wr_in, h2T_done, scored, scoreT_t, sgd, hidd, chosen_done, rank_done, rank_read, blk_done, blk_t, zeros2,
         hot_done, hot_used, ones_done) = (sem(n) for n in (
             "wr_in h2T scored scores_turned sh_silu sh_hid chosen ranks ranks_read blocks blocks_turned zeros2 "
             "onehots onehots_used ones_done".split()))
        sh_tiles = CH[("sh",)]["tiles"]
        nb = [(sh_tiles[0]["bank"] + i) % 8 for i in range(8)]
        B_RT, B_RK, B_CT, B_T2 = nb[4], nb[5], nb[6], nb[7]
        turn_banks = [b for b in range(4)]
        with nc.Block() as block:
            @block.sync
            def _(sp):
                sp.dma_start(wr[:, :, 0:NE], w_router[0].rearrange("(k p) n -> p k n", p=P)).then_inc(wr_in, 16)
                sp.dma_start(brt[:, :], bass.AP(tensor=b_router.tensor, offset=0, ap=[[0, P], [1, NE]])).then_inc(wr_in, 16)
                sp.dma_start(iota[:, :], k_iota).then_inc(wr_in, 16)
                sp.dma_start(slot[:, :, :], k_slot).then_inc(wr_in, 16)
                sp.dma_start(cols[:, :], k_cols).then_inc(wr_in, 16)
                sp.dma_start(h2_dram.rearrange("(t p) d -> p t d", p=P), h2[:, :, :]).then_inc(h2_out, 16)
                load_to(sp, len(HALVES))
                sp.wait_ge(h2_out, 16)
                sp.wait_ge(wr_in, 80)

            @block.gpsimd
            def _(pool):
                pool.memset(wr[:, :, NE:], 0.0).then_inc(zeros2, 1)
                pool.memset(ones[:, :], 1.0).then_inc(ones_done, 1)

            @block.scalar
            def _(act):
                act.wait_ge(wr_in, 80)
                act.wait_ge(zeros2, 1)
                act.activation(wr_hi[:, :, :], wr[:, :, :], ACT.Copy).then_inc(wrd, 1)
                turn_out_hi(act, h2T_hi, KD, turn_banks)
                act.wait_ge(h2T_done, 1)
                act.activation(scoreT[:, :], PS[0:NE, B_RT, :], ACT.Sigmoid).then_inc(scored, 1)
                split_hi(act, CH[("sh",)]["last"] + 2)
                for tile in sh_tiles:
                    act.wait_ge(tile_done, tile["n"] + 1)
                    act.activation(sgl[:, tile["t"], :], PS[:, tile["bank"], 0:FF], ACT.Silu).then_inc(sgd, 1)
                turn_out_hi(act, sT_hi, 2, [B_T2, B_RT])

            @block.vector
            def _(dve):
                dve.wait_ge(wrd, 1)
                dve.tensor_tensor(wr_lo[:, :, :], wr[:, :, :], wr_hi[:, :, :].bitcast(F), ALU.subtract).then_inc(wrd, 1)
                turn_out_lo(dve, h2T_lo, h2T_hi, KD, turn_banks)
                split_lo(dve, CH[("sh",)]["last"])
                dve.wait_ge(scoreT_t, 1)
                score = PS[:, B_RT, 0:TT * NE].rearrange("p (t e) -> p t e", t=TT)
                dch(dve, dve.tensor_tensor(sel[:, :, :], score, brt[:, None, :].to_broadcast([P, TT, NE]), ALU.add))
                for t in range(TT):
                    for g in range(NG):
                        ins = dve.max(g8[:, t, g, :], sel[:, t, g * 8:(g + 1) * 8])
                dch(dve, ins)
                dch(dve, dve.tensor_tensor(gs[:, :, :], g8[:, :, :, 0], g8[:, :, :, 1], ALU.add))
                for t in range(TT):
                    ins = dve.max(gtop[:, t, :], gs[:, t, :])
                dch(dve, ins)
                dch(dve, dve.tensor_tensor(gmask[:, :, :], gs[:, :, :], gtop[:, :, TOPG - 1:TOPG].to_broadcast([P, TT, NG]), ALU.is_ge))
                gm = gmask[:, :, :, None].to_broadcast([P, TT, NG, NE // NG])
                r4 = lambda a: a[:, :, :].rearrange("p t (g e) -> p t g e", g=NG)
                dch(dve, dve.tensor_tensor(r4(selm), r4(sel), gm, ALU.mult))
                dch(dve, dve.tensor_scalar(gmask[:, :, :], gmask[:, :, :], 1.0, -NEG, ALU.subtract, ALU.mult))
                dch(dve, dve.tensor_tensor(r4(selm), r4(selm), gm, ALU.add))
                for t in range(TT):
                    ins = dve.max(top8[:, t, :], selm[:, t, :])
                dch(dve, ins)
                for t in range(TT):
                    ins = dve.match_replace(rep[:, t, :], top8[:, t, :], selm[:, t, :], -3e38)
                dch(dve, ins)
                dve.tensor_tensor(chosen[:, :, :], rep[:, :, :], selm[:, :, :], ALU.not_equal).then_inc(chosen_done, 1)
                dve.wait_ge(chosen_done, 1)
                dch(dve, dve.tensor_tensor(gw[:, :, :], score, chosen[:, :, :], ALU.mult))
                dch(dve, dve.tensor_reduce(wsum[:, :], gw[:, :, :], AX.X, ALU.add))
                dch(dve, dve.reciprocal(wsum[:, :], wsum[:, :]))
                dch(dve, dve.scalar_tensor_tensor(out=gw[:, :, :], in0=gw[:, :, :], scalar=ROUTED_SCALE,
                                                  in1=wsum[:, :, None].to_broadcast([P, TT, NE]), op0=ALU.mult, op1=ALU.mult))
                dve.wait_ge(rank_done, 1)
                dch(dve, dve.tensor_copy(cnt[:, :], PS[:, B_CT, 0:NE]))
                dch(dve, dve.tensor_scalar(nbl[:, :], cnt[:, :], 0.0, None, ALU.is_gt))
                for m in range(1, TT):
                    dch(dve, dve.scalar_tensor_tensor(out=nbl[:, :], in0=cnt[:, :], scalar=float(m * P), in1=nbl[:, :],
                                                      op0=ALU.is_gt, op1=ALU.add))
                dch(dve, dve.tensor_tensor_scan(bend[:, :], ones[:, 0:NE], nbl[:, :], 0.0, ALU.mult, ALU.add))
                dch(dve, dve.tensor_tensor(bst[:, :], bend[:, :], nbl[:, :], ALU.subtract))
                dve.scalar_tensor_tensor(out=vpos[:, :, :], in0=bst[:, None, :].to_broadcast([P, TT, NE]), scalar=float(P),
                                         in1=PS[:, B_RK, 0:TT * NE].rearrange("p (t e) -> p t e", t=TT),
                                         op0=ALU.mult, op1=ALU.add).then_inc(rank_read, 1)
                dve.wait_ge(rank_read, 1)
                dch(dve, dve.scalar_tensor_tensor(out=vpos[:, :, :], in0=vpos[:, :, :], scalar=1.0, in1=chosen[:, :, :],
                                                  op0=ALU.add, op1=ALU.mult))
                for t in range(TT):
                    ins = dve.max(d1[:, t, :], vpos[:, t, :])
                dch(dve, ins)
                dch(dve, dve.tensor_scalar(dest[:, :, :], d1[:, :, :], 1.0, None, ALU.subtract))
                dch(dve, dve.tensor_scalar(dblk[:, :, :], dest[:, :, :], 1.0 / P, 0.5 * (P - 1) / P, ALU.mult, ALU.subtract))
                dch(dve, dve.tensor_scalar(dblk[:, :, :], dblk[:, :, :], ROUND, ROUND, ALU.add, ALU.subtract))
                dch(dve, dve.scalar_tensor_tensor(out=drow[:, :, :], in0=dblk[:, :, :], scalar=-float(P), in1=dest[:, :, :],
                                                  op0=ALU.mult, op1=ALU.add))
                dch(dve, dve.tensor_scalar(jle[:, :], bend[:, :], iota[:, 0:1], None, ALU.is_le))
                dch(dve, dve.tensor_reduce(blkcol[:, 0:1], jle[:, :], AX.X, ALU.add))
                dve.tensor_scalar(blkcol[:, 0:1], blkcol[:, 0:1], float(NE - 1), None, ALU.min).then_inc(blk_done, 1)
                dch(dve, dve.tensor_scalar(blkcol[:, 1:2], bend[:, NE - 1:NE], 0.5, 0.25 - PEEL, ALU.mult, ALU.add))
                dch(dve, dve.tensor_scalar(blkint[:, 1:2], blkcol[:, 1:2], ROUND, ROUND, ALU.add, ALU.subtract))
                dve.wait_ge(h2_out, 16)
                for t in range(TT):
                    if t >= 2:
                        dve.wait_ge(hot_used, t - 1)
                    dve.tensor_tensor(rowhot[:, t % 2], cols[:, None, :].to_broadcast([P, TOPK, P]),
                                      drow[:, t, :, None].to_broadcast([P, TOPK, P]), ALU.is_equal)
                    dch(dve, dve.tensor_tensor(blkhot[:, t % 2], cols[:, None, 0:NBLK].to_broadcast([P, TOPK, NBLK]),
                                               dblk[:, t, :, None].to_broadcast([P, TOPK, NBLK]), ALU.is_equal))
                    dve.tensor_tensor(blkhot[:, t % 2], blkhot[:, t % 2], slot[:, t, :, None].to_broadcast([P, TOPK, NBLK]), ALU.mult)\
                       .then_inc(hot_done, 1)
                dve.wait_ge(blk_t, 1)
                dch(dve, dve.tensor_copy(blkrow[0:1, :], PS[0:1, B_CT, 0:P]))
                dve.wait_ge(hot_used, TT)
                dch(dve, dve.tensor_scalar(nolist[:, :], PS[:, B_T2, 0:NBLK], 0.0, PAD, ALU.is_equal, ALU.mult))
                dch(dve, dve.scalar_tensor_tensor(out=lists[:, :], in0=PS[:, B_T2, 0:NBLK], scalar=1.0, in1=nolist[:, :],
                                                  op0=ALU.subtract, op1=ALU.add))
                dch(dve, dve.tensor_copy(slotidx[:, :], lists[:, :]))
                dch(dve, dve.tensor_scalar(lists[:, :], lists[:, :], 1.0 / TOPK, 0.5 * (TOPK - 1) / TOPK, ALU.mult, ALU.subtract))
                dch(dve, dve.tensor_scalar(tokidx[:, :], lists[:, :], ROUND, ROUND, ALU.add, ALU.subtract))
                for tile in sh_tiles:
                    dve.wait_ge(sgd, tile["t"] + 1)
                    dve.tensor_tensor(shid[:, tile["t"], :], PS[:, tile["bank"], FF:], sgl[:, tile["t"], :], ALU.mult).then_inc(emptied["D"], 1)
                split_lo(dve, len(HALVES))
                turn_out_lo(dve, sT_lo, sT_hi, 2, [B_T2, B_RT])
                for t in range(TT):
                    vb = vpos[:, t:t + 1, :].to_broadcast([P, TOPK, NE])
                    dch(dve, dve.tensor_tensor(eqk[:, :, :], vb, d1[:, t, :, None].to_broadcast([P, TOPK, NE]), ALU.is_equal))
                    dch(dve, dve.tensor_tensor(eqk[:, :, :], eqk[:, :, :], gw[:, t:t + 1, :].to_broadcast([P, TOPK, NE]), ALU.mult))
                    dch(dve, dve.tensor_reduce(wk[:, t, :], eqk[:, :, :], AX.X, ALU.add))
                for tile in CH[("down",)]["tiles"]:
                    dve.wait_ge(tile_done, tile["n"] + 1)
                    t, h = divmod(tile["t"], 2)
                    dve.tensor_copy(shacc[:, t, 512 * h:512 * h + 512], PS[:, tile["bank"], :]).then_inc(emptied["D"], 1)

            @block.tensor
            def _(pe):
                turn(pe, lambda t, m: h2[:, t, m * P:(m + 1) * P], KD, turn_banks)
                pe.wait_ge(turn_lo, nturn[0])
                pe.wait_ge(wrd, 2)
                for k in range(KD):
                    mm = mm3(pe, PS[:, B_RT, :], wr_hi[:, k], wr_lo[:, k], h2T_hi[:, k], h2T_lo[:, k], k == 0, k == KD - 1)
                mm.then_inc(h2T_done, 1)
                pe.wait_ge(scored, 1)
                for t in range(TT):
                    mm = pe.transpose(PS[:, B_RT, t * NE:(t + 1) * NE], scoreT[:, t * P:(t + 1) * P], ident[0:NE, 0:NE])
                mm.then_inc(scoreT_t, 1)
                project(pe, ("sh",), lambda kind: (h2T_hi, h2T_lo), part=0)
                pe.wait_ge(chosen_done, 1)
                pe.wait_ge(ones_done, 1)
                for t in range(TT):
                    for j in range(t + 1):
                        pe.matmul(PS[:, B_RK, t * NE:(t + 1) * NE], tri[:, 2, :] if j == t else ones[:, :], chosen[:, j, :],
                                  start=(j == 0), stop=(j == t))
                for j in range(TT):
                    mm = pe.matmul(PS[:, B_CT, 0:NE], ones[:, :], chosen[:, j, :], start=(j == 0), stop=(j == TT - 1))
                mm.then_inc(rank_done, 1)
                project(pe, ("sh",), lambda kind: (h2T_hi, h2T_lo), part=1)
                pe.wait_ge(blk_done, 1)
                pe.matmul(PS[0:1, B_CT, 0:P], blkcol[:, 0:1], ident[:, :], start=True, stop=True).then_inc(blk_t, 1)
                for t in range(TT):
                    pe.wait_ge(hot_done, t + 1)
                    for k in range(TOPK):
                        mm = pe.matmul(PS[:, B_T2, 0:NBLK], rowhot[:, t % 2, k], blkhot[:, t % 2, k],
                                       start=(t == 0 and k == 0), stop=(t == TT - 1 and k == TOPK - 1))
                    mm.then_inc(hot_used, 1)
                pe.wait_ge(emptied["D"], sh_tiles[-1]["nth"])
                turn(pe, lambda t, m: shid[:, t, m * P:(m + 1) * P], 2, [B_T2, B_RT])
                pe.wait_ge(turn_lo, nturn[0])
                project(pe, ("down",), lambda kind: (sT_hi, sT_lo))

        mhi = at("mhi", [P, 6, 2048], 104, R)
        mlo = at("mlo", [P, 6, 2048], 152, R)
        wraw = at("wraw", [P, 6, 2048], 152)
        xg = at("xg", [P, 2, D], 12)
        xT_hi = at("xT_hi", [P, 2, KD, P], 20, R)
        xT_lo = at("xT_lo", [P, 2, KD, P], 28, R)
        mhid = at("mhid", [P, 2, FF], 36)
        hT2_hi = at("hT2_hi", [P, 2, 2, P], 38, R)
        hT2_lo = at("hT2_lo", [P, 2, 2, P], 40, R)
        ysb = at("ysb", [P, 2, D], 42)
        msg = at("msg", [P, 2, FF], 50)
        idxcur = at("idxcur", [P, 2], 53.5, U32)
        slotcur = at("slotcur", [P, 2], 53.625, U32)
        y_dram = dram("y_dram", [SEQ * TOPK, D])
        wland = [sem(f"expert_landed{i}") for i in range(6)]
        mhi_done, mlo_done = ([sem(f"ex_{n}{pc}") for pc in range(3)] for n in ("hi", "lo"))
        (gu0_done, idx_done, idx_seen, xT_t, xT_hid, xT_lod,
         gu_done, silud, mhidd, hT_t, hT_hid, hT_lod, dn_done, y_a, y_d, slot_done, xg_zero) = (sem(n) for n in (
             "ex_half_used idx_col idx_seen ex_xT ex_xT_hi ex_xT_lo "
             "ex_gate_up ex_silu ex_hid ex_hidT ex_hidT_hi ex_hidT_lo ex_down y_act y_dve slot_col ex_x_zero".split()))
        xg_in, y_out = ([sem(f"{n}{u}") for u in range(2)] for n in ("expert_x_in", "y_out"))
        DS = bass.ds
        MAXP = NBLK // 2
        MINP = SEQ * TOPK // P // 2

        def steps(eng, body, last):
            n_pairs = eng.value_load(blkint[0:1, 1:2], min_val=MINP - PEEL, max_val=MAXP - PEEL) + PEEL
            for b in range(2 * PEEL):
                body(b // 2, b % 2, None)
            with eng.Fori(PEEL, MAXP) as i:
                with eng.If(i < n_pairs):
                    for u in range(2):
                        body(i, u, None)
            for k in range(last):
                body(n_pairs, k, k)
            return n_pairs

        def block_of(i, u, back, k):
            b = i * 2 + (u - back)
            return b, (u - back) % 2, not (isinstance(b, int) and b < 0) and (k is None or back > k)

        def some(n):
            return not isinstance(n, int) or n > 0

        def landings(i, u, back):
            return i + ((u - back) // 2 + 1)

        def sent(i, u, back):
            return i * 16 + ((u - back) // 2) * 16

        with nc.Block() as block:
            @block.sync
            def _(sp):
                def load(i, u, back, k, pc):
                    b, par, there = block_of(i, u, back, k)
                    if not there:
                        return
                    e = sp.value_load(blkrow[0:1, DS(b, 1)], min_val=0, max_val=NE - 1)
                    s = 3 * par + pc
                    if some(b - 1):
                        sp.wait_ge((gu0_done, gu_done, dn_done)[pc], b - 1)
                    if pc < 2:
                        dst = wraw[:, s].rearrange("p (c g f) -> p c g f", c=4, g=2)
                        for g, w in enumerate((w_exp_gate, w_exp_up)):
                            src = w[0][DS(e, 1)].rearrange("a (p c) f -> p (a c) f", p=P)[:, 4 * pc:4 * pc + 4, :]
                            sp.dma_start(dst[:, :, g, :], src).then_inc(wland[s], 16)
                    else:
                        src = w_exp_down[0][DS(e, 1)].rearrange("a (p c) n -> p (a c n)", p=P)
                        sp.dma_start(wraw[:, s], src).then_inc(wland[s], 16)

                def body(i, u, k):
                    load(i, u, 0, k, 0)
                    load(i, u, 0, k, 1)
                    load(i, u, 1, k, 2)
                steps(sp, body, 1)

            @block.gpsimd
            def _(pool):
                pool.memset(xg[:, :, :], 0.0).then_inc(xg_zero, 1)
                pool.wait_ge(xg_zero, 1)

                def gather(i, u, k):
                    b, par, there = block_of(i, u, 0, k)
                    if not there:
                        return
                    if some(b - 1):
                        pool.wait_ge(xg_in[par], i * 16)
                        pool.wait_ge(xT_t, b - 1)
                    pool.tensor_copy(idxcur[:, par:par + 1], tokidx[:, DS(b, 1)]).then_inc(idx_done, 1)
                    pool.wait_ge(idx_done, b + 1)
                    pool.sem_inc(idx_seen, 1)
                    pool.indirect_dma_start(xg[:, par, :], None, h2_dram, bass.IndirectOffsetOnAxis(ap=idxcur[:, par:par + 1], axis=0),
                                            bounds_check=SEQ - 1, oob_is_err=False).then_inc(xg_in[par], 16)

                def scatter(i, u, k):
                    b, par, there = block_of(i, u, 4, k)
                    if not there:
                        return
                    if some(b - 1):
                        pool.wait_ge(y_out[par], sent(i, u, 4))
                    pool.tensor_copy(slotcur[:, par:par + 1], slotidx[:, DS(b, 1)]).then_inc(slot_done, 1)
                    pool.wait_ge(slot_done, b + 1)
                    pool.sem_inc(idx_seen, 1)
                    pool.wait_ge(y_a, b + 1)
                    pool.wait_ge(y_d, b + 1)
                    pool.sem_inc(idx_seen, 1)
                    pool.indirect_dma_start(y_dram, bass.IndirectOffsetOnAxis(ap=slotcur[:, par:par + 1], axis=0), ysb[:, par, :], None,
                                            bounds_check=SEQ * TOPK - 1, oob_is_err=False).then_inc(y_out[par], 16)

                def body(i, u, k):
                    gather(i, u, k)
                    scatter(i, u, k)
                n_pairs = steps(pool, body, 4)
                for s in y_out:
                    pool.wait_ge(s, n_pairs * 16)

            @block.scalar
            def _(act):
                def hi(i, u, back, k, pc):
                    b, par, there = block_of(i, u, back, k)
                    if not there:
                        return
                    s = 3 * par + pc
                    act.wait_ge(wland[s], landings(i, u, back) * (32 if pc < 2 else 16))
                    act.activation(mhi[:, s, :], wraw[:, s], ACT.Copy).then_inc(mhi_done[pc], 1)

                def silu(i, u, k):
                    b, par, there = block_of(i, u, 1, k)
                    if there:
                        act.wait_ge(gu_done, b + 1)
                        if some(b - 1):
                            act.wait_ge(mhidd, b - 1)
                        act.activation(msg[:, par, :], PS[:, par, 0:FF], ACT.Silu).then_inc(silud, 1)

                def rows_hi(i, u, k):
                    b, par, there = block_of(i, u, 0, k)
                    if there:
                        act.wait_ge(xT_t, b + 1)
                        if some(b - 1):
                            act.wait_ge(gu_done, b - 1)
                        for h in range(2):
                            act.activation(xT_hi[:, par, 4 * h:4 * h + 4, :], PS[:, 2 + h, :], ACT.Copy).then_inc(xT_hid, 1)

                def hidden_hi(i, u, k):
                    b, par, there = block_of(i, u, 2, k)
                    if there:
                        act.wait_ge(hT_t, b + 1)
                        if some(b - 1):
                            act.wait_ge(dn_done, b - 1)
                        act.activation(hT2_hi[:, par], PS[:, 4, 0:2 * P], ACT.Copy).then_inc(hT_hid, 1)

                def result(i, u, k):
                    b, par, there = block_of(i, u, 3, k)
                    if there:
                        act.wait_ge(dn_done, b + 1)
                        if some(b - 1):
                            act.wait_ge(y_out[par], sent(i, u, 3))
                        act.activation(ysb[:, par, 0:512], PS[:, 5, :], ACT.Copy).then_inc(y_a, 1)

                def body(i, u, k):
                    hi(i, u, 0, k, 0)
                    rows_hi(i, u, k)
                    hidden_hi(i, u, k)
                    result(i, u, k)
                    hi(i, u, 0, k, 1)
                    silu(i, u, k)
                    hi(i, u, 1, k, 2)
                steps(act, body, 3)

            @block.vector
            def _(dve):
                def lo(i, u, back, k, pc):
                    b, par, there = block_of(i, u, back, k)
                    if not there:
                        return
                    s = 3 * par + pc
                    dve.wait_ge(mhi_done[pc], b + 1)
                    dve.tensor_tensor(mlo[:, s, :], wraw[:, s, :], mhi[:, s, :].bitcast(F), ALU.subtract).then_inc(mlo_done[pc], 1)

                def hidden(i, u, k):
                    b, par, there = block_of(i, u, 1, k)
                    if there:
                        dve.wait_ge(silud, b + 1)
                        if some(b - 1):
                            dve.wait_ge(hT_t, b - 1)
                        dve.tensor_tensor(mhid[:, par, :], PS[:, par, FF:], msg[:, par, :], ALU.mult).then_inc(mhidd, 1)

                def rows_lo(i, u, k):
                    b, par, there = block_of(i, u, 0, k)
                    if there:
                        for h in range(2):
                            dve.wait_ge(xT_hid, b * 2 + (h + 1))
                            dve.tensor_tensor(xT_lo[:, par, 4 * h:4 * h + 4, :], PS[:, 2 + h, :],
                                              xT_hi[:, par, 4 * h:4 * h + 4, :].bitcast(F), ALU.subtract).then_inc(xT_lod, 1)

                def hidden_lo(i, u, k):
                    b, par, there = block_of(i, u, 2, k)
                    if there:
                        dve.wait_ge(hT_hid, b + 1)
                        dve.tensor_tensor(hT2_lo[:, par], PS[:, 4, 0:2 * P], hT2_hi[:, par].bitcast(F), ALU.subtract).then_inc(hT_lod, 1)

                def result(i, u, k):
                    b, par, there = block_of(i, u, 3, k)
                    if there:
                        dve.wait_ge(dn_done, b + 1)
                        if some(b - 1):
                            dve.wait_ge(y_out[par], sent(i, u, 3))
                        dve.tensor_copy(ysb[:, par, 512:], PS[:, 6, :]).then_inc(y_d, 1)

                def body(i, u, k):
                    lo(i, u, 0, k, 0)
                    rows_lo(i, u, k)
                    hidden_lo(i, u, k)
                    result(i, u, k)
                    lo(i, u, 0, k, 1)
                    hidden(i, u, k)
                    lo(i, u, 1, k, 2)
                steps(dve, body, 3)

            @block.tensor
            def _(pe):
                def turn_rows(i, u, k):
                    b, par, there = block_of(i, u, 0, k)
                    if there:
                        pe.wait_ge(xg_in[par], i * 16 + 16)
                        if some(b):
                            pe.wait_ge(xT_lod, b * 2)
                        for c in range(KD):
                            mm = pe.transpose(PS[:, 2 + c // 4, (c % 4) * P:(c % 4 + 1) * P], xg[:, par, c:D:KD], ident[:, :])
                        mm.then_inc(xT_t, 1)

                def turn_hidden(i, u, k):
                    b, par, there = block_of(i, u, 2, k)
                    if there:
                        pe.wait_ge(mhidd, b + 1)
                        if some(b):
                            pe.wait_ge(hT_lod, b)
                        for c in range(2):
                            mm = pe.transpose(PS[:, 4, c * P:(c + 1) * P], mhid[:, par, c:FF:2], ident[:, :])
                        mm.then_inc(hT_t, 1)

                def gate_up(i, u, k):
                    b, par, there = block_of(i, u, 1, k)
                    if there:
                        pe.wait_ge(xT_lod, b * 2 + 2)
                        for pc in range(2):
                            pe.wait_ge(mlo_done[pc], b + 1)
                            for c in range(4):
                                w = slice(c * 512, (c + 1) * 512)
                                s = 3 * par + pc
                                mm = mm3(pe, PS[:, par, :], xT_hi[:, par, 4 * pc + c], xT_lo[:, par, 4 * pc + c], mhi[:, s, w], mlo[:, s, w],
                                         pc == 0 and c == 0, pc == 1 and c == 3)
                            mm.then_inc(gu_done if pc else gu0_done, 1)

                def down(i, u, k):
                    b, par, there = block_of(i, u, 2, k)
                    if there:
                        pe.wait_ge(hT_lod, b + 1)
                        pe.wait_ge(mlo_done[2], b + 1)
                        if some(b):
                            pe.wait_ge(y_a, b)
                            pe.wait_ge(y_d, b)
                        s = 3 * par + 2
                        for c in range(2):
                            for n in range(2):
                                w = slice((2 * c + n) * 512, (2 * c + n + 1) * 512)
                                mm = mm3(pe, PS[:, 5 + n, :], hT2_hi[:, par, c], hT2_lo[:, par, c], mhi[:, s, w], mlo[:, s, w],
                                         c == 0, c == 1)
                        mm.then_inc(dn_done, 1)

                def body(i, u, k):
                    turn_rows(i, u, k)
                    turn_hidden(i, u, k)
                    gate_up(i, u, k)
                    down(i, u, k)
                steps(pe, body, 3)

        NYB = 3
        HK = TOPK // 2
        yb = at("yb", [P, NYB, HK, D], 104)
        gfr = at("gfr", [P, D], 12)
        fin = at("fin", [P, TT, D], 16)
        jf = at("jf", [P, D], 32)
        y_in = [sem(f"rows_in{i}") for i in range(NYB)]
        summed, gf_in, x2d, sq3, ms3, pw3, find, out_done = (sem(n) for n in "summed gf_in x2 squares3 ms3 rstd3 final out_done".split())
        with nc.Block() as block:
            @block.sync
            def _(sp):
                rows = y_dram.rearrange("(t p k) d -> t p k d", t=TT, p=P)
                for n in range(2 * TT):
                    t, h = divmod(n, 2)
                    if n >= NYB:
                        sp.wait_ge(summed, (n - NYB + 1) * HK)
                    sp.dma_start(yb[:, n % NYB], rows[t, :, h * HK:(h + 1) * HK, :]).then_inc(y_in[n % NYB], 16)
                    if n == 0:
                        sp.dma_start(gfr[:, :], bass.AP(tensor=g_final.tensor, offset=0, ap=[[0, P], [1, D]])).then_inc(gf_in, 16)
                for t in range(TT):
                    sp.wait_ge(find, t + 1)
                    sp.dma_start(out[t * P:(t + 1) * P, :], fin[:, t, :]).then_inc(out_done, 16)
                sp.wait_ge(out_done, 16 * TT)

            @block.gpsimd
            def _(pool):
                for t in range(TT):
                    pool.wait_ge(ms3, t + 1)
                    pool.tensor_tensor(rstd[:, t:t + 1], ssum[:, t:t + 1], mhalf[:, t:t + 1], ALU.pow).then_inc(pw3, 1)

            @block.scalar
            def _(act):
                for t in range(TT):
                    act.wait_ge(x2d, t + 1)
                    act.activation(jf[:, :], fin[:, t, :], ACT.Square, accum_out=ssum[:, t:t + 1]).then_inc(sq3, 1)
                    act.wait_ge(sq3, t + 1)

            @block.vector
            def _(dve):
                for n in range(TT * TOPK):
                    t, k = divmod(n, TOPK)
                    part = n // HK
                    dve.wait_ge(y_in[part % NYB], 16 * (part // NYB + 1))
                    if n:
                        dve.wait_ge(summed, n)
                    dve.scalar_tensor_tensor(out=shacc[:, t, :], in0=yb[:, part % NYB, k % HK, :], scalar=wk[:, t, k:k + 1], in1=shacc[:, t, :],
                                             op0=ALU.mult, op1=ALU.add).then_inc(summed, 1)
                    if k == TOPK - 1:
                        dve.wait_ge(summed, n + 1)
                        dch(dve, dve.tensor_tensor(shacc[:, t, :], shacc[:, t, :], gt2[:, :], ALU.mult))
                        dve.tensor_tensor(fin[:, t, :], x1[:, t, :], shacc[:, t, :], ALU.add).then_inc(x2d, 1)
                        dve.wait_ge(sq3, t + 1)
                        dve.tensor_scalar(ssum[:, t:t + 1], ssum[:, t:t + 1], 1.0 / D, EPS, ALU.mult, ALU.add).then_inc(ms3, 1)
                dve.wait_ge(gf_in, 16)
                for t in range(TT):
                    dve.wait_ge(pw3, t + 1)
                    dve.scalar_tensor_tensor(out=fin[:, t, :], in0=fin[:, t, :], scalar=rstd[:, t:t + 1], in1=gfr[:, :],
                                             op0=ALU.mult, op1=ALU.mult).then_inc(find, 1)
    return nc


def finish(nc, out, es, sem, *ts):
    s = sem("dump")
    with nc.Block() as block:
        @block.sync
        def _(sp):
            n = 0
            for t in ts:
                f = int(np.prod(t.shape[1:]))
                fl = t[:] if len(t.shape) == 2 else t[:].rearrange("p a b -> p (a b)")
                sp.dma_start(bass.AP(tensor=out.tensor, offset=n, ap=[[f, P], [1, f]]), fl.bitcast(F)).then_inc(s, 16)
                n += P * f
            sp.wait_ge(s, 16 * len(ts))
    return nc


_INS = ['x', 'c', 'ctx', 'c_ctx', 'w_mod', 'b_mod', 'g_norm1', 'g_norm2', 'w_in', 'na_rpb', 'w_branch_na', 'conv_w',
        'w_branch_sc', 'gla_gate_w', 'gla_gate_b', 'gla_norm_g', 'w_branch_gla', 'w_out', 'w_router', 'b_router',
        'w_exp_gate', 'w_exp_up', 'w_exp_down', 'w_sh_gate', 'w_sh_up', 'w_sh_down', 'g_final']


def shape_constants():
    s, t = np.arange(P)[:, None], np.arange(P)[None, :]
    tri = np.stack([s <= t, s >= t, s < t]).astype(np.float32)
    q, k = (np.arange(P) % GRID)[:, None], np.arange(GRID)[None, :]
    start = np.clip(q - WIN_C // 2, 0, GRID - WIN_C)
    mask = ((k >= start) & (k < start + WIN_C)).astype(np.int32)
    iota = np.arange(SEQ, dtype=np.float32).reshape(TT, P).T.copy()
    slot = iota[:, :, None] * TOPK + np.arange(1, TOPK + 1, dtype=np.float32)
    return {"k_ident": np.eye(P, dtype=np.float32), "k_tri": tri, "k_mask": mask, "k_iota": iota,
            "k_slot": slot.astype(np.float32), "k_cols": np.tile(np.arange(P, dtype=np.float32), (P, 1))}


def kernel(**inputs):
    import concourse.bacc as _bacc
    from concourse.bass_utils import run_bass_kernel_spmd as _run

    nc = _bacc.Bacc("TRN2", target_bir_lowering=False, num_devices=1)
    arrays, args = {}, []
    tables = shape_constants()
    for name in _INS + list(tables):
        a = np.ascontiguousarray(inputs[name] if name in inputs else tables[name])
        arrays[f"in_{name}_dram"] = a
        args.append(nc.dram_tensor(f"in_{name}_dram", a.shape, mybir.dt.from_np(a.dtype), kind="ExternalInput").ap())
    out = nc.dram_tensor("out_0_dram", (SEQ, D), F, kind="ExternalOutput").ap()
    build(nc, *args, out)
    r = _run(nc, [arrays], core_ids=[0])
    return r.results[0]["out_0_dram"].reshape(1, SEQ, D)
```

```python
from contextlib import ExitStack

import numpy as np
import concourse.bass as bass
from concourse import mybir

P = 128
D = 1024
KD = D // P
SEQ = 512
CTX = 256
TOK = SEQ + CTX
TT = SEQ // P
TC = CTX // P
NA_H, NA_D = 8, 64
GRID = 64
WIN_R, WIN_C = 8, 16
RPB_R, RPB_C = 2 * WIN_R - 1, 2 * WIN_C - 1
GL_H, GL_DK, GL_DV = 4, 128, 256
RANK = 16
TAU = 16.0
NE, NG, TOPG, TOPK, FF = 64, 8, 4, 8, 256
ROUTED_SCALE = 2.5
EPS = 1e-6
NEG = -1e30
ROUND = 1.5 * 2.0 ** 23
PEEL = 3
PAD = 65536.0
NBLK = (SEQ * TOPK + NE * (P - 1)) // P
NBLK += NBLK % 2
RPB_T = RPB_R * RPB_C

F = mybir.dt.float32
R = mybir.dt.float32r
I32 = mybir.dt.int32
U32 = mybir.dt.uint32
ALU = mybir.AluOpType
ACT = mybir.ActivationFunctionType
AX = mybir.AxisListType

K_NA, V_NA, K_GLA, V_GLA, GATE, Q_NA, B_SC, C_SC, X_SC, Q_GLA, R_GLA, MERGE = (
    0, 512, 1024, 1536, 2560, 2592, 3104, 3616, 4128, 4640, 5152, 6176)

NROW = 8
ROW_BANK = 2
KB = 1024
BASE = 18 * KB
NRAW, NSPLIT = 3, 2


class Chain:

    def __init__(self, sem):
        self.sem, self.n = sem, 0

    def __call__(self, eng, ins):
        self.n += 1
        ins.then_inc(self.sem, 1)
        eng.wait_ge(self.sem, self.n)


def plan_tiles():
    halves, chunks, tiles = [], {}, []
    counts = {"A": 0, "D": 0}

    def chunk(name, weight, col, outs, rows=2):
        first = len(halves)
        for k in range(rows):
            halves.append((weight, 4 * k, col))
        mine = []
        for n, (kind, t) in enumerate(outs):
            who = "A" if name[0] in ("r", "c", "gate") else "D" if name[0] in (
                "mod", "x", "b", "br", "out", "row", "sh", "down", "k_na", "q_na") else "AD"[n % 2]
            counts[who] += 1
            tile = dict(n=len(tiles), bank=len(tiles) % 8, who=who, nth=counts[who], kind=kind, t=t)
            mine.append(tile)
            tiles.append(tile)
        chunks[name] = dict(name=name, first=first, last=len(halves) - 1, tiles=mine)

    feat = [("feat", m) for m in range(4)]
    feat_ctx = [("featc", m) for m in range(4)]
    tok = [("tok", t) for t in range(TT)]
    tok_ctx = [("tokc", t) for t in range(TC)]
    row = [("row", 0)]
    for j in range(4):
        chunk(("mod", j), "w_mod", 512 * j, row)
    chunk(("k_na",), "w_in", K_NA, feat + feat_ctx)
    chunk(("v_na",), "w_in", V_NA, tok + tok_ctx)
    chunk(("q_na",), "w_in", Q_NA, feat)
    chunk(("k_gla",), "w_in", K_GLA, feat + feat_ctx)
    chunk(("v_gla", 0), "w_in", V_GLA, tok + tok_ctx)
    chunk(("v_gla", 1), "w_in", V_GLA + 512, tok + tok_ctx)
    chunk(("q_gla",), "w_in", Q_GLA, feat)
    for j in range(NROW):
        chunk(("row", j), "w_mod", 2 * D + 512 * j, row)
        chunks["row", j]["tiles"][0]["bank"] = ROW_BANK
    chunk(("r", 0), "w_in", R_GLA, tok)
    chunk(("r", 1), "w_in", R_GLA + 512, tok)
    chunk(("c",), "w_in", C_SC, feat)
    chunk(("x",), "w_in", X_SC, feat)
    chunk(("b",), "w_in", B_SC, feat)
    for j in range(2):
        for br, (weight, rows) in enumerate((("w_branch_na", 1), ("w_branch_sc", 1), ("w_branch_gla", 2))):
            chunk(("gate", j, br), "w_in", MERGE + br * D + 512 * j, feat)
            chunk(("br", j, br), weight, 512 * j, [(f"b{br}", m) for m in range(4)], rows)
    for j in range(2):
        chunk(("out", j), "w_out", 512 * j, [("y", t) for t in range(TT)])
    chunk(("sh",), "w_sh", 0, tok)
    chunk(("down",), "w_sh_down", 0, [("down", t) for t in range(2 * TT)], 1)
    for n, tile in enumerate(chunks[("down",)]["tiles"]):
        tile["bank"] = (chunks[("sh",)]["tiles"][0]["bank"] + n) % 8
    return halves, chunks, tiles


def build(nc, x, c, ctx, c_ctx, w_mod, b_mod, g_norm1, g_norm2, w_in, na_rpb, w_branch_na, conv_w, w_branch_sc,
          gla_gate_w, gla_gate_b, gla_norm_g, w_branch_gla, w_out, w_router, b_router, w_exp_gate, w_exp_up,
          w_exp_down, w_sh_gate, w_sh_up, w_sh_down, g_final, k_ident, k_tri, k_mask, k_iota, k_slot, k_cols, out, dump=None):
    HALVES, CH, TILES = plan_tiles()
    es = ExitStack()
    weights = {"w_mod": w_mod[0], "w_in": w_in[0], "w_branch_na": w_branch_na[0], "w_branch_sc": w_branch_sc[0],
               "w_branch_gla": w_branch_gla[0], "w_out": w_out[0]}

    def at(name, shape, kb, dt=F):
        return nc.alloc_sbuf_tensor_at(name, shape, dt, offset=BASE + int(kb * KB))

    def sem(name):
        return es.enter_context(nc.semaphore(name))

    early = ExitStack()
    early_sems = []

    def esem(name):
        early_sems.append(early.enter_context(nc.semaphore(name)))
        return early_sems[-1]

    def dram(name, shape, dt=F):
        return nc.dram_tensor(name, shape, dt, kind="Internal").ap()

    with es:
        PS = es.enter_context(nc.psum_tensor("PS", [P, 8, 512], F))
        ident = at("ident", [P, P], 0)
        tri = at("tri", [P, 3, P], 0.5)
        namask = at("namask", [P, GRID], 2, I32)
        small = at("small", [P, 256], 2.5)
        csil = small[:, 0:16].rearrange("p (k w) -> p k w", w=2)
        ccol = small[:, 16:32].rearrange("p (w k) -> p w k", w=2)
        ssum = small[:, 32:48]
        rstd = small[:, 48:64]
        mhalf = small[:, 64:80]
        rsum = small[:, 80:112]
        rinv = small[:, 112:144]
        nmax = small[:, 144:176]
        convw = small[:, 176:188].rearrange("p (w m) -> p w m", w=3)
        tiny = small[:, 188:256]
        csel_hi = at("csel_hi", [P, KD, P], 4, R)
        csel_lo = at("csel_lo", [P, KD, P], 8, R)
        raw = at("raw", [P, NRAW, 4, 512], 12)
        whi = at("whi", [P, NSPLIT, 4, 512], 36, R)
        wlo = at("wlo", [P, NSPLIT, 4, 512], 52, R)
        hT_hi = at("hT_hi", [P, KD, SEQ], 68, R)
        hT_lo = at("hT_lo", [P, KD, SEQ], 84, R)
        hc_hi = at("hc_hi", [P, KD, CTX], 100, R)
        hc_lo = at("hc_lo", [P, KD, CTX], 108, R)
        onaT_hi = at("onaT_hi", [P, 4, SEQ], 116, R)
        onaT_lo = at("onaT_lo", [P, 4, SEQ], 124, R)
        onaT = at("onaT", [P, 4, SEQ], 124)

        landed = [sem(f"weights_landed{i}") for i in range(NRAW)]
        hi_done, lo_done, used = sem("hi_done"), sem("lo_done"), sem("half_used")
        tile_done = sem("tile_done")
        emptied = {"A": sem("emptied_by_act"), "D": sem("emptied_by_dve")}
        dch, ach = Chain(sem("dve_chain")), Chain(sem("act_chain"))

        arrive, per_slot = [], [0] * NRAW
        for i, (w, _, _) in enumerate(HALVES):
            per_slot[i % NRAW] += 32 if w == "w_sh" else 16
            arrive.append(per_slot[i % NRAW])
        freed, firsts = [None] * len(HALVES), 0
        for ch in CH.values():
            for i in range(ch["first"], ch["last"]):
                firsts += 1
                freed[i] = (used, firsts)
            freed[ch["last"]] = (tile_done, ch["tiles"][-1]["n"] + 1)
        splits_a, splits_d = [0], [0]
        nloads = [0]

        def load_to(eng, upto):
            while nloads[0] <= min(upto, len(HALVES) - 1):
                i = nloads[0]
                nloads[0] += 1
                if i >= NRAW:
                    eng.wait_ge(lo_done, i - NRAW + 1)
                w, k, col = HALVES[i]
                dst = raw[:, i % NRAW]
                if w == "w_sh":
                    for n, src in enumerate((w_sh_gate, w_sh_up)):
                        eng.dma_start(dst[:, :, n * FF:(n + 1) * FF],
                                      src[0].rearrange("(k p) n -> p k n", p=P)[:, k:k + 4, :]).then_inc(landed[i % NRAW], 16)
                elif w == "w_sh_down":
                    eng.dma_start(dst.rearrange("p (k h) n -> p k (h n)", h=2),
                                  w_sh_down[0].rearrange("(k p) n -> p k n", p=P)).then_inc(landed[i % NRAW], 16)
                else:
                    eng.dma_start(dst, weights[w].rearrange("(k p) n -> p k n", p=P)[:, k:k + 4, col:col + 512])\
                       .then_inc(landed[i % NRAW], 16)

        def split_hi(act, upto):
            while splits_a[0] <= min(upto, len(HALVES) - 1):
                i = splits_a[0]
                splits_a[0] += 1
                act.wait_ge(landed[i % NRAW], arrive[i])
                if i >= NSPLIT:
                    act.wait_ge(*freed[i - NSPLIT])
                act.activation(whi[:, i % NSPLIT], raw[:, i % NRAW], ACT.Copy).then_inc(hi_done, 1)

        def split_lo(dve, upto):
            while splits_d[0] <= min(upto, len(HALVES) - 1):
                i = splits_d[0]
                splits_d[0] += 1
                dve.wait_ge(hi_done, i + 1)
                dve.tensor_tensor(wlo[:, i % NSPLIT], raw[:, i % NRAW], whi[:, i % NSPLIT].bitcast(F), ALU.subtract)\
                   .then_inc(lo_done, 1)

        def mm3(pe, o, ahi, alo, bhi, blo, start, stop):
            pe.matmul(o, ahi, bhi, start=start, stop=False)
            pe.matmul(o, alo, bhi, start=False, stop=False)
            return pe.matmul(o, ahi, blo, start=False, stop=stop)

        def project(pe, name, acts, part=None, ready={}):
            ch = CH[name]
            for i in range(ch["first"], ch["last"] + 1) if part is None else [ch["first"] + part]:
                pe.wait_ge(lo_done, i + 1)
                s, first, last = i % NSPLIT, i == ch["first"], i == ch["last"]
                for nt, tile in enumerate(ch["tiles"]):
                    if nt in ready:
                        pe.wait_ge(*ready[nt])
                    if first and tile["n"] >= 8:
                        before = TILES[tile["n"] - 8]
                        pe.wait_ge(emptied[before["who"]], before["nth"])
                    kind, t = tile["kind"], tile["t"]
                    bank = PS[:, tile["bank"], :]
                    ahi, alo = acts(kind)
                    if kind == "down":
                        for k in range(2):
                            lhs = slice((t // 2) * P, (t // 2 + 1) * P)
                            w = 2 * k + t % 2
                            mm = mm3(pe, bank, ahi[:, k, lhs], alo[:, k, lhs], whi[:, s, w], wlo[:, s, w], k == 0, k == 1)
                        mm.then_inc(tile_done, 1)
                        continue
                    for k in range(4):
                        kk = k + 4 * (i - ch["first"])
                        st, sp = first and k == 0, last and k == 3
                        if kind in ("tok", "tokc", "y"):
                            lhs = slice(t * P, (t + 1) * P)
                            mm = mm3(pe, bank, ahi[:, kk, lhs], alo[:, kk, lhs], whi[:, s, k], wlo[:, s, k], st, sp)
                        elif kind == "row":
                            mm = mm3(pe, bank, ahi[:, kk], alo[:, kk], whi[:, s, k], wlo[:, s, k], st, sp)
                        else:
                            o = bank[:, 0:CTX] if kind == "featc" else bank
                            cols = slice(t * P, (t + 1) * P)
                            mm = mm3(pe, o, whi[:, s, k, cols], wlo[:, s, k, cols], ahi[:, kk], alo[:, kk], st, sp)
                    if last:
                        mm.then_inc(tile_done, 1)
                if not last:
                    mm.then_inc(used, 1)

        def mine(name, who):
            return [t for t in CH[name]["tiles"] if t["who"] == who]

        def wait_tiles(eng, name):
            for who in "AD":
                own = mine(name, who)
                if own:
                    eng.wait_ge(emptied[who], own[-1]["nth"])

        def build_csel(dve, halves):
            for n, (w, a, b) in enumerate(halves):
                src = csil[:, :, w:w + 1].to_broadcast([P, KD, b - a])
                dch(dve, dve.tensor_copy(csel_hi[:, :, a:b], src))
                dch(dve, dve.tensor_tensor(csel_lo[:, :, a:b], src, csel_hi[:, :, a:b].bitcast(F), ALU.subtract))

        def copy_tiles(eng, who, name, dst, scale=1.0):
            for tile in mine(name, who):
                eng.wait_ge(tile_done, tile["n"] + 1)
                o = dst(tile["kind"], tile["t"])
                src = PS[:, tile["bank"], 0:CTX] if tile["kind"] == "featc" else PS[:, tile["bank"], :]
                if who == "A":
                    eng.activation(o, src, ACT.Copy, scale=scale).then_inc(emptied["A"], 1)
                else:
                    eng.tensor_scalar(o, src, scale, None, ALU.mult).then_inc(emptied["D"], 1)

        xs = at("xs", [P, TT + TC, D], 132)
        mrow = at("mrow", [P, 2 * D], 156)
        brow = at("brow", [P, 2 * D], 164)
        junk = at("junk", [P, D], 172)
        hf = at("hf", [P, 2, TOK], 176)
        modc = at("modc", [P, 2 * KD, 2], 182)
        scale1 = at("scale1", [P, KD, 2], 182.25)
        g1c = at("g1c", [P, KD], 182.5)
        cpy = sem("rpb_padded")
        x_in, ctx_in, consts, c_in, b_in = (esem(n) for n in ("x_in", "ctx_in", "consts", "c_in", "b_in"))
        csil_done, csel_done, mrowT, modc_done = (esem(n) for n in ("csil", "csel", "mrowT", "modc"))
        sq_done, ms_done, pow_done, xn_done, xT, hf_done, hhi_done, hlo_done = (
            esem(n) for n in ("squares", "meansq", "rstd", "xn", "xT", "hf", "h_hi", "h_lo"))
        zero_done = sem("zeros")
        rpb_rep = dram("rpb_rep", [NA_H, GRID, RPB_T])
        LAST1 = CH[("mod", 3)]["last"]

        with nc.Block() as block:
            @block.sync
            def _(sp):
                sp.dma_start(ccol[:, 0, :], c[0].rearrange("(k p) -> p k", p=P), allow_slow_non_contiguous=True).then_inc(c_in, 16)
                sp.dma_start(ccol[:, 1, :], c_ctx.rearrange("(k p) -> p k", p=P), allow_slow_non_contiguous=True).then_inc(c_in, 16)
                load_to(sp, 2)
                sp.dma_start(brow[:, :], bass.AP(tensor=b_mod.tensor, offset=0, ap=[[0, P], [1, 2 * D]])).then_inc(b_in, 16)
                sp.dma_start(g1c[:, :], g_norm1[0].rearrange("(k p) -> p k", p=P), allow_slow_non_contiguous=True).then_inc(b_in, 16)
                sp.dma_start(xs[:, 0:TT, :], x[0].rearrange("(t p) d -> p t d", p=P)).then_inc(x_in, 16)
                load_to(sp, 4)
                sp.dma_start(xs[:, TT:, :], ctx[0].rearrange("(t p) d -> p t d", p=P)).then_inc(ctx_in, 16)
                load_to(sp, LAST1 + 3)

            @block.gpsimd
            def _(pool):
                pool.dma_start(ident[:, :], k_ident).then_inc(consts, 16)
                pool.dma_start(tri[:, :, :], k_tri.rearrange("m p t -> p m t")).then_inc(consts, 16)
                pool.dma_start(namask[:, :], k_mask).then_inc(consts, 16)
                pool.memset(mhalf[:, :], -0.5).then_inc(zero_done, 1)
                pool.dma_start(rpb_rep, bass.AP(tensor=na_rpb.tensor, offset=0, ap=[[RPB_T, NA_H], [0, GRID], [1, RPB_T]]))\
                    .then_inc(cpy, 16)
                pool.wait_ge(zero_done, 1)
                pool.wait_ge(cpy, 16)
                pool.wait_ge(consts, 48)
                pool.wait_ge(ms_done, 1)
                pool.tensor_tensor(rstd[:, 0:TT + TC], ssum[:, 0:TT + TC], mhalf[:, 0:TT + TC], ALU.pow).then_inc(pow_done, 1)

            @block.scalar
            def _(act):
                act.wait_ge(c_in, 32)
                act.activation(csil.rearrange("p k w -> p w k"), ccol, ACT.Silu).then_inc(csil_done, 1)
                split_hi(act, 2)
                act.wait_ge(x_in, 16)
                for t in range(TT + TC):
                    if t == TT:
                        act.wait_ge(ctx_in, 16)
                    ach(act, act.activation(junk[:, :], xs[:, t, :], ACT.Square, accum_out=ssum[:, t:t + 1]))
                    if t % 3 == 1:
                        split_hi(act, 3 + t // 3)
                act.copy(tiny[:, 67:68], ssum[:, 0:1]).then_inc(sq_done, 1)
                split_hi(act, LAST1 + 2)
                for k in range(KD):
                    act.wait_ge(hf_done, k + 1)
                    act.activation(hT_hi[:, k, :], hf[:, k % 2, 0:SEQ], ACT.Copy).then_inc(hhi_done, 1)
                    act.activation(hc_hi[:, k, :], hf[:, k % 2, SEQ:], ACT.Copy).then_inc(hhi_done, 1)
                split_hi(act, LAST1 + 2)

            @block.vector
            def _(dve):
                dve.wait_ge(csil_done, 1)
                build_csel(dve, [(0, 0, 64), (1, 64, P)])
                dve.tensor_copy(tiny[:, 66:67], csil[:, 0, 0:1]).then_inc(csel_done, 1)
                for j in range(4):
                    split_lo(dve, 2 * j + 2)
                    if j == 0:
                        dve.wait_ge(b_in, 32)
                    tile = CH[("mod", j)]["tiles"][0]
                    dve.wait_ge(tile_done, tile["n"] + 1)
                    cols = slice(512 * j, 512 * j + 512)
                    dve.tensor_tensor(mrow[:, cols], PS[:, tile["bank"], :], brow[:, cols], ALU.add).then_inc(emptied["D"], 1)
                    if j == 1:
                        dve.wait_ge(sq_done, 1)
                        dve.tensor_scalar(ssum[:, 0:TT + TC], ssum[:, 0:TT + TC], 1.0 / D, EPS, ALU.mult, ALU.add).then_inc(ms_done, 1)
                    if j >= 2:
                        dve.wait_ge(pow_done, 1)
                        for t in range(3 * (j - 2), 3 * (j - 1)):
                            dve.tensor_scalar(xs[:, t, :], xs[:, t, :], rstd[:, t:t + 1], None, ALU.mult).then_inc(xn_done, 1)
                dve.wait_ge(mrowT, 1)
                dch(dve, dve.tensor_copy(modc[:, :, :].rearrange("p (b k) w -> p b k w", b=4),
                                         PS[:, 4:8, :].rearrange("p b (k t) -> p b k t", t=P)[:, :, :, 0:P:64]))
                dve.tensor_scalar(scale1[:, :, :], modc[:, KD:, :], 1.0, None, ALU.add).then_inc(modc_done, 1)
                dve.wait_ge(modc_done, 1)
                dch(dve, dve.tensor_tensor(scale1[:, :, :], scale1[:, :, :],
                                           g1c[:, :, None].to_broadcast([P, KD, 2]), ALU.mult))
                def modulate(k):
                    dve.wait_ge(xT, k + 1)
                    if k >= 2:
                        dve.wait_ge(hhi_done, 2 * k - 2)
                        dve.wait_ge(hlo_done, 2 * k - 2)
                    b = 4 * (k % 2)
                    dve.tensor_scalar(hf[:, k % 2, 0:SEQ], PS[:, b, :], scale1[:, k, 0:1], modc[:, k, 0:1], ALU.mult, ALU.add)
                    dve.tensor_scalar(hf[:, k % 2, SEQ:], PS[:, b + 1, 0:CTX], scale1[:, k, 1:2], modc[:, k, 1:2], ALU.mult, ALU.add)\
                       .then_inc(hf_done, 1)

                modulate(0)
                for k in range(KD):
                    if k + 1 < KD:
                        modulate(k + 1)
                    dve.wait_ge(hf_done, k + 1)
                    dve.wait_ge(hhi_done, 2 * k + 2)
                    dve.tensor_tensor(hT_lo[:, k, :], hf[:, k % 2, 0:SEQ], hT_hi[:, k, :].bitcast(F), ALU.subtract).then_inc(hlo_done, 1)
                    dve.tensor_tensor(hc_lo[:, k, :], hf[:, k % 2, SEQ:], hc_hi[:, k, :].bitcast(F), ALU.subtract).then_inc(hlo_done, 1)
                split_lo(dve, LAST1 + 2)

            @block.tensor
            def _(pe):
                pe.wait_ge(csel_done, 1)
                for j in range(4):
                    project(pe, ("mod", j), lambda kind: (csel_hi, csel_lo))
                pe.wait_ge(consts, 48)
                pe.wait_ge(emptied["D"], 4)
                for m in range(2 * KD):
                    mm = pe.transpose(PS[:, 4 + m // 4, (m % 4) * P:(m % 4 + 1) * P], mrow[:, m * P:(m + 1) * P], ident[:, :])
                mm.then_inc(mrowT, 1)
                pe.wait_ge(xn_done, TT + TC)
                pe.wait_ge(modc_done, 1)
                for k in range(KD):
                    b = 4 * (k % 2)
                    if k >= 2:
                        pe.wait_ge(hf_done, k - 1)
                    for t in range(TT + TC):
                        o = PS[:, b + t // TT, (t % TT) * P:(t % TT + 1) * P]
                        mm = pe.transpose(o, xs[:, t, k * P:(k + 1) * P], ident[:, :])
                    mm.then_inc(xT, 1)

        def acts(kind):
            return (hc_hi, hc_lo) if kind in ("featc", "tokc") else (hT_hi, hT_lo)

        kna_hi = at("kna_hi", [P, 4, TOK], 132, R)
        kna_lo = at("kna_lo", [P, 4, TOK], 189.5, R)
        vna = at("vna", [P, TT + TC, 512], 144)
        qna_hi = at("qna_hi", [P, 4, SEQ], 156, R)
        qna_lo = at("qna_lo", [P, 4, SEQ], 116, R)
        prob = at("prob", [P, 3, TOK], 164)
        probT = at("probT", [P, 2, TOK], 173)
        braw = at("braw", [P, 14, GRID], 179)
        bias = at("bias", [P, 2, 14, GRID], 182.5)
        NI = NA_H * TT
        bias_in, bias_done, scores, scores_read, smax = (esem(n) for n in ("bias_in", "bias", "scores", "scores_read", "smax"))
        exped, probT_done, pT_a, pv_done, ona_done = (esem(n) for n in ("exped", "probT", "pT_act", "pv", "ona"))
        qk_hi, normed, bias_clear, ctx_read = (esem(n) for n in ("qk_hi", "normed", "bias_clear", "ctx_read"))
        turned, turn_hi, turn_lo = sem("turned"), sem("turn_hi"), sem("turn_lo")
        nturn = [0, 0, 0]

        def turn(pe, src, n_tiles, banks):
            for m in range(n_tiles):
                i = nturn[0]
                nturn[0] += 1
                if m >= len(banks):
                    pe.wait_ge(turn_lo, i - len(banks) + 1)
                for t in range(TT):
                    mm = pe.transpose(PS[:, banks[m % len(banks)], t * P:(t + 1) * P], src(t, m), ident[:, :])
                mm.then_inc(turned, 1)

        def turn_out_hi(act, dst, n_tiles, banks):
            for m in range(n_tiles):
                nturn[1] += 1
                act.wait_ge(turned, nturn[1])
                act.activation(dst[:, m, :], PS[:, banks[m % len(banks)], :], ACT.Copy).then_inc(turn_hi, 1)

        def turn_out_lo(dve, dst, hi, n_tiles, banks):
            for m in range(n_tiles):
                nturn[2] += 1
                dve.wait_ge(turn_hi, nturn[2])
                dve.tensor_tensor(dst[:, m, :], PS[:, banks[m % len(banks)], :], hi[:, m, :].bitcast(F), ALU.subtract)\
                   .then_inc(turn_lo, 1)

        def tile_hi(act, name, hi):
            for tile in CH[name]["tiles"]:
                act.wait_ge(tile_done, tile["n"] + 1)
                ctx_part = tile["kind"] == "featc"
                cols = slice(SEQ, TOK) if ctx_part else slice(0, SEQ)
                act.activation(hi[:, tile["t"], cols], PS[:, tile["bank"], 0:CTX] if ctx_part else PS[:, tile["bank"], :], ACT.Copy)\
                   .then_inc(qk_hi, 1)

        def tile_lo(dve, name, hi, lo, before):
            for n, tile in enumerate(CH[name]["tiles"]):
                dve.wait_ge(qk_hi, before + n + 1)
                ctx_part = tile["kind"] == "featc"
                cols = slice(SEQ, TOK) if ctx_part else slice(0, SEQ)
                dve.tensor_tensor(lo[:, tile["t"], cols], PS[:, tile["bank"], 0:CTX] if ctx_part else PS[:, tile["bank"], :],
                                  hi[:, tile["t"], cols].bitcast(F), ALU.subtract).then_inc(emptied["D"], 1)

        def vna_at(kind, t):
            return vna[:, TT + t, :] if kind == "tokc" else vna[:, t, :]

        na_names = [("k_na",), ("v_na",), ("q_na",)]
        LAST2 = CH[("q_na",)]["last"]
        with nc.Block() as block:
            @block.sync
            def _(sp):
                for h in range(NA_H):
                    if h:
                        sp.wait_ge(bias_done, h)
                    off = h * GRID * RPB_T + WIN_C - 1
                    for half in range(2):
                        sp.dma_start(braw[64 * half:64 * half + 64],
                                     bass.AP(tensor=rpb_rep.tensor, offset=off + (1 - half) * RPB_C,
                                             ap=[[RPB_T - 1, GRID], [RPB_C, 14], [1, GRID]])).then_inc(bias_in, 16)
                    if h == 0:
                        load_to(sp, LAST2 + 3)

            @block.gpsimd
            def _(pool):
                for h in range(NA_H):
                    if h >= 2:
                        pool.wait_ge(smax, (h - 1) * TT)
                    pool.memset(bias[:, h % 2], NEG).then_inc(bias_clear, 1)

            @block.scalar
            def _(act):
                split_hi(act, CH[("k_na",)]["last"] + 1)
                tile_hi(act, ("k_na",), kna_hi)
                split_hi(act, CH[("k_na",)]["last"] + 2)
                split_hi(act, CH[("v_na",)]["last"] + 1)
                copy_tiles(act, "A", ("v_na",), vna_at)
                split_hi(act, CH[("v_na",)]["last"] + 2)
                split_hi(act, CH[("q_na",)]["last"] + 1)
                tile_hi(act, ("q_na",), qna_hi)
                split_hi(act, CH[("q_na",)]["last"] + 2)
                def ctx_scores(i):
                    act.wait_ge(scores, i + 1)
                    if i >= 3:
                        act.wait_ge(probT_done, i - 2)
                    act.activation(prob[:, i % 3, SEQ:], PS[:, 2 + 5 * (i % 2), 0:CTX], ACT.Copy, scale=NA_D ** -0.5).then_inc(ctx_read, 1)

                ctx_scores(0)
                for i in range(NI + 1):
                    if i < NI:
                        act.wait_ge(smax, i + 1)
                        act.activation(prob[:, i % 3, :], prob[:, i % 3, :], ACT.Exp, bias=nmax[:, i:i + 1],
                                       accum_out=rsum[:, i:i + 1]).then_inc(exped, 1)
                    if i + 1 < NI:
                        ctx_scores(i + 1)
                    if i >= 1:
                        j = i - 1
                        act.wait_ge(probT_done, j + 1)
                        if j >= 2:
                            act.wait_ge(pv_done, j - 1)
                        act.activation(probT[:, j % 2, 0:512], PS[:, 3, :], ACT.Copy).then_inc(pT_a, 1)
                        act.activation(probT[:, j % 2, 512:], PS[:, 4, 0:CTX], ACT.Copy).then_inc(pT_a, 1)

            @block.vector
            def _(dve):
                split_lo(dve, CH[("k_na",)]["last"] + 1)
                tile_lo(dve, ("k_na",), kna_hi, kna_lo, 0)
                split_lo(dve, CH[("k_na",)]["last"] + 2)
                split_lo(dve, CH[("v_na",)]["last"] + 1)
                copy_tiles(dve, "D", ("v_na",), vna_at)
                split_lo(dve, CH[("v_na",)]["last"] + 2)
                split_lo(dve, CH[("q_na",)]["last"] + 1)
                tile_lo(dve, ("q_na",), qna_hi, qna_lo, len(CH[("k_na",)]["tiles"]))
                split_lo(dve, CH[("q_na",)]["last"] + 2)
                for i in range(NI + 3):
                    if i < NI:
                        h, qt = divmod(i, TT)
                        if qt == 0:
                            dve.wait_ge(bias_in, 32 * (h + 1))
                            dve.wait_ge(bias_clear, h + 1)
                            dve.copy_predicated(bias[:, h % 2], namask[:, None, :].to_broadcast([P, 14, GRID]), braw[:, :, :])\
                               .then_inc(bias_done, 1)
                            dve.wait_ge(bias_done, h + 1)
                        dve.wait_ge(scores, i + 1)
                        if i >= 3:
                            dve.wait_ge(probT_done, i - 2)
                        dve.scalar_tensor_tensor(out=prob[:, i % 3, 0:512].rearrange("p (j k) -> p j k", k=GRID),
                                                 in0=PS[:, i % 2, :].rearrange("p (j k) -> p j k", k=GRID),
                                                 scalar=NA_D ** -0.5,
                                                 in1=bias[:, h % 2, 6 - 2 * qt:14 - 2 * qt, :],
                                                 op0=ALU.mult, op1=ALU.add).then_inc(scores_read, 1)
                        dve.wait_ge(scores_read, i + 1)
                        dve.wait_ge(ctx_read, i + 1)
                        dve.tensor_reduce(nmax[:, i:i + 1], prob[:, i % 3, :], AX.X, ALU.max, negate=True).then_inc(smax, 1)
                    if 1 <= i <= NI:
                        j = i - 1
                        dve.wait_ge(exped, j + 1)
                        dch(dve, dve.reciprocal(rinv[:, j:j + 1], rsum[:, j:j + 1]))
                        dve.tensor_scalar(prob[:, j % 3, :], prob[:, j % 3, :], rinv[:, j:j + 1], None, ALU.mult).then_inc(normed, 1)
                    if i >= 3:
                        j = i - 3
                        h, qt = divmod(j, TT)
                        rows = slice(64 * (h % 2), 64 * (h % 2) + 64)
                        dve.wait_ge(pv_done, j + 1)
                        dve.tensor_copy(onaT[rows, h // 2, qt * P:(qt + 1) * P], PS[0:64, 5 + j % 2, 0:P]).then_inc(ona_done, 1)

            @block.tensor
            def _(pe):
                for name in na_names:
                    project(pe, name, acts)
                for name in na_names:
                    wait_tiles(pe, name)

                def score(i):
                    h, qt = divmod(i, TT)
                    rows = slice(64 * (h % 2), 64 * (h % 2) + 64)
                    if i >= 2:
                        pe.wait_ge(scores_read, i - 1)
                        pe.wait_ge(ctx_read, i - 1)
                    qhi, qlo = (q[rows, h // 2, qt * P:(qt + 1) * P] for q in (qna_hi, qna_lo))
                    mm3(pe, PS[:, i % 2, :], qhi, qlo, kna_hi[rows, h // 2, 0:SEQ], kna_lo[rows, h // 2, 0:SEQ], True, True)
                    mm3(pe, PS[:, 2 + 5 * (i % 2), 0:CTX], qhi, qlo, kna_hi[rows, h // 2, SEQ:], kna_lo[rows, h // 2, SEQ:], True, True)\
                      .then_inc(scores, 1)

                def values(j):
                    h = j // TT
                    pe.wait_ge(pT_a, 2 * j + 2)
                    if j >= 2:
                        pe.wait_ge(ona_done, j - 1)
                    for t in range(TT + TC):
                        mm = pe.matmul(PS[0:NA_D, 5 + j % 2, 0:P], vna[:, t, h * NA_D:(h + 1) * NA_D],
                                       probT[:, j % 2, t * P:(t + 1) * P], start=(t == 0), stop=(t == TT + TC - 1))
                    mm.then_inc(pv_done, 1)

                def turn_probs(j):
                    pe.wait_ge(normed, j + 1)
                    if j:
                        pe.wait_ge(pT_a, 2 * j)
                    for t in range(TT + TC):
                        mm = pe.transpose(PS[:, 3 + t // 4, (t % 4) * P:(t % 4 + 1) * P],
                                          prob[:, j % 3, t * P:(t + 1) * P], ident[:, :])
                    mm.then_inc(probT_done, 1)

                score(0)
                for i in range(NI + 2):
                    if i + 1 < NI:
                        score(i + 1)
                    if 1 <= i <= NI:
                        turn_probs(i - 1)
                    if i >= 2:
                        values(i - 2)

        if dump == "na":
            return finish(nc, out, es, sem, onaT)

        kgl = at("kgl", [P, GL_H, TOK], 132)
        vgl = at("vgl", [P, TT + TC, D], 144)
        qgl = at("qgl", [P, GL_H, SEQ], 168)
        lrT = at("lrT", [64, TOK], 176)
        ogl = at("ogl", [P, TT, D], 189)
        wgp = at("wgp", [P, KD, P], 189)
        wg_hi = at("wg_hi", [P, KD, P], 193, R)
        wg_lo = at("wg_lo", [P, KD, P], 197, R)
        wgr = at("wgr", [P, KD, 2 * RANK], 201)
        w2 = at("w2", [64, 512], 179)
        gate_in, w2_in, wgp_done, wg_done, lr_done, lr_out = (esem(n) for n in ("gate_in", "w2_in", "wgp", "wg", "lr", "lr_out"))
        gl_names = [("k_gla",), ("v_gla", 0), ("v_gla", 1), ("q_gla",)]
        LAST3 = CH[("q_gla",)]["last"]
        LR_BANKS = [(CH[("q_gla",)]["tiles"][0]["n"] + 4 + b) % 8 for b in range(2)]

        def kgl_at(kind, m):
            return kgl[:, m, SEQ:] if kind == "featc" else kgl[:, m, 0:SEQ]

        def vgl_at(j):
            return lambda kind, t: vgl[:, (TT if kind == "tokc" else 0) + t, 512 * j:512 * j + 512]

        gl_dst = [kgl_at, vgl_at(0), vgl_at(1), lambda kind, m: qgl[:, m, :]]
        with nc.Block() as block:
            @block.sync
            def _(sp):
                sp.dma_start(wgr[:, :, :], w_in[0].rearrange("(k p) n -> p k n", p=P)[:, :, GATE:GATE + 2 * RANK]).then_inc(gate_in, 16)
                for d in range(2):
                    sp.dma_start(w2[32 * d:32 * d + RANK, :], gla_gate_w[0, d]).then_inc(w2_in, 16)
                    sp.dma_start(w2[32 * d + RANK:32 * d + RANK + 1, :], gla_gate_b[:, d, :]).then_inc(w2_in, 16)
                sp.wait_ge(w2_in, 64)
                load_to(sp, LAST3 + 3)

            @block.scalar
            def _(act):
                act.wait_ge(wgp_done, 4)
                act.activation(wg_hi[:, :, :], wgp[:, :, :], ACT.Copy).then_inc(wg_done, 1)
                for name, dst in zip(gl_names, gl_dst):
                    split_hi(act, CH[name]["last"] + 1)
                    copy_tiles(act, "A", name, dst, GL_DK ** -0.5 if name == ("q_gla",) else 1.0)
                    split_hi(act, CH[name]["last"] + 2)

            @block.vector
            def _(dve):
                dch(dve, dve.memset(wgp[:, :, :], 0.0))
                dve.memset(lrT[:, :], 1.0).then_inc(wgp_done, 1)
                dve.wait_ge(gate_in, 16)
                for d in range(2):
                    dve.tensor_copy(wgp[:, :, 32 * d:32 * d + RANK], wgr[:, :, RANK * d:RANK * d + RANK]).then_inc(wgp_done, 1)
                dve.wait_ge(wgp_done, 3)
                dve.tensor_copy(tiny[:, 0:1], wgp[:, 0, 0:1]).then_inc(wgp_done, 1)
                dve.wait_ge(wg_done, 1)
                dve.tensor_tensor(wg_lo[:, :, :], wgp[:, :, :], wg_hi[:, :, :].bitcast(F), ALU.subtract).then_inc(wg_done, 1)
                for name, dst in zip(gl_names, gl_dst):
                    split_lo(dve, CH[name]["last"] + 1)
                    copy_tiles(dve, "D", name, dst, GL_DK ** -0.5 if name == ("q_gla",) else 1.0)
                    split_lo(dve, CH[name]["last"] + 2)
                dve.wait_ge(lr_done, 1)
                for d in range(2):
                    rows = slice(32 * d, 32 * d + RANK)
                    dve.tensor_copy(lrT[rows, 0:SEQ], PS[rows, LR_BANKS[0], :]).then_inc(lr_out, 1)
                    dve.tensor_copy(lrT[rows, SEQ:], PS[rows, LR_BANKS[1], 0:CTX]).then_inc(lr_out, 1)

            @block.tensor
            def _(pe):
                for name in gl_names:
                    project(pe, name, acts)
                for name in gl_names[:-1]:
                    wait_tiles(pe, name)
                pe.wait_ge(wg_done, 2)
                for b, (hi, lo, n) in enumerate(((hT_hi, hT_lo, SEQ), (hc_hi, hc_lo, CTX))):
                    for k in range(KD):
                        mm = mm3(pe, PS[:, LR_BANKS[b], 0:n], wg_hi[:, k], wg_lo[:, k], hi[:, k], lo[:, k], k == 0, k == KD - 1)
                mm.then_inc(lr_done, 1)

        state = at("state", [P, 2, GL_H, GL_DV], 100)
        smid = at("smid", [P, GL_H, GL_DV], 108)
        eq = at("eq", [P, 2, GL_H, P], 112)
        ek = at("ek", [P, 2, GL_H, P], 116)
        rowbuf = at("rowbuf", [1, 2, 512], 120)
        lgate = at("lgate", [P, 512], 181)
        tneg = at("tneg", [P, 512], 183)
        attn = at("attn", [P, GL_H, P], 185)
        kdec = at("kdec", [P, GL_H, P], 187)
        edges = tiny[:, 0:24].rearrange("p (w h e) -> p w h e", w=2, e=3)
        one = tiny[:, 24:25]
        (logit_done, absd, expd, lnd, gdone, cumd, dsub, kexp, kfd, qfd, smidd, kT_done, kT_out, atd, atm, od, oout, ud, sdone) = (
            esem("gl_" + n) for n in "logit abs exp ln gate cum diff decays kf qf smid kT kT_out attn attn_out o o_out update state".split())
        units = []
        order = {0: [("c", 0), ("c", 1)] + [("l", t) for t in range(TT)],
                 1: [("c", 1), ("c", 0)] + [("l", TT - 1 - t) for t in range(TT)]}
        seen = set()
        for j in range(TC + TT):
            for d in range(2):
                kind, t = order[d][j]
                lat = kind == "l"
                units.append(dict(d=d, j=j, lat=lat, t=t, tok=(0 if lat else SEQ) + t * P, vt=t if lat else TT + t,
                                  add=lat and t in seen, last=j == TC + TT - 1, nlat=sum(u["lat"] for u in units),
                                  nup=sum(not u["last"] for u in units)))
                if lat:
                    seen.add(t)
        NU = len(units)
        rows_dram = dram("rows_dram", [1, NROW * 512])
        row_out = [sem(f"row_out{i}") for i in range(2)]
        bias_row = [esem(f"bias_row{i}") for i in range(2)]
        row_halves = [(j, part) for j in range(NROW) for part in range(2)]
        n_early = len(row_halves) - NU
        early_burst = row_halves[:n_early]
        bursts = [[row_halves[n_early + u]] for u in range(NU)]

        def row_half(j, part):
            return CH[("row", j)]["first"] + part

        with nc.Block() as block:
            @block.sync
            def _(sp):
                for j in range(NROW):
                    if j >= 2:
                        sp.wait_ge(row_out[j % 2], 16 * (j // 2))
                    sp.dma_start(rowbuf[0:1, j % 2, :], bass.AP(tensor=b_mod.tensor, offset=2 * D + 512 * j, ap=[[0, 1], [1, 512]]))\
                      .then_inc(bias_row[j % 2], 16)
                    load_to(sp, row_half(j, 1) + 3)
                    sp.wait_ge(emptied["D"], CH[("row", j)]["tiles"][0]["nth"])
                    sp.dma_start(rows_dram[0:1, 512 * j:512 * j + 512], rowbuf[0:1, j % 2, :]).then_inc(row_out[j % 2], 16)
                for w in row_out:
                    sp.wait_ge(w, 16 * NROW // 2)

            @block.scalar
            def _(act):
                def gate_logs(u):
                    act.wait_ge(logit_done, u + 1)
                    if u:
                        act.wait_ge(gdone, u)
                    act.activation(tneg[:, :], PS[:, 0, :], ACT.Abs).then_inc(absd, 1)
                    act.wait_ge(absd, u + 2)
                    act.activation(tneg[:, :], tneg[:, :], ACT.Exp, scale=-1.0).then_inc(expd, 1)
                    act.wait_ge(expd, u + 1)
                    act.activation(tneg[:, :], tneg[:, :], ACT.Ln, bias=one).then_inc(lnd, 1)

                def decays(u):
                    d = units[u]["d"]
                    act.wait_ge(dsub, u + 1)
                    act.activation(ek[:, u % 2], eq[:, u % 2], ACT.Exp, scale=-1.0 / TAU).then_inc(kexp, 1)
                    act.wait_ge(kexp, 3 * u + 1)
                    act.activation(eq[:, u % 2], eq[:, u % 2], ACT.Exp, scale=1.0 / TAU).then_inc(kexp, 1)
                    act.activation(edges[:, d], edges[:, d], ACT.Exp, scale=1.0 / TAU).then_inc(kexp, 1)

                act.wait_ge(absd, 1)
                gate_logs(0)
                split_hi(act, row_half(*early_burst[2]))
                decays(0)
                gate_logs(1)
                split_hi(act, row_half(*bursts[0][0]))
                for u, un in enumerate(units):
                    if not un["last"]:
                        act.wait_ge(kT_done, un["nup"] + 1)
                        if un["nup"]:
                            act.wait_ge(ud, un["nup"])
                        act.activation(kdec[:, :, :], PS[:, 3, :], ACT.Copy).then_inc(kT_out, 1)
                    if u + 1 < NU:
                        decays(u + 1)
                    if u + 2 < NU:
                        gate_logs(u + 2)
                    for j, part in bursts[min(u + 1, NU - 1)]:
                        split_hi(act, row_half(j, part))
                split_hi(act, row_half(NROW - 1, 1) + 2)

            @block.vector
            def _(dve):
                def gates(u):
                    if u:
                        dve.wait_ge(cumd, u)
                    dve.wait_ge(lnd, u + 1)
                    dve.scalar_tensor_tensor(out=lgate[:, :], in0=PS[:, 0, :], scalar=0.0, in1=tneg[:, :],
                                             op0=ALU.min, op1=ALU.subtract).then_inc(gdone, 1)

                def differences(u):
                    un = units[u]
                    d = un["d"]
                    dve.wait_ge(cumd, u + 1)
                    cum = PS[:, 1, :].rearrange("p (h t) -> p h t", h=GL_H)
                    mid, last = (63, P - 1) if d == 0 else (64, 0)
                    dve.tensor_copy(edges[:, d, :, 0:1], cum[:, :, mid:mid + 1])
                    dch(dve, dve.tensor_copy(edges[:, d, :, 1:2], cum[:, :, last:last + 1]))
                    dch(dve, dve.tensor_tensor(edges[:, d, :, 2:3], edges[:, d, :, 1:2], edges[:, d, :, 0:1], ALU.subtract))
                    if u >= 2:
                        dve.wait_ge(kT_done, units[u - 1]["nup"])
                        if units[u - 1]["nlat"]:
                            dve.wait_ge(od, units[u - 1]["nlat"])
                    dve.tensor_tensor(eq[:, u % 2], cum, edges[:, d, :, 0:1].to_broadcast([P, GL_H, P]), ALU.subtract).then_inc(dsub, 1)

                def factors(u):
                    un = units[u]
                    dve.wait_ge(kexp, 3 * u + 3)
                    dve.tensor_tensor(ek[:, u % 2], kgl[:, :, un["tok"]:un["tok"] + P], ek[:, u % 2], ALU.mult).then_inc(kfd, 1)
                    if un["lat"]:
                        dve.tensor_tensor(eq[:, u % 2], qgl[:, :, un["tok"]:un["tok"] + P], eq[:, u % 2], ALU.mult).then_inc(qfd, 1)

                def row_copy(halves):
                    for j, part in halves:
                        if part == 1:
                            tile = CH[("row", j)]["tiles"][0]
                            dve.wait_ge(tile_done, tile["n"] + 1)
                            dve.wait_ge(bias_row[j % 2], 16 * (j // 2 + 1))
                            dve.tensor_tensor(rowbuf[0:1, j % 2, :], PS[0:1, tile["bank"], :], rowbuf[0:1, j % 2, :], ALU.add)\
                               .then_inc(emptied["D"], 1)

                dve.memset(one, 1.0).then_inc(absd, 1)
                gates(0)
                split_lo(dve, row_half(*early_burst[1]))
                differences(0)
                row_copy(early_burst[:2])
                split_lo(dve, row_half(*early_burst[2]))
                factors(0)
                gates(1)
                split_lo(dve, row_half(*early_burst[3]))
                for u, un in enumerate(units):
                    d, t = un["d"], un["t"]
                    if un["lat"]:
                        if un["nlat"]:
                            dve.wait_ge(od, un["nlat"])
                        dve.tensor_tensor(smid[:, :, :], state[:, d], edges[:, d, :, 0:1].to_broadcast([P, GL_H, GL_DV]), ALU.mult)\
                           .then_inc(smidd, 1)
                        dve.wait_ge(atd, un["nlat"] + 1)
                        dve.tensor_tensor(attn[:, :, :], PS[:, 0, :].rearrange("p (h t) -> p h t", h=GL_H),
                                          tri[:, d:d + 1, :].to_broadcast([P, GL_H, P]), ALU.mult).then_inc(atm, 1)
                    row_copy(bursts[u - 1] if u else early_burst[2:])
                    if u + 1 < NU:
                        differences(u + 1)
                    for j, part in bursts[u]:
                        split_lo(dve, row_half(j, part))
                    if u + 1 < NU:
                        factors(u + 1)
                    if un["lat"]:
                        dve.wait_ge(od, un["nlat"] + 1)
                        o = PS[:, 4:6, :].rearrange("p b n -> p (b n)")
                        if un["add"]:
                            dve.tensor_tensor(ogl[:, t, :], ogl[:, t, :], o, ALU.add).then_inc(oout, 1)
                        else:
                            dve.tensor_copy(ogl[:, t, :], o).then_inc(oout, 1)
                        dve.wait_ge(oout, un["nlat"] + 1)
                    if u + 2 < NU:
                        gates(u + 2)
                    if not un["last"]:
                        if un["j"]:
                            dch(dve, dve.tensor_tensor(state[:, d], state[:, d],
                                                       edges[:, d, :, 1:2].to_broadcast([P, GL_H, GL_DV]), ALU.mult))
                        dve.wait_ge(ud, un["nup"] + 1)
                        for h in range(GL_H):
                            upd = PS[:, 6 + h // 2, (h % 2) * GL_DV:(h % 2 + 1) * GL_DV]
                            if un["j"]:
                                ins = dve.scalar_tensor_tensor(out=state[:, d, h], in0=upd, scalar=edges[:, d, h, 2:3],
                                                               in1=state[:, d, h], op0=ALU.mult, op1=ALU.add)
                            else:
                                ins = dve.tensor_scalar(state[:, d, h], upd, edges[:, d, h, 2:3], None, ALU.mult)
                        ins.then_inc(sdone, 1)
                        dve.wait_ge(sdone, un["nup"] + 1)
                row_copy(bursts[NU - 1])
                split_lo(dve, row_half(NROW - 1, 1) + 2)

            @block.tensor
            def _(pe):
                def logits(u):
                    un = units[u]
                    d, rows = un["d"], slice(32 * un["d"], 32 * un["d"] + RANK + 1)
                    if u:
                        pe.wait_ge(gdone, u)
                    pe.matmul(PS[:, 0, :], lrT[rows, un["tok"]:un["tok"] + P], w2[rows, :], start=True, stop=True).then_inc(logit_done, 1)

                def sums(u):
                    pe.wait_ge(gdone, u + 1)
                    if u:
                        pe.wait_ge(dsub, u)
                    for h in range(GL_H):
                        mm = pe.matmul(PS[:, 1, h * P:(h + 1) * P], lgate[:, h * P:(h + 1) * P], tri[:, units[u]["d"], :], start=True, stop=True)
                    mm.then_inc(cumd, 1)

                def burst(halves):
                    for j, part in halves:
                        if part == 0 and j:
                            pe.wait_ge(emptied["D"], CH[("row", j - 1)]["tiles"][0]["nth"])
                        project(pe, ("row", j), lambda kind: (csel_hi, csel_lo), part=part)

                logits(0)
                burst(early_burst[:2])
                sums(0)
                logits(1)
                burst(early_burst[2:])
                for u, un in enumerate(units):
                    pe.wait_ge(kfd, u + 1)
                    if not un["last"]:
                        if un["nup"]:
                            pe.wait_ge(kT_out, un["nup"])
                        for h in range(GL_H):
                            mm = pe.transpose(PS[:, 3, h * P:(h + 1) * P], ek[:, u % 2, h, :], ident[:, :])
                        mm.then_inc(kT_done, 1)
                    if un["lat"]:
                        pe.wait_ge(qfd, un["nlat"] + 1)
                        pe.wait_ge(gdone, min(u + 2, NU))
                        for h in range(GL_H):
                            mm = pe.matmul(PS[:, 0, h * P:(h + 1) * P], ek[:, u % 2, h, :], eq[:, u % 2, h, :], start=True, stop=True)
                        mm.then_inc(atd, 1)
                    if u + 1 < NU:
                        sums(u + 1)
                    if un["lat"]:
                        pe.wait_ge(atm, un["nlat"] + 1)
                    if u + 2 < NU:
                        logits(u + 2)
                    if un["lat"]:
                        pe.wait_ge(smidd, un["nlat"] + 1)
                        if un["nlat"]:
                            pe.wait_ge(oout, un["nlat"])
                        for h in range(GL_H):
                            o = PS[:, 4 + h // 2, (h % 2) * GL_DV:(h % 2 + 1) * GL_DV]
                            pe.matmul(o, attn[:, h, :], vgl[:, un["vt"], h * GL_DV:(h + 1) * GL_DV], start=True, stop=False)
                            mm = pe.matmul(o, eq[:, u % 2, h, :], smid[:, h, :], start=False, stop=True)
                        mm.then_inc(od, 1)
                    if not un["last"]:
                        pe.wait_ge(kT_out, un["nup"] + 1)
                        if un["nup"]:
                            pe.wait_ge(sdone, un["nup"])
                        for h in range(GL_H):
                            mm = pe.matmul(PS[:, 6 + h // 2, (h % 2) * GL_DV:(h % 2 + 1) * GL_DV], kdec[:, h, :],
                                           vgl[:, un["vt"], h * GL_DV:(h + 1) * GL_DV], start=True, stop=True)
                        mm.then_inc(ud, 1)
                    burst(bursts[u])

        if dump == "gla":
            return finish(nc, out, es, sem, ogl)

        oglT_hi = at("oglT_hi", [P, KD, SEQ], 132, R)
        oglT_lo = at("oglT_lo", [P, KD, SEQ], 148, R)
        oscT_hi = at("oscT_hi", [P, 4, SEQ], 100, R)
        oscT_lo = at("oscT_lo", [P, 4, SEQ], 108, R)
        cT = at("cT", [P, 4, SEQ], 164)
        uT = at("uT", [P, 4, SEQ + 2], 172)
        sr = at("sr", [P, 2, 512], 181)
        gnr = at("gnr", [P, GL_DV], 185)
        jk = at("jk", [P, GL_DV], 186)
        bsc = sr
        gn_in, cw_in, osq, oms, opow, onrm, srm, u0, bsd, bhi, ona_hi = (
            esem(n) for n in "gn_in cw_in o_squares o_ms o_rstd o_normed gated u_edges b_times sc_hi ona_hi".split())
        LAST5 = CH[("b",)]["last"]
        OG_BANKS = [tile["bank"] for tile in CH[("c",)]["tiles"]]
        with nc.Block() as block:
            @block.sync
            def _(sp):
                sp.dma_start(gnr[:, :], bass.AP(tensor=gla_norm_g.tensor, offset=0, ap=[[0, P], [1, GL_DV]])).then_inc(gn_in, 16)
                for w in range(3):
                    sp.dma_start(convw[:, w, :], conv_w[0, w].rearrange("(m p) -> p m", p=P), allow_slow_non_contiguous=True)\
                      .then_inc(cw_in, 16)
                load_to(sp, LAST5 + 3)

            @block.gpsimd
            def _(pool):
                pool.wait_ge(oms, 1)
                pool.tensor_tensor(rstd[:, 0:16], ssum[:, 0:16], mhalf[:, 0:16], ALU.pow).then_inc(opow, 1)

            @block.scalar
            def _(act):
                act.activation(onaT_hi[:, :, :], onaT[:, :, :], ACT.Copy).then_inc(ona_hi, 1)
                for t in range(TT):
                    for h in range(GL_H):
                        ach(act, act.activation(jk[:, :], ogl[:, t, h * GL_DV:(h + 1) * GL_DV], ACT.Square,
                                                accum_out=ssum[:, GL_H * t + h:GL_H * t + h + 1]))
                act.copy(tiny[:, 67:68], ssum[:, 0:1]).then_inc(osq, 1)
                for j in range(2):
                    split_hi(act, CH[("r", j)]["last"] + 2)
                    for tile in CH[("r", j)]["tiles"]:
                        act.wait_ge(tile_done, tile["n"] + 1)
                        n = TT * j + tile["t"]
                        if n >= 2:
                            act.wait_ge(srm, n - 1)
                        act.activation(sr[:, n % 2, :], PS[:, tile["bank"], :], ACT.Silu).then_inc(emptied["A"], 1)
                split_hi(act, CH[("c",)]["last"] + 2)
                copy_tiles(act, "A", ("c",), lambda kind, m: cT[:, m, :])
                split_hi(act, CH[("x",)]["last"] + 2)
                turn_out_hi(act, oglT_hi, KD, OG_BANKS)
                split_hi(act, CH[("b",)]["last"] + 1)
                for m in range(4):
                    act.wait_ge(bsd, m + 1)
                    act.activation(oscT_hi[:, m, :], bsc[:, m % 2, :], ACT.Copy).then_inc(bhi, 1)
                split_hi(act, CH[("b",)]["last"] + 2)

            @block.vector
            def _(dve):
                dve.wait_ge(osq, 1)
                dve.tensor_scalar(ssum[:, 0:16], ssum[:, 0:16], 1.0 / GL_DV, EPS, ALU.mult, ALU.add).then_inc(oms, 1)
                dve.memset(uT[:, :, 0:SEQ + 2:SEQ + 1], 0.0).then_inc(u0, 1)
                dve.wait_ge(opow, 1)
                dve.wait_ge(gn_in, 16)
                for t in range(TT):
                    for h in range(GL_H):
                        n = GL_H * t + h
                        o = ogl[:, t, h * GL_DV:(h + 1) * GL_DV]
                        ins = dve.scalar_tensor_tensor(out=o, in0=o, scalar=rstd[:, n:n + 1], in1=gnr[:, :],
                                                       op0=ALU.mult, op1=ALU.mult)
                ins.then_inc(onrm, 1)
                dve.wait_ge(onrm, 1)
                dve.wait_ge(ona_hi, 1)
                dve.tensor_tensor(onaT_lo[:, :, :], onaT[:, :, :], onaT_hi[:, :, :].bitcast(F), ALU.subtract)
                for j in range(2):
                    split_lo(dve, CH[("r", j)]["last"] + 2)
                    for tile in CH[("r", j)]["tiles"]:
                        n = TT * j + tile["t"]
                        dve.wait_ge(emptied["A"], tile["nth"])
                        o = ogl[:, tile["t"], 512 * j:512 * j + 512]
                        dve.tensor_tensor(o, o, sr[:, n % 2, :], ALU.mult).then_inc(srm, 1)
                split_lo(dve, CH[("x",)]["last"] + 2)
                for tile in CH[("x",)]["tiles"]:
                    m = tile["t"]
                    dve.wait_ge(tile_done, tile["n"] + 1)
                    wait_tiles(dve, ("c",))
                    dve.tensor_tensor(uT[:, m, 1:SEQ + 1], PS[:, tile["bank"], :], cT[:, m, :], ALU.mult).then_inc(emptied["D"], 1)
                turn_out_lo(dve, oglT_lo, oglT_hi, KD, OG_BANKS)
                wait_tiles(dve, ("x",))
                dve.wait_ge(cw_in, 48)
                dve.wait_ge(u0, 1)
                for w in range(3):
                    for m in range(4):
                        if w == 0:
                            ins = dve.tensor_scalar(cT[:, m, :], uT[:, m, 0:SEQ], convw[:, 0, m:m + 1], None, ALU.mult)
                        else:
                            ins = dve.scalar_tensor_tensor(out=cT[:, m, :], in0=uT[:, m, w:SEQ + w], scalar=convw[:, w, m:m + 1],
                                                           in1=cT[:, m, :], op0=ALU.mult, op1=ALU.add)
                    dch(dve, ins)
                split_lo(dve, CH[("b",)]["last"] + 1)
                dve.wait_ge(srm, 2 * TT)
                for tile in CH[("b",)]["tiles"]:
                    m = tile["t"]
                    dve.wait_ge(tile_done, tile["n"] + 1)
                    dve.tensor_tensor(bsc[:, m % 2, :], PS[:, tile["bank"], :], cT[:, m, :], ALU.mult).then_inc(bsd, 1)
                    dve.wait_ge(bhi, m + 1)
                    dve.tensor_tensor(oscT_lo[:, m, :], bsc[:, m % 2, :], oscT_hi[:, m, :].bitcast(F), ALU.subtract).then_inc(emptied["D"], 1)
                    dve.wait_ge(emptied["D"], tile["nth"])
                split_lo(dve, CH[("b",)]["last"] + 2)

            @block.tensor
            def _(pe):
                for name in (("r", 0), ("r", 1), ("c",), ("x",)):
                    project(pe, name, acts)
                wait_tiles(pe, ("c",))
                pe.wait_ge(srm, 2 * TT)
                turn(pe, lambda t, m: ogl[:, t, m * P:(m + 1) * P], KD, OG_BANKS)
                pe.wait_ge(turn_lo, nturn[0])
                project(pe, ("b",), acts)

        yT_hi = at("yT_hi", [P, KD, SEQ], 164, R)
        yT_lo = at("yT_lo", [P, KD, SEQ], 180, R)
        yacc = at("yacc", [P, 4, SEQ], 196)
        sgate = at("sgate", [P, 4, SEQ], 4)
        yhi = sem("y_hi")
        branch = {"b0": (onaT_hi, onaT_lo), "b1": (oscT_hi, oscT_lo), "b2": (oglT_hi, oglT_lo)}
        LAST6 = CH[("br", 1, 2)]["last"]
        jb = [(j, br) for j in range(2) for br in range(3)]
        with nc.Block() as block:
            @block.sync
            def _(sp):
                load_to(sp, LAST6 + 3)

            @block.gpsimd
            def _(pool):
                for s in early_sems:
                    pool.sem_clear(s)

            @block.scalar
            def _(act):
                for n, (j, br) in enumerate(jb):
                    split_hi(act, CH[("gate", j, br)]["last"] + 2)
                    for tile in CH[("gate", j, br)]["tiles"]:
                        act.wait_ge(tile_done, tile["n"] + 1)
                        if n:
                            act.wait_ge(emptied["D"], CH[("br", *jb[n - 1])]["tiles"][tile["t"]]["nth"])
                        act.activation(sgate[:, tile["t"], :], PS[:, tile["bank"], :], ACT.Sigmoid).then_inc(emptied["A"], 1)
                    split_hi(act, CH[("br", j, br)]["last"] + 2)
                    if br == 2:
                        for tile in CH[("br", j, br)]["tiles"]:
                            act.wait_ge(emptied["D"], tile["nth"])
                            act.activation(yT_hi[:, 4 * j + tile["t"], :], yacc[:, tile["t"], :], ACT.Copy).then_inc(yhi, 1)

            @block.vector
            def _(dve):
                for n, (j, br) in enumerate(jb):
                    split_lo(dve, CH[("gate", j, br)]["last"] + 2)
                    split_lo(dve, CH[("br", j, br)]["last"] + 2)
                    for tile in CH[("br", j, br)]["tiles"]:
                        m = tile["t"]
                        dve.wait_ge(tile_done, tile["n"] + 1)
                        dve.wait_ge(emptied["A"], CH[("gate", j, br)]["tiles"][m]["nth"])
                        if br == 0:
                            dve.tensor_tensor(yacc[:, m, :], PS[:, tile["bank"], :], sgate[:, m, :], ALU.mult).then_inc(emptied["D"], 1)
                        else:
                            dch(dve, dve.tensor_tensor(sgate[:, m, :], PS[:, tile["bank"], :], sgate[:, m, :], ALU.mult))
                            dve.tensor_tensor(yacc[:, m, :], yacc[:, m, :], sgate[:, m, :], ALU.add).then_inc(emptied["D"], 1)
                    dve.wait_ge(emptied["D"], CH[("br", j, br)]["tiles"][-1]["nth"])
                    if br == 2:
                        for m in range(4):
                            dve.wait_ge(yhi, 4 * j + m + 1)
                            ins = dve.tensor_tensor(yT_lo[:, 4 * j + m, :], yacc[:, m, :], yT_hi[:, 4 * j + m, :].bitcast(F), ALU.subtract)
                        dch(dve, ins)

            @block.tensor
            def _(pe):
                for j, br in jb:
                    project(pe, ("gate", j, br), acts)
                    project(pe, ("br", j, br), lambda kind: branch[kind])

        early.close()
        if dump == "y":
            return finish(nc, out, es, sem, yT_hi)

        x1 = at("x1", [P, TT, D], 68)
        shacc = at("shacc", [P, TT, D], 84)
        gt2 = at("gt2", [P, D], 100)
        gt1 = at("gt1", [P, D], 104)
        sh2 = at("sh2", [P, D], 108)
        sc2 = at("sc2", [P, D], 112)
        g2r = at("g2r", [P, D], 132)
        ptmp = at("ptmp", [P, 2, 512], 136)
        brt = at("brt", [P, NE], 140)
        h2 = at("h2", [P, TT, D], 148)
        wr = at("wr", [P, KD, P], 196)
        wr_hi = at("wr_hi", [P, KD, P], 134, R)
        wr_lo = at("wr_lo", [P, KD, P], 142, R)
        h2T_hi = at("h2T_hi", [P, KD, SEQ], 164, R)
        h2T_lo = at("h2T_lo", [P, KD, SEQ], 180, R)
        rows_in, x1d, h2d, sqd2, ms2, pw2, wrd = (sem(n) for n in "rows_in x1 h2 squares2 ms2 rstd2 wr".split())
        h2_out = sem("h2_out")
        h2_dram = dram("h2_dram", [SEQ, D])
        with nc.Block() as block:
            @block.sync
            def _(sp):
                for n, dst in enumerate((gt1, sh2, sc2, gt2)):
                    sp.dma_start(dst[:, :], bass.AP(tensor=rows_dram.tensor, offset=n * D, ap=[[0, P], [1, D]])).then_inc(rows_in, 16)
                    if n == 0:
                        sp.dma_start(x1[:, :, :], x[0].rearrange("(t p) d -> p t d", p=P)).then_inc(rows_in, 16)
                        load_to(sp, CH[("out", 0)]["last"] + 2)
                load_to(sp, CH[("out", 1)]["last"] + 3)

            @block.gpsimd
            def _(pool):
                pool.dma_start(g2r[:, :], bass.AP(tensor=g_norm2.tensor, offset=0, ap=[[0, P], [1, D]])).then_inc(cpy, 16)
                pool.wait_ge(cpy, 32)
                for t in range(TT):
                    pool.wait_ge(ms2, t + 1)
                    pool.tensor_tensor(rstd[:, t:t + 1], ssum[:, t:t + 1], mhalf[:, t:t + 1], ALU.pow).then_inc(pw2, 1)

            @block.scalar
            def _(act):
                split_hi(act, CH[("out", 0)]["last"] + 2)
                split_hi(act, CH[("out", 1)]["last"])
                for t in range(TT):
                    act.wait_ge(x1d, TT + t + 1)
                    if t:
                        act.wait_ge(sqd2, t)
                    act.activation(h2[:, t, :], x1[:, t, :], ACT.Square, accum_out=ssum[:, t:t + 1]).then_inc(sqd2, 1)
                split_hi(act, CH[("out", 1)]["last"] + 2)

            @block.vector
            def _(dve):
                dve.wait_ge(rows_in, 80)
                dve.wait_ge(cpy, 32)
                dch(dve, dve.scalar_tensor_tensor(out=sc2[:, :], in0=sc2[:, :], scalar=1.0, in1=g2r[:, :], op0=ALU.add, op1=ALU.mult))

                def mean(t):
                    dve.wait_ge(sqd2, t + 1)
                    dve.tensor_scalar(ssum[:, t:t + 1], ssum[:, t:t + 1], 1.0 / D, EPS, ALU.mult, ALU.add).then_inc(ms2, 1)

                def norm(t):
                    dve.wait_ge(pw2, t + 1)
                    dch(dve, dve.scalar_tensor_tensor(out=h2[:, t, :], in0=x1[:, t, :], scalar=rstd[:, t:t + 1], in1=sc2[:, :],
                                                      op0=ALU.mult, op1=ALU.mult))
                    dve.tensor_tensor(h2[:, t, :], h2[:, t, :], sh2[:, :], ALU.add).then_inc(h2d, 1)

                for j in range(2):
                    split_lo(dve, CH[("out", j)]["last"])
                    for tile in CH[("out", j)]["tiles"]:
                        t = tile["t"]
                        if j and t >= 1:
                            mean(t - 1)
                        if j and t >= 2:
                            norm(t - 2)
                        dve.wait_ge(tile_done, tile["n"] + 1)
                        dve.tensor_tensor(ptmp[:, t % 2, :], PS[:, tile["bank"], :], gt1[:, 512 * j:512 * j + 512], ALU.mult)\
                           .then_inc(emptied["D"], 1)
                        dve.wait_ge(emptied["D"], tile["nth"])
                        o = x1[:, t, 512 * j:512 * j + 512]
                        dve.tensor_tensor(o, o, ptmp[:, t % 2, :], ALU.add).then_inc(x1d, 1)
                mean(TT - 1)
                for t in range(max(TT - 2, 0), TT):
                    norm(t)

            @block.tensor
            def _(pe):
                for j in range(2):
                    project(pe, ("out", j), lambda kind: (yT_hi, yT_lo))

        if dump == "h2":
            return finish(nc, out, es, sem, h2)
        wk = at("wk", [P, TT, TOPK], 202)
        tokidx = at("tokidx", [P, NBLK], 202.5, U32)
        blktab = at("blktab", [1, 6, P], 4, I32)
        T_EXPERT, T_NEW, T_COUNT, T_FILLS, T_BEFORE, T_PLACE = range(6)
        blkcol = at("blkcol", [P, 8], 203.5)
        blkint = at("blkint", [P, 4], 203.625, I32)
        iota = at("iota", [P, TT], 203.75)
        slot = at("slot", [P, TT, TOPK], 203.875)
        cols = at("cols", [P, P], 204)
        slotidx = at("slotidx", [P, NBLK], 205, U32)
        rowhot = at("rowhot", [P, 2, TOPK, P], 134)
        blkhot = at("blkhot", [P, 2, TOPK, NBLK], 142)
        scoreT = at("scoreT", [NE, SEQ], 146)
        ones = at("ones", [P, P], 204.5)
        shid = at("shid", [P, TT, FF], 104)
        sgl = at("sgl", [P, TT, FF], 108)
        sT_hi = at("sT_hi", [P, 2, SEQ], 112, R)
        sT_lo = at("sT_lo", [P, 2, SEQ], 116, R)

        def pk(name, shape, kb):
            return at(name, [P] + shape, kb)

        sel, selm, rep = (pk(n, [TT, NE], 121 + i) for i, n in enumerate(("sel", "selm", "rep")))
        chosen = pk("chosen", [TT, NE], 124)
        gw, vpos = (pk(n, [TT, NE], 7 + i) for i, n in enumerate(("gw", "vpos")))
        g8 = pk("g8", [TT, NG, 8], 127)
        gs, gtop, gmask, top8 = (pk(n, [TT, 8], 128 + 0.125 * i) for i, n in enumerate(("gs", "gtop", "gmask", "top8")))
        d1 = pk("d1", [TT, 8], 9)
        wsum = pk("wsum", [TT], 128.75)
        cnt, nbl, bend, bst, jle = (pk(n, [NE], 129 + 0.25 * i) for i, n in enumerate(("cnt", "nbl", "bend", "bst", "jle")))
        eqk = pk("eqk", [TOPK, NE], 10)
        dest, dblk, drow = (pk(n, [TT, TOPK], 130.25 + 0.125 * i) for i, n in enumerate(("dest", "dblk", "drow")))
        lists, nolist = (pk(n, [NBLK], 133 + 0.375 * i) for i, n in enumerate(("lists", "nolist")))
        nonempty, begun, isbegun = (at(n, [P, NE], 120 + 0.25 * i) for i, n in enumerate(("nonempty", "begun", "isbegun")))
        late8, half = at("late8", [P, 8], 120.75), at("half", [P, 4], 120.875)
        (wr_in, h2T_done, scored, scoreT_t, sgd, chosen_done, rank_done, rank_read, blk_done, blk_t, zeros2,
         hot_done, hot_used, ones_done, tab_done, lists_done) = (sem(n) for n in (
             "wr_in h2T scored scores_turned sh_silu chosen ranks ranks_read blocks blocks_turned zeros2 "
             "onehots onehots_used ones_done blktab lists".split()))
        sh_tiles = CH[("sh",)]["tiles"]
        nb = [(sh_tiles[0]["bank"] + i) % 8 for i in range(8)]
        B_RT, B_RK, B_CT, B_T2 = nb[4], nb[5], nb[6], nb[7]
        turn_banks = list(range(8))
        mhi = at("mhi", [P, 6, 2048], 104, R)
        mlo = at("mlo", [P, 6, 2048], 152, R)
        wraw = at("wraw", [P, 6, 2048], 152)
        xg = at("xg", [P, 2, D], 12)
        xT_hi = at("xT_hi", [P, 2, KD, P], 20, R)
        xT_lo = at("xT_lo", [P, 2, KD, P], 28, R)
        mhid = at("mhid", [P, 2, FF], 36)
        hT2_hi = at("hT2_hi", [P, 2, 2, P], 38, R)
        hT2_lo = at("hT2_lo", [P, 2, 2, P], 40, R)
        ysb = at("ysb", [P, 2, D], 42)
        msg = at("msg", [P, 2, FF], 50)
        idxcur = at("idxcur", [P, 2], 203, U32)
        slotcur = at("slotcur", [P, 2], 203.25, U32)
        y_dram = dram("y_dram", [SEQ * TOPK, D])
        wland = [sem(f"expert_landed{i}") for i in range(6)]
        mhi_done, mlo_done = ([sem(f"ex_{n}{pc}") for pc in range(3)] for n in ("hi", "lo"))
        (gu0_done, idx_done, idx_seen, xT_t, xT_hid, xT_lod,
         gu_done, silud, mhidd, hT_t, hT_hid, hT_lod, dn_done, y_a, y_d, slot_done, xg_zero, place_free) = (sem(n) for n in (
             "ex_half_used idx_col idx_seen ex_xT ex_xT_hi ex_xT_lo "
             "ex_gate_up ex_silu ex_hid ex_hidT ex_hidT_hi ex_hidT_lo ex_down y_act y_dve slot_col ex_x_zero ex_place_free".split()))
        xg_in, y_out = ([sem(f"{n}{u}") for u in range(2)] for n in ("expert_x_in", "y_out"))
        DS = bass.ds
        MAXP = NBLK // 2
        MINP = SEQ * TOPK // P // 2

        def steps(eng, body, last, first=0):
            n_pairs = eng.value_load(blkint[0:1, 1:2], min_val=MINP - PEEL, max_val=MAXP - PEEL) + PEEL
            for b in range(first, 2 * PEEL):
                body(b // 2, b % 2, None)
            with eng.Fori(PEEL, MAXP) as i:
                with eng.If(i < n_pairs):
                    for u in range(2):
                        body(i, u, None)
            for k in range(last):
                body(n_pairs, k, k)
            return n_pairs

        def block_of(i, u, back, k):
            b = i * 2 + (u - back)
            return b, (u - back) % 2, not (isinstance(b, int) and b < 0) and (k is None or back > k)

        def some(n):
            return not isinstance(n, int) or n > 0

        def look(eng, row, b, most):
            return eng.value_load(blktab[0:1, row, DS(b, 1)], min_val=0, max_val=most)

        def sent(i, u, back):
            return i * 16 + ((u - back) // 2) * 16

        def load(sp, i, u, back, k, pc):
            b, par, there = block_of(i, u, back, k)
            if not there:
                return
            new = look(sp, T_NEW, b, 2)
            for place in range(2):
                with sp.If(new == place + 1):
                    e, n, before = (look(sp, row, b, most) for row, most in ((T_EXPERT, NE - 1), (T_COUNT, NE), (T_BEFORE, NBLK)))
                    s = 3 * place + pc
                    with sp.If(n > 2):
                        sp.wait_ge((gu0_done, gu_done, dn_done)[pc], before)
                        sp.sem_inc(place_free, 1)
                    if pc < 2:
                        dst = wraw[:, s].rearrange("p (c g f) -> p c g f", c=4, g=2)
                        for g, w in enumerate((w_exp_gate, w_exp_up)):
                            src = w[0][DS(e, 1)].rearrange("a (p c) f -> p (a c) f", p=P)[:, 4 * pc:4 * pc + 4, :]
                            sp.dma_start(dst[:, :, g, :], src).then_inc(wland[s], 16)
                    else:
                        src = w_exp_down[0][DS(e, 1)].rearrange("a (p c) n -> p (a c n)", p=P)
                        sp.dma_start(wraw[:, s], src).then_inc(wland[s], 16)

        def gather(pool, i, u, k):
            b, par, there = block_of(i, u, 0, k)
            if not there:
                return
            if some(b - 1):
                pool.wait_ge(xg_in[par], i * 16)
                pool.wait_ge(xT_t, b - 1)
            pool.tensor_copy(idxcur[:, par:par + 1], tokidx[:, DS(b, 1)]).then_inc(idx_done, 1)
            pool.wait_ge(idx_done, b + 1)
            pool.sem_inc(idx_seen, 1)
            pool.indirect_dma_start(xg[:, par, :], None, h2_dram, bass.IndirectOffsetOnAxis(ap=idxcur[:, par:par + 1], axis=0),
                                    bounds_check=SEQ - 1, oob_is_err=False).then_inc(xg_in[par], 16)

        with nc.Block() as block:
            @block.sync
            def _(sp):
                sp.dma_start(wr[:, :, 0:NE], w_router[0].rearrange("(k p) n -> p k n", p=P)).then_inc(wr_in, 16)
                sp.dma_start(brt[:, :], bass.AP(tensor=b_router.tensor, offset=0, ap=[[0, P], [1, NE]])).then_inc(wr_in, 16)
                sp.dma_start(iota[:, :], k_iota).then_inc(wr_in, 16)
                sp.dma_start(slot[:, :, :], k_slot).then_inc(wr_in, 16)
                sp.dma_start(cols[:, :], k_cols).then_inc(wr_in, 16)
                sp.dma_start(h2_dram.rearrange("(t p) d -> p t d", p=P), h2[:, :, :]).then_inc(h2_out, 16)
                load_to(sp, len(HALVES))
                sp.wait_ge(h2_out, 16)
                sp.wait_ge(wr_in, 80)
                sp.wait_ge(tile_done, sh_tiles[-1]["n"] + 1)
                sp.wait_ge(tab_done, 1)
                for u in range(2):
                    load(sp, 0, u, 0, None, 0)
                    load(sp, 0, u, 0, None, 1)
                    load(sp, 0, u, 1, None, 2)

            @block.gpsimd
            def _(pool):
                pool.memset(wr[:, :, NE:], 0.0).then_inc(zeros2, 1)
                pool.memset(ones[:, :], 1.0).then_inc(ones_done, 1)
                pool.wait_ge(lo_done, len(HALVES))
                pool.memset(xg[:, :, :], 0.0).then_inc(xg_zero, 1)
                pool.wait_ge(xg_zero, 1)
                pool.wait_ge(h2_out, 16)
                pool.wait_ge(lists_done, 1)
                for u in range(2):
                    gather(pool, 0, u, None)

            @block.scalar
            def _(act):
                turn_out_hi(act, h2T_hi, KD, turn_banks)
                act.wait_ge(wr_in, 80)
                act.wait_ge(zeros2, 1)
                act.activation(wr_hi[:, :, :], wr[:, :, :], ACT.Copy).then_inc(wrd, 1)
                act.wait_ge(h2T_done, 1)
                act.activation(scoreT[:, :], PS[0:NE, B_RT, :], ACT.Sigmoid).then_inc(scored, 1)
                split_hi(act, CH[("sh",)]["last"] + 2)
                for tile in sh_tiles:
                    act.wait_ge(tile_done, tile["n"] + 1)
                    act.activation(sgl[:, tile["t"], :], PS[:, tile["bank"], 0:FF], ACT.Silu).then_inc(sgd, 1)
                turn_out_hi(act, sT_hi, 2, [B_RT, B_RK])

            @block.vector
            def _(dve):
                turn_out_lo(dve, h2T_lo, h2T_hi, KD, turn_banks)
                dve.wait_ge(wrd, 1)
                dve.tensor_tensor(wr_lo[:, :, :], wr[:, :, :], wr_hi[:, :, :].bitcast(F), ALU.subtract).then_inc(wrd, 1)
                split_lo(dve, CH[("sh",)]["last"])
                dve.wait_ge(scoreT_t, 1)
                score = PS[:, B_RT, 0:TT * NE].rearrange("p (t e) -> p t e", t=TT)
                dch(dve, dve.tensor_tensor(sel[:, :, :], score, brt[:, None, :].to_broadcast([P, TT, NE]), ALU.add))
                for t in range(TT):
                    for g in range(NG):
                        ins = dve.max(g8[:, t, g, :], sel[:, t, g * 8:(g + 1) * 8])
                dch(dve, ins)
                dch(dve, dve.tensor_tensor(gs[:, :, :], g8[:, :, :, 0], g8[:, :, :, 1], ALU.add))
                for t in range(TT):
                    ins = dve.max(gtop[:, t, :], gs[:, t, :])
                dch(dve, ins)
                dch(dve, dve.tensor_tensor(gmask[:, :, :], gs[:, :, :], gtop[:, :, TOPG - 1:TOPG].to_broadcast([P, TT, NG]), ALU.is_ge))
                gm = gmask[:, :, :, None].to_broadcast([P, TT, NG, NE // NG])
                r4 = lambda a: a[:, :, :].rearrange("p t (g e) -> p t g e", g=NG)
                dch(dve, dve.tensor_tensor(r4(selm), r4(sel), gm, ALU.mult))
                dch(dve, dve.tensor_scalar(gmask[:, :, :], gmask[:, :, :], 1.0, -NEG, ALU.subtract, ALU.mult))
                dch(dve, dve.tensor_tensor(r4(selm), r4(selm), gm, ALU.add))
                for t in range(TT):
                    ins = dve.max(top8[:, t, :], selm[:, t, :])
                dch(dve, ins)
                for t in range(TT):
                    ins = dve.match_replace(rep[:, t, :], top8[:, t, :], selm[:, t, :], -3e38)
                dch(dve, ins)
                dve.tensor_tensor(chosen[:, :, :], rep[:, :, :], selm[:, :, :], ALU.not_equal).then_inc(chosen_done, 1)
                dve.wait_ge(chosen_done, 1)
                dch(dve, dve.tensor_tensor(gw[:, :, :], score, chosen[:, :, :], ALU.mult))
                dch(dve, dve.tensor_reduce(wsum[:, :], gw[:, :, :], AX.X, ALU.add))
                dch(dve, dve.reciprocal(wsum[:, :], wsum[:, :]))
                dch(dve, dve.scalar_tensor_tensor(out=gw[:, :, :], in0=gw[:, :, :], scalar=ROUTED_SCALE,
                                                  in1=wsum[:, :, None].to_broadcast([P, TT, NE]), op0=ALU.mult, op1=ALU.mult))
                dve.wait_ge(rank_done, 1)
                dch(dve, dve.tensor_copy(cnt[:, :], PS[:, B_CT, 0:NE]))
                dch(dve, dve.tensor_scalar(nbl[:, :], cnt[:, :], 0.0, None, ALU.is_gt))
                for m in range(1, TT):
                    dch(dve, dve.scalar_tensor_tensor(out=nbl[:, :], in0=cnt[:, :], scalar=float(m * P), in1=nbl[:, :],
                                                      op0=ALU.is_gt, op1=ALU.add))
                dch(dve, dve.tensor_tensor_scan(bend[:, :], ones[:, 0:NE], nbl[:, :], 0.0, ALU.mult, ALU.add))
                dch(dve, dve.tensor_tensor(bst[:, :], bend[:, :], nbl[:, :], ALU.subtract))
                dve.scalar_tensor_tensor(out=vpos[:, :, :], in0=bst[:, None, :].to_broadcast([P, TT, NE]), scalar=float(P),
                                         in1=PS[:, B_RK, 0:TT * NE].rearrange("p (t e) -> p t e", t=TT),
                                         op0=ALU.mult, op1=ALU.add).then_inc(rank_read, 1)
                dve.wait_ge(rank_read, 1)
                dch(dve, dve.scalar_tensor_tensor(out=vpos[:, :, :], in0=vpos[:, :, :], scalar=1.0, in1=chosen[:, :, :],
                                                  op0=ALU.add, op1=ALU.mult))
                for t in range(TT):
                    ins = dve.max(d1[:, t, :], vpos[:, t, :])
                dch(dve, ins)
                dch(dve, dve.tensor_scalar(dest[:, :, :], d1[:, :, :], 1.0, None, ALU.subtract))
                dch(dve, dve.tensor_scalar(dblk[:, :, :], dest[:, :, :], 1.0 / P, 0.5 * (P - 1) / P, ALU.mult, ALU.subtract))
                dch(dve, dve.tensor_scalar(dblk[:, :, :], dblk[:, :, :], ROUND, ROUND, ALU.add, ALU.subtract))
                dch(dve, dve.scalar_tensor_tensor(out=drow[:, :, :], in0=dblk[:, :, :], scalar=-float(P), in1=dest[:, :, :],
                                                  op0=ALU.mult, op1=ALU.add))
                dch(dve, dve.tensor_scalar(blkcol[:, 1:2], bend[:, NE - 1:NE], 0.5, 0.25 - PEEL, ALU.mult, ALU.add))
                dch(dve, dve.tensor_scalar(blkint[:, 1:2], blkcol[:, 1:2], ROUND, ROUND, ALU.add, ALU.subtract))
                col = lambda row: blkcol[:, row:row + 1]
                dch(dve, dve.tensor_scalar(jle[:, :], bend[:, :], iota[:, 0:1], None, ALU.is_le))
                dch(dve, dve.tensor_reduce(col(T_EXPERT), jle[:, :], AX.X, ALU.add))
                dch(dve, dve.tensor_scalar(col(T_EXPERT), col(T_EXPERT), float(NE - 1), None, ALU.min))
                dch(dve, dve.tensor_scalar(nonempty[:, :], cnt[:, :], 0.0, None, ALU.is_gt))
                dch(dve, dve.scalar_tensor_tensor(out=nonempty[:, :], in0=bst[:, :], scalar=1.0, in1=nonempty[:, :], op0=ALU.add, op1=ALU.mult))
                dch(dve, dve.scalar_tensor_tensor(out=begun[:, :], in0=bst[:, :], scalar=iota[:, 0:1], in1=nonempty[:, :],
                                                  op0=ALU.is_le, op1=ALU.mult))
                dve.max(late8[:, :], begun[:, :])
                dch(dve, dve.tensor_scalar(isbegun[:, :], begun[:, :], 0.0, None, ALU.is_gt))
                dch(dve, dve.tensor_reduce(col(T_COUNT), isbegun[:, :], AX.X, ALU.add))
                dve.tensor_scalar(col(T_BEFORE), late8[:, 1:2], 1.0, 0.0, ALU.subtract, ALU.max)
                dve.scalar_tensor_tensor(out=half[:, 1:2], in0=late8[:, 0:1], scalar=1.0, in1=iota[:, 0:1], op0=ALU.subtract, op1=ALU.is_equal)
                dch(dve, dve.tensor_scalar(half[:, 0:1], col(T_COUNT), 0.5, 0.75, ALU.mult, ALU.subtract))
                dch(dve, dve.tensor_scalar(half[:, 0:1], half[:, 0:1], ROUND, ROUND, ALU.add, ALU.subtract))
                dve.tensor_scalar(col(T_FILLS), half[:, 0:1], 1.0, None, ALU.add)
                dch(dve, dve.scalar_tensor_tensor(out=col(T_PLACE), in0=half[:, 0:1], scalar=-2.0, in1=col(T_COUNT), op0=ALU.mult, op1=ALU.add))
                dch(dve, dve.tensor_tensor(col(T_NEW), col(T_PLACE), half[:, 1:2], ALU.mult))
                dve.tensor_scalar(col(T_PLACE), col(T_PLACE), 1.0, None, ALU.subtract).then_inc(blk_done, 1)
                dve.wait_ge(blk_t, 1)
                dch(dve, dve.tensor_copy(blktab[0:1, 0:4, :], PS[0:1, B_CT, :].rearrange("p (r b) -> p r b", r=4)))
                dve.tensor_copy(blktab[0:1, 4:6, :], PS[0:1, B_RK, 0:2 * P].rearrange("p (r b) -> p r b", r=2)).then_inc(tab_done, 1)
                dve.wait_ge(tab_done, 1)
                for t in range(TT):
                    if t == 2:
                        for tile in sh_tiles:
                            dve.wait_ge(sgd, tile["t"] + 1)
                            dve.tensor_tensor(shid[:, tile["t"], :], PS[:, tile["bank"], FF:], sgl[:, tile["t"], :], ALU.mult)\
                               .then_inc(emptied["D"], 1)
                        split_lo(dve, len(HALVES))
                    if t >= 2:
                        dve.wait_ge(hot_used, t - 1)
                    dve.tensor_tensor(rowhot[:, t % 2], cols[:, None, :].to_broadcast([P, TOPK, P]),
                                      drow[:, t, :, None].to_broadcast([P, TOPK, P]), ALU.is_equal)
                    dch(dve, dve.tensor_tensor(blkhot[:, t % 2], cols[:, None, 0:NBLK].to_broadcast([P, TOPK, NBLK]),
                                               dblk[:, t, :, None].to_broadcast([P, TOPK, NBLK]), ALU.is_equal))
                    dve.tensor_tensor(blkhot[:, t % 2], blkhot[:, t % 2], slot[:, t, :, None].to_broadcast([P, TOPK, NBLK]), ALU.mult)\
                       .then_inc(hot_done, 1)
                turn_out_lo(dve, sT_lo, sT_hi, 2, [B_RT, B_RK])
                dve.wait_ge(hot_used, TT)
                dch(dve, dve.tensor_scalar(nolist[:, :], PS[:, B_T2, 0:NBLK], 0.0, PAD, ALU.is_equal, ALU.mult))
                dch(dve, dve.scalar_tensor_tensor(out=lists[:, :], in0=PS[:, B_T2, 0:NBLK], scalar=1.0, in1=nolist[:, :],
                                                  op0=ALU.subtract, op1=ALU.add))
                dch(dve, dve.tensor_copy(slotidx[:, :], lists[:, :]))
                dch(dve, dve.tensor_scalar(lists[:, :], lists[:, :], 1.0 / TOPK, 0.5 * (TOPK - 1) / TOPK, ALU.mult, ALU.subtract))
                dve.tensor_scalar(tokidx[:, :], lists[:, :], ROUND, ROUND, ALU.add, ALU.subtract).then_inc(lists_done, 1)
                dve.wait_ge(lists_done, 1)
                for tile in CH[("down",)]["tiles"]:
                    dve.wait_ge(tile_done, tile["n"] + 1)
                    t, h = divmod(tile["t"], 2)
                    dve.tensor_copy(shacc[:, t, 512 * h:512 * h + 512], PS[:, tile["bank"], :]).then_inc(emptied["D"], 1)

            @block.tensor
            def _(pe):
                turn(pe, lambda t, m: h2[:, t, m * P:(m + 1) * P], KD, turn_banks)
                pe.wait_ge(turn_lo, nturn[0])
                pe.wait_ge(wrd, 2)
                for k in range(KD):
                    mm = mm3(pe, PS[:, B_RT, :], wr_hi[:, k], wr_lo[:, k], h2T_hi[:, k], h2T_lo[:, k], k == 0, k == KD - 1)
                mm.then_inc(h2T_done, 1)
                pe.wait_ge(scored, 1)
                for t in range(TT):
                    mm = pe.transpose(PS[:, B_RT, t * NE:(t + 1) * NE], scoreT[:, t * P:(t + 1) * P], ident[0:NE, 0:NE])
                mm.then_inc(scoreT_t, 1)
                project(pe, ("sh",), lambda kind: (h2T_hi, h2T_lo), part=0)
                pe.wait_ge(chosen_done, 1)
                pe.wait_ge(ones_done, 1)
                for t in range(TT):
                    for j in range(t + 1):
                        pe.matmul(PS[:, B_RK, t * NE:(t + 1) * NE], tri[:, 2, :] if j == t else ones[:, :], chosen[:, j, :],
                                  start=(j == 0), stop=(j == t))
                for j in range(TT):
                    mm = pe.matmul(PS[:, B_CT, 0:NE], ones[:, :], chosen[:, j, :], start=(j == 0), stop=(j == TT - 1))
                mm.then_inc(rank_done, 1)
                project(pe, ("sh",), lambda kind: (h2T_hi, h2T_lo), part=1)
                pe.wait_ge(blk_done, 1)
                for row in range(6):
                    mm = pe.matmul(PS[0:1, B_CT if row < 4 else B_RK, row % 4 * P:(row % 4 + 1) * P], blkcol[:, row:row + 1], ident[:, :],
                                   start=True, stop=True)
                mm.then_inc(blk_t, 1)
                for t in range(TT):
                    if t == 2:
                        pe.wait_ge(tab_done, 1)
                        pe.wait_ge(emptied["D"], sh_tiles[-1]["nth"])
                        turn(pe, lambda t, m: shid[:, t, m * P:(m + 1) * P], 2, [B_RT, B_RK])
                    pe.wait_ge(hot_done, t + 1)
                    for k in range(TOPK):
                        mm = pe.matmul(PS[:, B_T2, 0:NBLK], rowhot[:, t % 2, k], blkhot[:, t % 2, k],
                                       start=(t == 0 and k == 0), stop=(t == TT - 1 and k == TOPK - 1))
                    mm.then_inc(hot_used, 1)
                pe.wait_ge(turn_lo, nturn[0])
                project(pe, ("down",), lambda kind: (sT_hi, sT_lo), ready={4: (lists_done, 1)})

        with nc.Block() as block:
            @block.sync
            def _(sp):
                def body(i, u, k):
                    load(sp, i, u, 0, k, 0)
                    load(sp, i, u, 0, k, 1)
                    load(sp, i, u, 1, k, 2)
                steps(sp, body, 1, first=2)

            @block.gpsimd
            def _(pool):

                def scatter(i, u, k):
                    b, par, there = block_of(i, u, 4, k)
                    if not there:
                        return
                    if some(b - 1):
                        pool.wait_ge(y_out[par], sent(i, u, 4))
                    pool.tensor_copy(slotcur[:, par:par + 1], slotidx[:, DS(b, 1)]).then_inc(slot_done, 1)
                    pool.wait_ge(slot_done, b + 1)
                    pool.sem_inc(idx_seen, 1)
                    pool.wait_ge(y_a, b + 1)
                    pool.wait_ge(y_d, b + 1)
                    pool.sem_inc(idx_seen, 1)
                    pool.indirect_dma_start(y_dram, bass.IndirectOffsetOnAxis(ap=slotcur[:, par:par + 1], axis=0), ysb[:, par, :], None,
                                            bounds_check=SEQ * TOPK - 1, oob_is_err=False).then_inc(y_out[par], 16)

                def body(i, u, k):
                    if not (isinstance(i, int) and i == 0):
                        gather(pool, i, u, k)
                    scatter(i, u, k)
                n_pairs = steps(pool, body, 4)
                for s in y_out:
                    pool.wait_ge(s, n_pairs * 16)

            @block.scalar
            def _(act):
                def hi(i, u, back, k, pc):
                    b, par, there = block_of(i, u, back, k)
                    if not there:
                        return
                    new = look(act, T_NEW, b, 2)
                    for place in range(2):
                        with act.If(new == place + 1):
                            s = 3 * place + pc
                            act.wait_ge(wland[s], look(act, T_FILLS, b, NE) * (32 if pc < 2 else 16))
                            act.activation(mhi[:, s, :], wraw[:, s], ACT.Copy).then_inc(mhi_done[pc], 1)

                def silu(i, u, k):
                    b, par, there = block_of(i, u, 1, k)
                    if there:
                        act.wait_ge(gu_done, b + 1)
                        if some(b - 1):
                            act.wait_ge(mhidd, b - 1)
                        act.activation(msg[:, par, :], PS[:, par, 0:FF], ACT.Silu).then_inc(silud, 1)

                def rows_hi(i, u, k):
                    b, par, there = block_of(i, u, 0, k)
                    if there:
                        act.wait_ge(xT_t, b + 1)
                        if some(b - 1):
                            act.wait_ge(gu_done, b - 1)
                        for h in range(2):
                            act.activation(xT_hi[:, par, 4 * h:4 * h + 4, :], PS[:, 2 + h, :], ACT.Copy).then_inc(xT_hid, 1)

                def hidden_hi(i, u, k):
                    b, par, there = block_of(i, u, 2, k)
                    if there:
                        act.wait_ge(hT_t, b + 1)
                        if some(b - 1):
                            act.wait_ge(dn_done, b - 1)
                        act.activation(hT2_hi[:, par], PS[:, 4, 0:2 * P], ACT.Copy).then_inc(hT_hid, 1)

                def result(i, u, k):
                    b, par, there = block_of(i, u, 3, k)
                    if there:
                        act.wait_ge(dn_done, b + 1)
                        if some(b - 1):
                            act.wait_ge(y_out[par], sent(i, u, 3))
                        act.activation(ysb[:, par, 0:512], PS[:, 5, :], ACT.Copy).then_inc(y_a, 1)

                def body(i, u, k):
                    hi(i, u, 0, k, 0)
                    rows_hi(i, u, k)
                    hidden_hi(i, u, k)
                    result(i, u, k)
                    hi(i, u, 0, k, 1)
                    silu(i, u, k)
                    hi(i, u, 1, k, 2)
                steps(act, body, 3)

            @block.vector
            def _(dve):
                def lo(i, u, back, k, pc):
                    b, par, there = block_of(i, u, back, k)
                    if not there:
                        return
                    new = look(dve, T_NEW, b, 2)
                    for place in range(2):
                        with dve.If(new == place + 1):
                            s = 3 * place + pc
                            dve.wait_ge(mhi_done[pc], look(dve, T_COUNT, b, NE))
                            dve.tensor_tensor(mlo[:, s, :], wraw[:, s, :], mhi[:, s, :].bitcast(F), ALU.subtract).then_inc(mlo_done[pc], 1)

                def hidden(i, u, k):
                    b, par, there = block_of(i, u, 1, k)
                    if there:
                        dve.wait_ge(silud, b + 1)
                        if some(b - 1):
                            dve.wait_ge(hT_t, b - 1)
                        dve.tensor_tensor(mhid[:, par, :], PS[:, par, FF:], msg[:, par, :], ALU.mult).then_inc(mhidd, 1)

                def rows_lo(i, u, k):
                    b, par, there = block_of(i, u, 0, k)
                    if there:
                        for h in range(2):
                            dve.wait_ge(xT_hid, b * 2 + (h + 1))
                            dve.tensor_tensor(xT_lo[:, par, 4 * h:4 * h + 4, :], PS[:, 2 + h, :],
                                              xT_hi[:, par, 4 * h:4 * h + 4, :].bitcast(F), ALU.subtract).then_inc(xT_lod, 1)

                def hidden_lo(i, u, k):
                    b, par, there = block_of(i, u, 2, k)
                    if there:
                        dve.wait_ge(hT_hid, b + 1)
                        dve.tensor_tensor(hT2_lo[:, par], PS[:, 4, 0:2 * P], hT2_hi[:, par].bitcast(F), ALU.subtract).then_inc(hT_lod, 1)

                def result(i, u, k):
                    b, par, there = block_of(i, u, 3, k)
                    if there:
                        dve.wait_ge(dn_done, b + 1)
                        if some(b - 1):
                            dve.wait_ge(y_out[par], sent(i, u, 3))
                        dve.tensor_copy(ysb[:, par, 512:], PS[:, 6, :]).then_inc(y_d, 1)

                def body(i, u, k):
                    lo(i, u, 0, k, 0)
                    rows_lo(i, u, k)
                    hidden_lo(i, u, k)
                    result(i, u, k)
                    lo(i, u, 0, k, 1)
                    hidden(i, u, k)
                    lo(i, u, 1, k, 2)
                steps(dve, body, 3)

            @block.tensor
            def _(pe):
                def turn_rows(i, u, k):
                    b, par, there = block_of(i, u, 0, k)
                    if there:
                        pe.wait_ge(xg_in[par], i * 16 + 16)
                        if some(b):
                            pe.wait_ge(xT_lod, b * 2)
                        for c in range(KD):
                            mm = pe.transpose(PS[:, 2 + c // 4, (c % 4) * P:(c % 4 + 1) * P], xg[:, par, c:D:KD], ident[:, :])
                        mm.then_inc(xT_t, 1)

                def turn_hidden(i, u, k):
                    b, par, there = block_of(i, u, 2, k)
                    if there:
                        pe.wait_ge(mhidd, b + 1)
                        if some(b):
                            pe.wait_ge(hT_lod, b)
                        for c in range(2):
                            mm = pe.transpose(PS[:, 4, c * P:(c + 1) * P], mhid[:, par, c:FF:2], ident[:, :])
                        mm.then_inc(hT_t, 1)

                def gate_up(i, u, k):
                    b, par, there = block_of(i, u, 1, k)
                    if there:
                        count, place = look(pe, T_COUNT, b, NE), look(pe, T_PLACE, b, 1)
                        pe.wait_ge(xT_lod, b * 2 + 2)
                        for pc in range(2):
                            pe.wait_ge(mlo_done[pc], count)
                            for c in range(4):
                                w = slice(c * 512, (c + 1) * 512)
                                s = DS(place * 3 + pc, 1)
                                mm = mm3(pe, PS[:, par, :], xT_hi[:, par, 4 * pc + c], xT_lo[:, par, 4 * pc + c], mhi[:, s, w], mlo[:, s, w],
                                         pc == 0 and c == 0, pc == 1 and c == 3)
                            mm.then_inc(gu_done if pc else gu0_done, 1)

                def down(i, u, k):
                    b, par, there = block_of(i, u, 2, k)
                    if there:
                        count, place = look(pe, T_COUNT, b, NE), look(pe, T_PLACE, b, 1)
                        pe.wait_ge(hT_lod, b + 1)
                        pe.wait_ge(mlo_done[2], count)
                        if some(b):
                            pe.wait_ge(y_a, b)
                            pe.wait_ge(y_d, b)
                        s = DS(place * 3 + 2, 1)
                        for c in range(2):
                            for n in range(2):
                                w = slice((2 * c + n) * 512, (2 * c + n + 1) * 512)
                                mm = mm3(pe, PS[:, 5 + n, :], hT2_hi[:, par, c], hT2_lo[:, par, c], mhi[:, s, w], mlo[:, s, w],
                                         c == 0, c == 1)
                        mm.then_inc(dn_done, 1)

                def body(i, u, k):
                    turn_rows(i, u, k)
                    turn_hidden(i, u, k)
                    gate_up(i, u, k)
                    down(i, u, k)
                steps(pe, body, 3)

        NYB = 3
        HK = TOPK // 2
        PE_K = (0, 1, 4)
        DVE_K = tuple(k for k in range(TOPK) if k not in PE_K)
        yb = at("yb", [P, NYB, HK, D], 104)
        gfr = at("gfr", [P, D], 12)
        fin = at("fin", [P, TT, D], 16)
        jf = at("jf", [P, D], 32)
        diag = at("diag", [P, TT, len(PE_K), P], 36)
        y_in = [sem(f"rows_in{i}") for i in range(NYB)]
        summed, gf_in, x2d, sq3, ms3, pw3, find, out_done, diag_done, pe_read, pe_added, wk_done = (sem(n) for n in (
            "summed gf_in x2 squares3 ms3 rstd3 final out_done diagonals pe_read pe_added choice_weights".split()))
        with nc.Block() as block:
            @block.sync
            def _(sp):
                rows = y_dram.rearrange("(t p k) d -> t p k d", t=TT, p=P)

                def send(t):
                    sp.wait_ge(find, t + 1)
                    sp.dma_start(out[t * P:(t + 1) * P, :], fin[:, t, :]).then_inc(out_done, 16)

                for n in range(2 * TT):
                    t, h = divmod(n, 2)
                    if n >= NYB:
                        sp.wait_ge(summed, sum(k // HK + 2 * tt <= n - NYB for tt in range(TT) for k in DVE_K))
                        sp.wait_ge(pe_read, n - NYB + 1)
                    sp.dma_start(yb[:, n % NYB], rows[t, :, h * HK:(h + 1) * HK, :]).then_inc(y_in[n % NYB], 16)
                    if n == 0:
                        sp.dma_start(gfr[:, :], bass.AP(tensor=g_final.tensor, offset=0, ap=[[0, P], [1, D]])).then_inc(gf_in, 16)
                for t in range(TT):
                    send(t)
                sp.wait_ge(out_done, 16 * TT)

            @block.gpsimd
            def _(pool):
                for t in range(TT):
                    pool.wait_ge(wk_done, t + 1)
                    for n, k in enumerate(PE_K):
                        ins = pool.tensor_tensor(diag[:, t, n, :], ident[:, :], wk[:, t, k:k + 1].to_broadcast([P, P]), ALU.mult)
                    ins.then_inc(diag_done, 1)
                for t in range(TT):
                    pool.wait_ge(ms3, t + 1)
                    pool.tensor_tensor(rstd[:, t:t + 1], ssum[:, t:t + 1], mhalf[:, t:t + 1], ALU.pow).then_inc(pw3, 1)

            @block.scalar
            def _(act):
                for t in range(TT):
                    act.wait_ge(x2d, t + 1)
                    act.activation(jf[:, :], fin[:, t, :], ACT.Square, accum_out=ssum[:, t:t + 1]).then_inc(sq3, 1)
                    act.wait_ge(sq3, t + 1)

            @block.vector
            def _(dve):
                def mean(t):
                    dve.wait_ge(sq3, t + 1)
                    dve.tensor_scalar(ssum[:, t:t + 1], ssum[:, t:t + 1], 1.0 / D, EPS, ALU.mult, ALU.add).then_inc(ms3, 1)

                def last(t):
                    dve.wait_ge(pw3, t + 1)
                    dve.scalar_tensor_tensor(out=fin[:, t, :], in0=fin[:, t, :], scalar=rstd[:, t:t + 1], in1=gfr[:, :],
                                             op0=ALU.mult, op1=ALU.mult).then_inc(find, 1)

                for t in range(TT):
                    vb = vpos[:, t:t + 1, :].to_broadcast([P, TOPK, NE])
                    dch(dve, dve.tensor_tensor(eqk[:, :, :], vb, d1[:, t, :, None].to_broadcast([P, TOPK, NE]), ALU.is_equal))
                    dch(dve, dve.tensor_tensor(eqk[:, :, :], eqk[:, :, :], gw[:, t:t + 1, :].to_broadcast([P, TOPK, NE]), ALU.mult))
                    dve.tensor_reduce(wk[:, t, :], eqk[:, :, :], AX.X, ALU.add).then_inc(wk_done, 1)
                    dve.wait_ge(wk_done, t + 1)
                n = 0
                for t in range(TT):
                    for m, k in enumerate(DVE_K):
                        part = 2 * t + k // HK
                        dve.wait_ge(y_in[part % NYB], 16 * (part // NYB + 1))
                        if n:
                            dve.wait_ge(summed, n)
                        dve.scalar_tensor_tensor(out=shacc[:, t, :], in0=yb[:, part % NYB, k % HK, :], scalar=wk[:, t, k:k + 1], in1=shacc[:, t, :],
                                                 op0=ALU.mult, op1=ALU.add).then_inc(summed, 1)
                        n += 1
                        if t and m == 1:
                            mean(t - 1)
                        if t and m == 3:
                            last(t - 1)
                    dve.wait_ge(pe_read, 2 * t + 2)
                    dve.wait_ge(summed, n)
                    dve.tensor_tensor(shacc[:, t, :], shacc[:, t, :], PS[:, 2 * (t % 2):2 * (t % 2) + 2, :].rearrange("p b n -> p (b n)"), ALU.add)\
                       .then_inc(pe_added, 1)
                    dve.wait_ge(pe_added, t + 1)
                    dch(dve, dve.tensor_tensor(shacc[:, t, :], shacc[:, t, :], gt2[:, :], ALU.mult))
                    dve.tensor_tensor(fin[:, t, :], x1[:, t, :], shacc[:, t, :], ALU.add).then_inc(x2d, 1)
                    if t == 0:
                        dve.wait_ge(gf_in, 16)
                mean(TT - 1)
                last(TT - 1)

            @block.tensor
            def _(pe):
                for t in range(TT):
                    pe.wait_ge(diag_done, t + 1)
                    if t >= 2:
                        pe.wait_ge(pe_added, t - 1)
                    for h in range(2):
                        part = 2 * t + h
                        pe.wait_ge(y_in[part % NYB], 16 * (part // NYB + 1))
                        for n, k in enumerate(PE_K):
                            if k // HK == h:
                                for c in range(2):
                                    mm = pe.matmul(PS[:, 2 * (t % 2) + c, :], diag[:, t, n, :], yb[:, part % NYB, k % HK, 512 * c:512 * c + 512],
                                                   start=(n == 0), stop=(n == len(PE_K) - 1))
                        mm.then_inc(pe_read, 1)
    return nc


def finish(nc, out, es, sem, *ts):
    s = sem("dump")
    with nc.Block() as block:
        @block.sync
        def _(sp):
            n = 0
            for t in ts:
                f = int(np.prod(t.shape[1:]))
                fl = t[:] if len(t.shape) == 2 else t[:].rearrange("p a b -> p (a b)")
                sp.dma_start(bass.AP(tensor=out.tensor, offset=n, ap=[[f, P], [1, f]]), fl.bitcast(F)).then_inc(s, 16)
                n += P * f
            sp.wait_ge(s, 16 * len(ts))
    return nc


_INS = ['x', 'c', 'ctx', 'c_ctx', 'w_mod', 'b_mod', 'g_norm1', 'g_norm2', 'w_in', 'na_rpb', 'w_branch_na', 'conv_w',
        'w_branch_sc', 'gla_gate_w', 'gla_gate_b', 'gla_norm_g', 'w_branch_gla', 'w_out', 'w_router', 'b_router',
        'w_exp_gate', 'w_exp_up', 'w_exp_down', 'w_sh_gate', 'w_sh_up', 'w_sh_down', 'g_final']


def shape_constants():
    s, t = np.arange(P)[:, None], np.arange(P)[None, :]
    tri = np.stack([s <= t, s >= t, s < t]).astype(np.float32)
    q, k = (np.arange(P) % GRID)[:, None], np.arange(GRID)[None, :]
    start = np.clip(q - WIN_C // 2, 0, GRID - WIN_C)
    mask = ((k >= start) & (k < start + WIN_C)).astype(np.int32)
    iota = np.arange(SEQ, dtype=np.float32).reshape(TT, P).T.copy()
    slot = iota[:, :, None] * TOPK + np.arange(1, TOPK + 1, dtype=np.float32)
    return {"k_ident": np.eye(P, dtype=np.float32), "k_tri": tri, "k_mask": mask, "k_iota": iota,
            "k_slot": slot.astype(np.float32), "k_cols": np.tile(np.arange(P, dtype=np.float32), (P, 1))}


def kernel(**inputs):
    import concourse.bacc as _bacc
    from concourse.bass_utils import run_bass_kernel_spmd as _run

    nc = _bacc.Bacc("TRN2", target_bir_lowering=False, num_devices=1)
    arrays, args = {}, []
    tables = shape_constants()
    for name in _INS + list(tables):
        a = np.ascontiguousarray(inputs[name] if name in inputs else tables[name])
        arrays[f"in_{name}_dram"] = a
        args.append(nc.dram_tensor(f"in_{name}_dram", a.shape, mybir.dt.from_np(a.dtype), kind="ExternalInput").ap())
    out = nc.dram_tensor("out_0_dram", (SEQ, D), F, kind="ExternalOutput").ap()
    build(nc, *args, out)
    r = _run(nc, [arrays], core_ids=[0])
    return r.results[0]["out_0_dram"].reshape(1, SEQ, D)
```
